# Optimizing a Trainium2 kernel written in Bass

```python
import math
import numpy as np
import jax
import jax.numpy as jnp
from jax import lax

D_MODEL = 1024
BATCH = 1
SEQ = 512
DEPTH = 2

GRID_W = 64
CTX_LEN = 256
EPS = 1e-6

A_HEADS = 4
A_QK_DIM = 64
A_V_DIM = 2 * A_QK_DIM
B_HEADS = 8
B_HEAD_DIM = 64
A_Q_W = A_HEADS * 2 * A_QK_DIM
A_V_W = A_HEADS * A_V_DIM
B_W = B_HEADS * B_HEAD_DIM
ATTN_SPLITS = [A_Q_W, 2 * A_Q_W, 2 * A_Q_W + A_V_W, 2 * A_Q_W + A_V_W + B_W, 2 * A_Q_W + A_V_W + 2 * B_W]
ATTN_IN_W = 2 * A_Q_W + A_V_W + 3 * B_W
ATTN_OUT_W = A_V_W + B_W
Q_BLOCK = 128
NA_ROWS = 8
NA_COLS = 16
ROPE_BASE = 10000.0

CHUNK = 128
C_GROUPS = 8
C_WIDTH = D_MODEL
C_GROUP_W = C_WIDTH // C_GROUPS

PEER_HEADS = 8
N_KEYS = 128
N_EXPERTS = N_KEYS * N_KEYS
PEER_KEY_DIM = 256
PEER_HALF = PEER_KEY_DIM // 2
PEER_TOPK = 16
PEER_BLOCK = 128

N_ATTN_LAYERS = (DEPTH + 1) // 2
N_CHUNK_LAYERS = DEPTH // 2

kernel_name = "hybrid_diffattn_natten_chunkgmlp_peer_prefix"

def rms_norm(x):
    xf = x.astype(jnp.float32)
    y = xf * lax.rsqrt(jnp.mean(xf * xf, axis=-1, keepdims=True) + EPS)
    return y.astype(x.dtype)

def layer_norm(x, g, b):
    xf = x.astype(jnp.float32)
    mu = jnp.mean(xf, axis=-1, keepdims=True)
    var = jnp.mean(jnp.square(xf - mu), axis=-1, keepdims=True)
    return ((xf - mu) * lax.rsqrt(var + EPS)).astype(x.dtype) * g + b

def modulate(h, shift, scale):
    return rms_norm(h) * (1 + scale) + shift

def adaln(cond, w_mod, b_mod):
    return jnp.split(jax.nn.silu(cond) @ w_mod + b_mod, 6, axis=-1)

def axial_rope_tables(n_tokens, dim):
    axis_dim = dim // 2
    inv_freq = 1.0 / (ROPE_BASE ** (jnp.arange(0, axis_dim, 2, dtype=jnp.float32) / axis_dim))
    t = jnp.arange(n_tokens)
    row = (t // GRID_W).astype(jnp.float32)
    col = (t % GRID_W).astype(jnp.float32)
    ang = jnp.stack([row[:, None] * inv_freq, col[:, None] * inv_freq], axis=1)
    return jnp.cos(ang), jnp.sin(ang)

def apply_axial_rope(x, cos, sin):
    shp = x.shape
    xr = x.reshape(shp[:-1] + (2, 2, shp[-1] // 4)).astype(jnp.float32)
    x1, x2 = xr[..., 0, :], xr[..., 1, :]
    out = jnp.stack([x1 * cos - x2 * sin, x2 * cos + x1 * sin], axis=-2)
    return out.reshape(shp).astype(x.dtype)

def split_heads_ab(z):
    b, n, _ = z.shape
    qa, ka, va, qb, kb, vb = jnp.split(z, ATTN_SPLITS, axis=-1)
    qa = qa.reshape(b, n, A_HEADS, 2, A_QK_DIM).transpose(0, 2, 3, 1, 4)
    ka = ka.reshape(b, n, A_HEADS, 2, A_QK_DIM).transpose(0, 2, 3, 1, 4)
    va = va.reshape(b, n, A_HEADS, A_V_DIM).transpose(0, 2, 1, 3)
    qb = qb.reshape(b, n, B_HEADS, B_HEAD_DIM).transpose(0, 2, 1, 3)
    kb = kb.reshape(b, n, B_HEADS, B_HEAD_DIM).transpose(0, 2, 1, 3)
    vb = vb.reshape(b, n, B_HEADS, B_HEAD_DIM).transpose(0, 2, 1, 3)
    return qa, ka, va, qb, kb, vb

def merge_heads_ab(oa, ob, w_out):
    b, _, n, _ = oa.shape
    oa = oa.transpose(0, 2, 1, 3).reshape(b, n, A_V_W)
    ob = ob.transpose(0, 2, 1, 3).reshape(b, n, B_W)
    return jnp.concatenate([oa, ob], axis=-1) @ w_out

def diff_attention(q, k, v, lam, lam_init, subln_g):
    b, h, _, nq, d = q.shape
    scale = d ** -0.5
    qb = jnp.moveaxis(q.reshape(b, h, 2, nq // Q_BLOCK, Q_BLOCK, d), 3, 0)

    def one_block(q_blk):
        s = jnp.einsum("bhmqd,bhmkd->bhmqk", q_blk, k).astype(jnp.float32) * scale
        p = jax.nn.softmax(s, axis=-1)
        a = p[:, :, 0] - lam * p[:, :, 1]
        return jnp.einsum("bhqk,bhkd->bhqd", a.astype(v.dtype), v)

    o = lax.map(one_block, qb)
    o = jnp.moveaxis(o, 0, 2).reshape(b, h, nq, 2 * d)
    return rms_norm(o) * subln_g * (1.0 - lam_init)

def neighbourhood_attention(q, k, v, k_ctx, v_ctx, rpb):
    b, h, n, d = q.shape
    rows = n // GRID_W
    wr = min(NA_ROWS, rows)
    nk = wr * NA_COLS
    scale = d ** -0.5
    qg = q.reshape(b, h, rows, GRID_W, d)
    kg = k.reshape(b, h, rows, GRID_W, d)
    vg = v.reshape(b, h, rows, GRID_W, d)
    cols = np.arange(GRID_W)
    col_start = np.clip(cols - NA_COLS // 2, 0, GRID_W - NA_COLS)
    col_idx = col_start[:, None] + np.arange(NA_COLS)[None, :]
    rpb_cols = rpb[:, :, col_idx - cols[:, None] + (NA_COLS - 1)]

    def one_row(r):
        r0 = jnp.clip(r - wr // 2, 0, rows - wr)
        k_nb = lax.dynamic_slice_in_dim(kg, r0, wr, axis=2)[:, :, :, col_idx]
        v_nb = lax.dynamic_slice_in_dim(vg, r0, wr, axis=2)[:, :, :, col_idx]
        q_r = lax.dynamic_index_in_dim(qg, r, axis=2, keepdims=False)
        bias = jnp.take(rpb_cols, r0 + jnp.arange(wr) - r + (NA_ROWS - 1), axis=1)
        s_loc = (jnp.einsum("bhqd,bhrqwd->bhqrw", q_r, k_nb).astype(jnp.float32) * scale
                 + jnp.transpose(bias, (0, 2, 1, 3)).astype(jnp.float32))
        s_ctx = jnp.einsum("bhqd,bhkd->bhqk", q_r, k_ctx).astype(jnp.float32) * scale
        s = jnp.concatenate([s_loc.reshape(b, h, GRID_W, nk), s_ctx], axis=-1)
        p = jax.nn.softmax(s, axis=-1).astype(v.dtype)
        p_loc = p[..., :nk].reshape(b, h, GRID_W, wr, NA_COLS)
        return (jnp.einsum("bhqrw,bhrqwd->bhqd", p_loc, v_nb)
                + jnp.einsum("bhqk,bhkd->bhqd", p[..., nk:], v_ctx))

    o = lax.map(one_row, jnp.arange(rows))
    return jnp.transpose(o, (1, 2, 0, 3, 4)).reshape(b, h, n, d)

def dense_attention(q, k, v):
    s = jnp.einsum("bhqd,bhkd->bhqk", q, k).astype(jnp.float32) * (q.shape[-1] ** -0.5)
    return jnp.einsum("bhqk,bhkd->bhqd", jax.nn.softmax(s, axis=-1).astype(v.dtype), v)

def mixer_diff_na(xl, xc, w_in, w_out, lam, lam_init, subln_g, rpb, need_ctx):
    qa_l, ka_l, va_l, qb_l, kb_l, vb_l = split_heads_ab(xl @ w_in)
    qa_c, ka_c, va_c, qb_c, kb_c, vb_c = split_heads_ab(xc @ w_in)
    cos, sin = axial_rope_tables(xl.shape[1], A_QK_DIM)
    qa_l = apply_axial_rope(qa_l, cos, sin)
    ka_l = apply_axial_rope(ka_l, cos, sin)
    ka_all = jnp.concatenate([ka_l, ka_c], axis=3)
    va_all = jnp.concatenate([va_l, va_c], axis=2)
    oa_l = diff_attention(qa_l, ka_all, va_all, lam, lam_init, subln_g)
    ob_l = neighbourhood_attention(qb_l, kb_l, vb_l, kb_c, vb_c, rpb)
    out_l = merge_heads_ab(oa_l, ob_l, w_out)
    if not need_ctx:
        return out_l, None
    oa_c = diff_attention(qa_c, ka_c, va_c, lam, lam_init, subln_g)
    ob_c = dense_attention(qb_c, kb_c, vb_c)
    return out_l, merge_heads_ab(oa_c, ob_c, w_out)

def chunk_spatial_gating(x, w_in, b_in, ln_g, ln_b, w_s, b_s, w_out):
    b, n, _ = x.shape
    z = jax.nn.gelu(x @ w_in + b_in)
    u, v = jnp.split(z, 2, axis=-1)
    v = layer_norm(v, ln_g, ln_b).reshape(b, n // CHUNK, CHUNK, C_GROUPS, C_GROUP_W)
    sv = jnp.einsum("gpq,bnqgc->bnpgc", w_s, v) + b_s.T[:, :, None]
    return (u * sv.reshape(b, n, C_WIDTH)) @ w_out

def peer(x, w_query, sub_keys, u_emb, v_emb):
    b, n, d = x.shape
    xt = x.reshape(b * n // PEER_BLOCK, PEER_BLOCK, d)

    def one_block(xb):
        q = (xb @ w_query).reshape(PEER_BLOCK, PEER_HEADS, 2, PEER_HALF)
        s = jnp.einsum("thpd,hpkd->thpk", q, sub_keys).astype(jnp.float32)
        s1, i1 = lax.top_k(s[:, :, 0], PEER_TOPK)
        s2, i2 = lax.top_k(s[:, :, 1], PEER_TOPK)
        cand = (s1[..., :, None] + s2[..., None, :]).reshape(PEER_BLOCK, PEER_HEADS, PEER_TOPK * PEER_TOPK)
        sc, flat = lax.top_k(cand, PEER_TOPK)
        e = (jnp.take_along_axis(i1, flat // PEER_TOPK, axis=-1) * N_KEYS
             + jnp.take_along_axis(i2, flat % PEER_TOPK, axis=-1))
        g = jax.nn.softmax(sc, axis=-1)
        a = jax.nn.gelu(jnp.einsum("thkd,td->thk", u_emb[e], xb).astype(jnp.float32))
        return jnp.einsum("thk,thkd->td", (g * a).astype(xb.dtype), v_emb[e])

    return lax.map(one_block, xt).reshape(b, n, d)

def setup_inputs(seed: int = 0) -> dict:
    key = jax.random.key(seed)
    ks = jax.random.split(key, 26)
    D = D_MODEL
    La, Lc = N_ATTN_LAYERS, N_CHUNK_LAYERS

    def nrm(k, shape, s):
        return jax.random.normal(k, shape, jnp.float32) * s

    return {
        "x": nrm(ks[0], (BATCH, SEQ, D), 1.0),
        "c": nrm(ks[1], (BATCH, D), 1.0),
        "ctx": nrm(ks[2], (BATCH, CTX_LEN, D), 1.0),
        "c_ctx": nrm(ks[3], (D,), 1.0),
        "w_mod": nrm(ks[4], (DEPTH, D, 6 * D), D ** -0.5),
        "b_mod": nrm(ks[5], (DEPTH, 6 * D), 0.02),
        "attn_w_in": nrm(ks[6], (La, D, ATTN_IN_W), D ** -0.5),
        "attn_w_out": nrm(ks[7], (La, ATTN_OUT_W, D), ATTN_OUT_W ** -0.5),
        "lambda_q1": nrm(ks[8], (La, A_QK_DIM), 0.1),
        "lambda_k1": nrm(ks[9], (La, A_QK_DIM), 0.1),
        "lambda_q2": nrm(ks[10], (La, A_QK_DIM), 0.1),
        "lambda_k2": nrm(ks[11], (La, A_QK_DIM), 0.1),
        "subln_g": 1.0 + nrm(ks[12], (La, A_V_DIM), 0.05),
        "na_rpb": nrm(ks[13], (La, B_HEADS, 2 * NA_ROWS - 1, 2 * NA_COLS - 1), 0.5),
        "chunk_w_in": nrm(ks[14], (Lc, D, 2 * C_WIDTH), D ** -0.5),
        "chunk_b_in": nrm(ks[15], (Lc, 2 * C_WIDTH), 0.02),
        "chunk_ln_g": 1.0 + nrm(ks[16], (Lc, C_WIDTH), 0.05),
        "chunk_ln_b": nrm(ks[17], (Lc, C_WIDTH), 0.02),
        "chunk_w_s": nrm(ks[18], (Lc, C_GROUPS, CHUNK, CHUNK), CHUNK ** -0.5),
        "chunk_b_s": 1.0 + nrm(ks[19], (Lc, C_GROUPS, CHUNK), 0.05),
        "chunk_w_out": nrm(ks[20], (Lc, C_WIDTH, D), C_WIDTH ** -0.5),
        "peer_w_query": nrm(ks[21], (DEPTH, D, PEER_HEADS * PEER_KEY_DIM), D ** -0.5),
        "peer_sub_keys": nrm(ks[22], (DEPTH, PEER_HEADS, 2, N_KEYS, PEER_HALF), PEER_HALF ** -0.5),
        "peer_u": nrm(ks[23], (DEPTH, N_EXPERTS, D), D ** -0.5),
        "peer_v": nrm(ks[24], (DEPTH, N_EXPERTS, D), PEER_HEADS ** -0.5),
        "final_norm_g": 1.0 + nrm(ks[25], (D,), 0.05),
    }

def reference(x, c, ctx, c_ctx, w_mod, b_mod, attn_w_in, attn_w_out, lambda_q1, lambda_k1,
              lambda_q2, lambda_k2, subln_g, na_rpb, chunk_w_in, chunk_b_in, chunk_ln_g, chunk_ln_b,
              chunk_w_s, chunk_b_s, chunk_w_out, peer_w_query, peer_sub_keys, peer_u, peer_v,
              final_norm_g):
    h, hc = x, ctx
    for i in range(DEPTH):
        is_attn = i % 2 == 0
        need_ctx = any(j % 2 == 0 for j in range(i + 1, DEPTH))
        sh1, sc1, g1, sh2, sc2, g2 = [m[:, None, :] for m in adaln(c, w_mod[i], b_mod[i])]
        if is_attn or need_ctx:
            csh1, csc1, cg1, csh2, csc2, cg2 = adaln(c_ctx, w_mod[i], b_mod[i])
        if is_attn:
            a = i // 2
            lam_init = 0.8 - 0.6 * math.exp(-0.3 * i)
            lam = (jnp.exp(jnp.sum(lambda_q1[a] * lambda_k1[a]).astype(jnp.float32))
                   - jnp.exp(jnp.sum(lambda_q2[a] * lambda_k2[a]).astype(jnp.float32)) + lam_init)
            out_l, out_c = mixer_diff_na(modulate(h, sh1, sc1), modulate(hc, csh1, csc1),
                                         attn_w_in[a], attn_w_out[a], lam, lam_init, subln_g[a],
                                         na_rpb[a], need_ctx)
        else:
            m = i // 2
            cw = (chunk_w_in[m], chunk_b_in[m], chunk_ln_g[m], chunk_ln_b[m], chunk_w_s[m], chunk_b_s[m], chunk_w_out[m])
            out_l = chunk_spatial_gating(modulate(h, sh1, sc1), *cw)
            out_c = chunk_spatial_gating(modulate(hc, csh1, csc1), *cw) if need_ctx else None
        h = h + g1 * out_l
        h = h + g2 * peer(modulate(h, sh2, sc2), peer_w_query[i], peer_sub_keys[i], peer_u[i], peer_v[i])
        if need_ctx:
            hc = hc + cg1 * out_c
            hc = hc + cg2 * peer(modulate(hc, csh2, csc2), peer_w_query[i], peer_sub_keys[i], peer_u[i], peer_v[i])
    return rms_norm(h) * final_norm_g


_drawn_inputs = setup_inputs


def setup_inputs(seed=0):
    import zlib

    import numpy as np

    out = dict(_drawn_inputs(seed))
    spreads = {}
    factors = {'lambda_k1': 5.891, 'lambda_q2': 6.397, 'chunk_b_in': 3.39, 'chunk_ln_b': 4.607}
    for name, (base, spread) in spreads.items():
        noise = np.random.default_rng([zlib.crc32(name.encode()), seed]).standard_normal(out[name].shape)
        drawn = base * np.exp(spread * noise) if base else spread * noise
        out[name] = jnp.asarray(drawn.astype(out[name].dtype))
    for name, factor in factors.items():
        out[name] = (out[name] * factor).astype(out[name].dtype)
    return out
```

```python
import math
from contextlib import ExitStack

import numpy as np

import concourse.bass as bass
from concourse import mybir

F32 = mybir.dt.float32
F32R = mybir.dt.float32r
U32 = mybir.dt.uint32
ACT = mybir.ActivationFunctionType
ALU = mybir.AluOpType
AX = mybir.AxisListType.X

P = 128
D = 1024
KT = D // P
T = 512
TT = T // P
TC = 256
TK = T + TC
KK = TK // P
CW = 512
NMOD = 6 * D // CW
GRID_W = 64
NA_ROWS, NA_COLS = 8, 16
HA, HB, DH = 4, 8, 64
QK_SCALE = DH ** -0.5
LAM_INIT = 0.8 - 0.6 * math.exp(-0.3 * 0)
EPS = 1e-6
PH, NKEY, TOPK = 8, 128, 16
HP = 2 * PH
NE = NKEY * NKEY
NG = NKEY // 2
DEPTH = 2
NEG = -3.0e38
MASKED = -1.0e30
RING = 3
TOK = 8
NB = P // TOK

BASE = 17408


def at_least(eng, sem, value):
    if isinstance(value, int) and value <= 0:
        return
    eng.wait_ge(sem, value)


class Chain:

    def __init__(self, eng, sem, start=0):
        self.eng, self.sem, self.n = eng, sem, start

    def __call__(self, ins):
        self.n = self.n + 1
        ins.then_inc(self.sem, 1)
        self.eng.wait_ge(self.sem, self.n)


def backbone(nc, a, out):
    with ExitStack() as ctx:
        def sb(name, kib, shape, dt=F32):
            return nc.alloc_sbuf_tensor_at(name, shape, dt, offset=BASE + int(kib * 1024))

        def sem(name):
            return ctx.enter_context(nc.semaphore(name))

        hT = sb("hT", 0, [P, KT, T])
        mods = sb("mods", 16, [P, DEPTH, 6 * KT, 2])
        ones = sb("ones", 16.75, [P, P])
        ident = sb("ident", 17.25, [P, P])
        iota = sb("iota", 17.75, [P, P])
        cond = sb("cond", 18.25, [P, KT, 2])
        condS = sb("condS", 18.375, [P, KT, 2])
        bmod = sb("bmod", 18.5, [P, DEPTH, 6 * KT])
        fing = sb("fing", 19, [P, KT])
        rinv = sb("rinv", 20, [P, T])
        rms = sb("rms", 204, [P, T])
        bu = sb("bu", 22, [P, KT])
        carrier = sb("carrier", 22.6875, [P, 1])
        iota16 = sb("iota16", 22.125, [P, TOPK])
        lamv = sb("lamv", 22.25, [P, 8])
        sublg = sb("sublg", 22.5, [P, 1])
        subg8 = sb("subg8", 22.53125, [P, 1])
        ones_row = sb("ones_row", 19.25, [1, P])
        lamtmp = sb("lamtmp", 104, [P, 2, DH])
        lamin = sb("lamin", 23, [P, 4, DH])
        xm = sb("xm", 24, [P, KT, T])
        sq = sb("sq", 128, [P, 2, T])
        ring = [sb(f"ring{n}", 134 + 16 * n, [P, KT, CW]) for n in range(RING)]
        xc = sb("xc", 40, [P, KT, TC])
        ctxT = sb("ctxT", 48, [P, KT, TC])
        qaT = sb("qaT", 56, [P, HA, T])
        kaT = sb("kaT", 64, [P, HA, TK])
        qbT = sb("qbT", 76, [P, HB // 2, T])
        kbT = sb("kbT", 84, [P, HB // 2, TK])
        va = sb("va", 96, [P, KK, CW])
        vb = sb("vb", 108, [P, KK, CW])
        cosT = sb("cosT", 120, [P, T])
        sinT = sb("sinT", 122, [P, T])
        ropein = sb("ropein", 124, [P, 2, T])
        rot = sb("rot", 132, [P, P])
        mask = sb("mask", 132.5, [P, GRID_W])
        ropetmp = sb("ropetmp", 198, [P, 2, T])
        oT = sb("oT", 24, [P, KT, T])
        btab = sb("btab", 40, [P, 2, 16, GRID_W])
        osq = sb("osq", 48, [P, T])
        orinv = sb("orinv", 50, [P, T])
        Ebuf = sb("Ebuf", 182, [P, 4, TK])
        ATbuf = sb("ATbuf", 120, [P, 2, TK])
        Abuf = sb("Abuf", 126, [P, 2, TK])
        Sbuf = sb("Sbuf", 194, [P, 2, TK])
        mx = sb("mx", 200, [P, 64])
        nmx = sb("nmx", 200.25, [P, 64])
        zs = sb("zs", 200.5, [P, 64])
        rz = sb("rz", 200.75, [P, 64])
        nlr = sb("nlr", 201, [P, 16])
        vsb = sb("vsb", 40, [P, TT, D])
        uT = sb("uT", 56, [P, KT, T])
        lng = sb("lng", 72, [P, D])
        lnb = sb("lnb", 76, [P, D])
        bsb = sb("bsb", 80, [P, KT, P])
        wsT = sb("wsT", 84, [P, KT, P])
        yT = sb("yT", 88, [P, KT, T])
        svb = sb("svb", 104, [P, 2, T])
        bvrow = sb("bvrow", 116, [1, D])
        bnst = sb("bnst", 120, [P, TT, 2, 6])
        bnag = sb("bnag", 120.25, [P, TT, 2])
        rstd = sb("rstd", 120.5, [P, 2, TT])
        qT = sb("qT", 40, [P, HP, T])
        keysT = sb("keysT", 72, [P, HP, NKEY])
        qs = sb("qs", 80, [P, HP, P])
        S = sb("S", 88, [P, HP, NKEY])
        S2 = sb("S2", 96, [P, HP, NKEY])
        eq = sb("eq", 104, [P, PH, TOPK, TOPK])
        Ahot = sb("Ahot", 112, [P, 2, TOK, P])
        Bhot = sb("Bhot", 120, [P, 2, TOK, P])
        topv = sb("topv", 128, [P, PH, 2, TOPK])
        topi = sb("topi", 129, [P, PH, 2, TOPK], U32)
        candv = sb("candv", 130, [P, PH, TOPK])
        candi = sb("candi", 130.5, [P, PH, TOPK], U32)
        rank = sb("rank", 131, [P, 2, PH, TOPK], U32)
        pick = sb("pick", 132, [P, 3, PH, TOPK])
        zsum = sb("zsum", 133.5, [P, 2, PH])
        pickT = sb("pickT", 198, [P, 3, P])
        G_st = sb("G_st", 134, [P, NKEY, P])
        cand = S[:, :, :].rearrange("p (h a) n -> p h (a n)", a=2)
        cand2 = S2[:, :, :].rearrange("p (h a) n -> p h (a n)", a=2)
        cand4 = S[:, :, :].rearrange("p a n -> p (a n)").rearrange("p (h a b) -> p h a b", h=PH, a=TOPK)
        xhi = sb("xhi", 40, [P, KT, T], F32R)
        xlo = sb("xlo", 56, [P, KT, T], F32R)
        Uraw = sb("Uraw", 72, [P, 2, KT, 2 * P])
        Vraw = sb("Vraw", 88, [P, 2, 2, D])
        Uhi = sb("Uhi", 104, [P, 2, KT, 2 * P], F32R)
        Ulo = sb("Ulo", 120, [P, 2, KT, 2 * P], F32R)
        Vhi = sb("Vhi", 136, [P, 2, 2, D], F32R)
        Vlo = sb("Vlo", 152, [P, 2, 2, D], F32R)
        Gin = sb("Gin", 168, [P, 2, 2, T])
        act = sb("act", 176, [P, 2, T])
        Hf = sb("Hf", 180, [P, 2, T])
        Hhi = sb("Hhi", 184, [P, 2, 2, T], F32R)
        Hlo = sb("Hlo", 192, [P, 2, 2, T], F32R)

        G_dram = nc.dram_tensor("G_scratch", (DEPTH, NG, P, 2, TT, P), F32, kind="Internal").ap()
        ps = ctx.enter_context(nc.psum_tensor("ps", [P, 8, T], F32))

        def wide(pair):
            return ps[:, 2 * pair:2 * pair + 2, :].rearrange("p b n -> p (b n)")

        NIN, NOUT, NQ, NGI = 6, 2, 4, 4
        chunks = ([("w_mod", 0, c) for c in range(NMOD)] + [("attn_in", 0, c) for c in range(NIN)]
                  + [("w_mod", 1, c) for c in range(NMOD)] + [("attn_out", 0, c) for c in range(NOUT)]
                  + [("query", 0, c) for c in range(NQ)] + [("gate_in", 0, c) for c in range(NGI)]
                  + [("gate_out", 0, c) for c in range(NOUT)] + [("query", 1, c) for c in range(NQ)])
        W_MOD = [0, NMOD + NIN]
        W_IN = NMOD
        W_OUT = 2 * NMOD + NIN
        W_Q0 = W_OUT + NOUT
        W_GIN = W_Q0 + NQ
        W_GOUT = W_GIN + NGI
        W_Q = [W_Q0, W_GOUT + NOUT]
        slots = [ring[n % RING] for n in range(len(chunks))]

        in_jobs = []

        def in_job(kind, c, width, dst, operands):
            rope = sum(job[0] == "rope" for job in in_jobs)
            in_jobs.append((kind, ps[:, len(in_jobs) % 4, 0:width], dst, rope, c, operands))

        def columns(c, f, x):
            slot = slots[W_IN + c]
            return lambda k: (slot[:, k, f * P:(f + 1) * P], x[:, k, :])

        def tokens(c, x, tt):
            slot = slots[W_IN + c]
            return lambda k: (x[:, k, tt * P:(tt + 1) * P], slot[:, k, :])

        for c, (name, dst) in enumerate((("rope", qaT), ("rope", kaT), ("v", va), ("copy", qbT), ("copy", kbT),
                                         ("v", vb))):
            if name == "v":
                for tt in range(TT):
                    in_job("copy", c, CW, dst[:, tt, :], tokens(c, xm, tt))
                for tt in range(TC // P):
                    in_job("copy", c, CW, dst[:, TT + tt, :], tokens(c, xc, tt))
                continue
            for f in range(4):
                in_job(name, c, T, dst[:, f, 0:T], columns(c, f, xm))
            if c in (1, 4):
                for f in range(4):
                    in_job("copy", c, TC, dst[:, f, T:TK], columns(c, f, xc))

        consts_in = sem("consts_in")
        x_in = sem("x_in")
        w_in = [sem(f"w_in{n}") for n in range(RING)]
        mod_mm = sem("mod_mm")
        cond_ready = sem("cond_ready")
        mod_ready = sem("mod_ready")
        dve_step = sem("dve_step")
        lam_sum = sem("lam_sum")
        lam_exp = sem("lam_exp")
        lam_ready = sem("lam_ready")
        sq_ready = sem("sq_ready")
        sq_used = sem("sq_used")
        ms_ready = sem("ms_ready")
        rms_ready = sem("rms_ready")
        oms_ready = sem("oms_ready")
        orms_ready = sem("orms_ready")
        var_ready = sem("var_ready")
        std_ready = sem("std_ready")
        rinv_ready = sem("rinv_ready")
        x_scaled = sem("x_scaled")
        x_ready = sem("x_ready")
        proj_mm = sem("proj_mm")
        proj_out = sem("proj_out")
        rope_raw = sem("rope_raw")
        rope_mm = sem("rope_mm")
        rope_out = sem("rope_out")
        bias_in = [sem(f"bias_in{n}") for n in range(2)]
        score_mm = sem("score_mm")
        nmax_ready = sem("nmax_ready")
        exp_done = sem("exp_done")
        probs_ready = sem("probs_ready")
        probsT_mm = sem("probsT_mm")
        probsT_ready = sem("probsT_ready")
        av_mm = sem("av_mm")
        o_out = sem("o_out")
        osq_ready = sem("osq_ready")
        osum_mm = sem("osum_mm")
        o_normed = sem("o_normed")
        h_mm = sem("h_mm")
        h_added = sem("h_added")
        q_mm = sem("q_mm")
        q_out = sem("q_out")
        keys_in = sem("keys_in")
        qs_ready = sem("qs_ready")
        score_done = sem("score_done")
        S_ready = sem("S_ready")
        gate_logits = sem("gate_logits")
        gate_exp = sem("gate_exp")
        pick_ready = sem("pick_ready")
        pickT_out = sem("pickT_out")
        route_step = sem("route_step")
        bias_used = sem("bias_used")
        H_step = sem("H_step")
        pickT_mm = sem("pickT_mm")
        hot_ready = sem("hot_ready")
        G_mm = sem("G_mm")
        G_out = sem("G_out")
        G_stored = sem("G_stored")
        x_hi = sem("x_hi")
        x_split = sem("x_split")
        U_in = [sem(f"U_in{n}") for n in range(2)]
        V_in = [sem(f"V_in{n}") for n in range(2)]
        G_in = [sem(f"G_in{n}") for n in range(2)]
        U_hi = sem("U_hi")
        U_split = sem("U_split")
        V_hi = sem("V_hi")
        V_split = sem("V_split")
        up_mm = sem("up_mm")
        act_ready = sem("act_ready")
        H_ready = sem("H_ready")
        dn_mm = sem("dn_mm")
        dn_added = sem("dn_added")
        gl_in = sem("gl_in")
        v_mm = sem("v_mm")
        v_gelu = sem("v_gelu")
        v_normed = sem("v_normed")
        u_mm = sem("u_mm")
        u_gelu = sem("u_gelu")
        sv_mm = sem("sv_mm")
        y_ready = sem("y_ready")
        stored = sem("stored")

        units = []
        for h in range(HA):
            for qt in range(TT):
                units.append(("diff", h, qt))
        for h in range(HB):
            for qt in range(TT):
                units.append(("near", h, qt))
        job_of = []
        njobs = 0
        for kind, h, qt in units:
            job_of.append(njobs)
            njobs += 2 if kind == "diff" else 1
        HEAD_END = HA * TT
        sh1, sc1, g1, sh2, sc2, g2 = [KT * n for n in range(6)]
        NORMS = [(ctxT, TC, xc, 0, sh1, sc1, 1), (hT, T, xm, 0, sh1, sc1, 0), (hT, T, xm, 0, sh2, sc2, 0),
                 (hT, T, xm, 1, sh1, sc1, 0), (hT, T, xm, 1, sh2, sc2, 0), (hT, T, xm, None, None, None, 0)]
        n_mixer = [KT, 2 * KT]
        n_peer = [KT * NG, 2 * KT * NG]

        def chunk_used(n):
            kind, layer, c = chunks[n]
            if kind == "w_mod":
                return mod_mm, layer * NMOD + c + 1
            if kind == "attn_in":
                return proj_mm, sum(job[4] <= c for job in in_jobs)
            if kind == "attn_out":
                return h_mm, 4 * (c + 1)
            if kind == "gate_out":
                return h_mm, KT + 4 * (c + 1)
            if kind == "query":
                return q_mm, layer * HP + 4 * (c + 1)
            return (v_mm, TT * (c + 1)) if c < 2 else (u_mm, 4 * (c - 1))

        block = ctx.enter_context(nc.Block())

        @block.sync
        def _(sp):
            sp.sem_inc(G_stored, 32)
            sp.dma_start(cond[:, :, :], a["cond"]).then_inc(consts_in, 16)
            sp.dma_start(bmod[:, :, :], a["b_mod"]).then_inc(consts_in, 16)

            def load_chunk(n):
                if n >= RING:
                    sp.wait_ge(*chunk_used(n - RING))
                kind, layer, c = chunks[n]
                sp.dma_start(slots[n][:, :, :],
                             a[kind][layer].rearrange("(k p) n -> p k n", p=P)[:, :, c * CW:(c + 1) * CW]
                             ).then_inc(w_in[n % RING], 16)

            for n in range(RING):
                load_chunk(n)
            sp.dma_start(hT[:, :, :], a["xT"].rearrange("(k p) t -> p k t", p=P)).then_inc(x_in, 16)
            sp.dma_start(ctxT[:, :, :], a["ctxT"].rearrange("(k p) t -> p k t", p=P)).then_inc(x_in, 16)
            for dst, name in ((ones, "ones"), (ident, "ident"), (iota, "iota"), (iota16, "iota16"),
                              (fing, "final_g"), (bu, "bu"), (cosT, "cosT"), (sinT, "sinT"), (rot, "rot"),
                              (mask, "mask"), (sublg, "subln_g"), (lamin, "lam"), (ones_row, "ones_row")):
                sp.dma_start(dst[tuple(slice(None) for _ in dst.shape)], a[name]).then_inc(x_in, 16)
            for n in range(RING, W_IN + NIN + RING):
                load_chunk(n)
            events = [(4 * i + 3, "chunk", W_IN + NIN + RING + i) for i in range(NMOD)]
            events += [(0 if h < 2 else HEAD_END + 4 * (h - 1), "bias", h) for h in range(HB)]
            for _, what, n in sorted(events):
                if what == "chunk":
                    load_chunk(n)
                    continue
                if n < 2:
                    sp.wait_ge(proj_mm, len(in_jobs))
                else:
                    sp.wait_ge(bias_used, n - 1)
                sp.dma_start(btab[:, n % 2, :, :], a["btab"][n]).then_inc(bias_in[n % 2], 16)
            for n in range(W_IN + NIN + RING + NMOD, W_GIN):
                load_chunk(n)

            def peer_loads(layer):
                sp.wait_ge(h_added, n_mixer[layer])
                sp.dma_start(keysT[:, :, :], a["keysT"][layer]).then_inc(keys_in, 16)
                with sp.Fori(0, TT) as r:
                    sp.wait_ge(G_out, (r + (layer * TT + 1)) * (P // 4) + 4)
                    for j in range(2):
                        sp.dma_start(G_dram[layer, :, :, j, bass.ds(r, 1), :].rearrange("g p r t -> p g (r t)"),
                                     G_st[:, :, :].rearrange("p (g j) t -> p g j t", j=2)[:, :, j, :]
                                     ).then_inc(G_stored, 16)
                sp.wait_ge(G_stored, 32 * (TT * (layer + 1) + 1))

                def load_group(g, par):
                    n = g + layer * NG
                    at_least(sp, U_split, n - 1)
                    sp.dma_start(Uraw[:, par, :, :], a["UT"][layer][bass.ds(g, 1)].rearrange("o p k e -> p (o k) e")
                                 ).then_inc(U_in[par], 16)
                    at_least(sp, V_split, n - 1)
                    sp.dma_start(Vraw[:, par, :, :], a["V"][layer][bass.ds(g, 1)].rearrange("o j p d -> p (o j) d")
                                 ).then_inc(V_in[par], 16)
                    at_least(sp, H_ready, (n - 1) * 2)
                    sp.dma_start(Gin[:, par, :, :], G_dram[layer][bass.ds(g, 1)].rearrange("o p j r t -> p (o j) (r t)")
                                 ).then_inc(G_in[par], 16)

                for g in range(2):
                    load_group(g, g)
                with sp.Fori(1, NG // 2) as it:
                    for par in range(2):
                        load_group(it * 2 + par, par)

            peer_loads(0)
            sp.wait_ge(h_added, n_mixer[0])
            sp.wait_ge(dn_added, n_peer[0])
            for n in range(W_GIN, W_GIN + RING):
                load_chunk(n)
            for dst, name in ((lng, "ln_g"), (lnb, "ln_b"), (bsb, "b_s")):
                sp.dma_start(dst[tuple(slice(None) for _ in dst.shape)],
                             a[name].partition_broadcast(P)).then_inc(gl_in, 16)
            sp.dma_start(wsT[:, :, :], a["w_sT"]).then_inc(gl_in, 16)
            sp.dma_start(bvrow[:, :], a["bv"]).then_inc(gl_in, 16)
            for n in range(W_GIN + RING, len(chunks)):
                load_chunk(n)
            peer_loads(1)
            for k in range(KT):
                sp.wait_ge(x_scaled, 5 * KT + k + 1)
                sp.dma_start(out[k * P:(k + 1) * P, :], xm[:, k, :]).then_inc(stored, 16)
            sp.wait_ge(stored, 16 * KT)

        @block.scalar
        def _(act_e):
            act_e.sem_inc(G_out, 4)
            act_e.wait_ge(consts_in, 32)
            nc.scalar.activation(condS[:, :, :], cond[:, :, :], ACT.Silu).then_inc(cond_ready, 1)
            act_e.wait_ge(x_in, 16 * 15)

            def norm(n):
                src, width, dst, layer, sh, sc, who = NORMS[n]
                for k in range(KT):
                    at_least(act_e, sq_used, n * KT + k - 1)
                    nc.scalar.activation(sq[:, k % 2, 0:width], src[:, k, :], ACT.Square).then_inc(sq_ready, 1)
                act_e.wait_ge(ms_ready, n + 1)
                nc.scalar.activation(rms[:, 0:width], rms[:, 0:width], ACT.Sqrt).then_inc(rms_ready, 1)
                if sh is None:
                    return
                for k in range(KT):
                    act_e.wait_ge(x_scaled, n * KT + k + 1)
                    nc.scalar.activation(dst[:, k, :], dst[:, k, :], ACT.Identity,
                                         bias=mods[:, layer, sh + k, who:who + 1]).then_inc(x_ready, 1)

            act_e.wait_ge(mod_ready, 1)
            norm(0)
            norm(1)

            for j, (kind, bank, dst, rope, _, _) in enumerate(in_jobs):
                act_e.wait_ge(proj_mm, j + 1)
                if kind == "copy":
                    nc.scalar.copy(dst, bank).then_inc(proj_out, 1)
                else:
                    at_least(act_e, rope_out, rope - 1)
                    nc.scalar.copy(ropein[:, rope % 2, :], bank).then_inc(rope_raw, 1)
            act_e.wait_ge(lam_sum, 1)
            nc.scalar.activation(lamv[:, 2:4], lamv[:, 0:2], ACT.Exp).then_inc(lam_exp, 1)

            def evac_probsT(u):
                act_e.wait_ge(probsT_mm, u + 1)
                at_least(act_e, av_mm, u - 1)
                nc.scalar.copy(ATbuf[:, u % 2, :], wide(2)[:, 0:TK]).then_inc(probsT_ready, 1)

            for u, (kind, h, qt) in enumerate(units):
                j = job_of[u]
                for m in range(2 if kind == "diff" else 1):
                    act_e.wait_ge(nmax_ready, j + m + 1)
                    first_over = [w for w in range(u) if job_of[w] <= j + m - 4]
                    if first_over:
                        act_e.wait_ge(probs_ready, first_over[-1] + 1)
                    src = wide((j + m) % 2)[:, 0:TK] if kind == "diff" else Sbuf[:, (j + m) % 2, :]
                    nc.scalar.activation(Ebuf[:, (j + m) % 4, :], src, ACT.Exp, bias=nmx[:, j + m:j + m + 1],
                                         scale=QK_SCALE if kind == "diff" else 1.0,
                                         accum_out=zs[:, j + m:j + m + 1]).then_inc(exp_done, 1)
                if u >= 1:
                    evac_probsT(u - 1)
                    if units[u - 1][0] == "diff" and units[u - 1][2] == TT - 1:
                        act_e.wait_ge(oms_ready, units[u - 1][1] + 1)
                        nc.scalar.activation(osq[:, :], osq[:, :], ACT.Sqrt).then_inc(orms_ready, 1)
            evac_probsT(len(units) - 1)

            def peer_route(layer):
                for n in range(HP):
                    act_e.wait_ge(q_mm, layer * HP + n + 1)
                    nc.scalar.copy(qT[:, n, :], ps[:, n % 4, :]).then_inc(q_out, 1)
                act_e.wait_ge(q_out, (layer + 1) * HP)
                with act_e.Fori(0, TT) as r:
                    tile = r + layer * TT
                    act_e.wait_ge(score_done, tile + 1)
                    nc.scalar.copy(qs[:, :, :], qT[:, :, bass.ds(r * P, P)]).then_inc(qs_ready, 1)
                    act_e.wait_ge(score_done, tile + 2)
                    act_e.wait_ge(pick_ready, tile + 1)
                    for b in range(4):
                        nc.scalar.copy(S[:, 4 * b:4 * b + 4, :].rearrange("p a n -> p (a n)"), ps[:, 4 + b, :]
                                       ).then_inc(S_ready, 1)
                    act_e.wait_ge(gate_logits, tile + 1)
                    nc.scalar.activation(pick[:, 2, :, :], pick[:, 2, :, :], ACT.Exp).then_inc(gate_exp, 1)
                    act_e.wait_ge(G_stored, (tile + 1) * 32)
                    with act_e.Fori(0, NB // 2) as it:
                        for par in range(2):
                            for b in range(2):
                                act_e.wait_ge(G_mm, (tile * NB + it * 2 + par) * 2 + b + 5)
                                nc.scalar.copy(
                                    G_st[:, :, bass.ds((it * 2 + par) * TOK + 4 * b, 4)].rearrange("p i t -> p t i"),
                                    ps[:, 2 * par + b, :].rearrange("p (t i) -> p t i", t=4)).then_inc(G_out, 1)

            def peer_dense(layer):
                act_e.wait_ge(G_stored, 32 * ((layer + 1) * TT + 1))
                for k in range(KT):
                    nc.scalar.copy(xhi[:, k, :], xm[:, k, :]).then_inc(x_hi, 1)

                def split_U(g, par, it):
                    n = g + layer * NG
                    act_e.wait_ge(U_in[par], (it + (layer * (NG // 2) + 1)) * 16)
                    at_least(act_e, up_mm, (n - 1) * 2)
                    nc.scalar.copy(Uhi[:, par, :, :], Uraw[:, par, :, :]).then_inc(U_hi, 1)

                def split_V(g, par, it):
                    n = g + layer * NG
                    act_e.wait_ge(V_in[par], (it + (layer * (NG // 2) + 1)) * 16)
                    at_least(act_e, dn_mm, (n - 1) * KT)
                    nc.scalar.copy(Vhi[:, par, :, :], Vraw[:, par, :, :]).then_inc(V_hi, 1)

                def gelus(g, j):
                    n = (g + layer * NG) * 2 + j
                    act_e.wait_ge(up_mm, n + 1)
                    at_least(act_e, H_ready, n - 1)
                    nc.scalar.activation(act[:, j, :], ps[:, j, :], ACT.Gelu_apprx_tanh).then_inc(act_ready, 1)

                def period(g, par, it, last=False):
                    if not last:
                        split_U(g + 1, 1 - par, it + par)
                    split_V(g, par, it)
                    gelus(g, 0)
                    gelus(g, 1)

                split_U(0, 0, 0)
                period(0, 0, 0)
                period(1, 1, 0)
                with act_e.Fori(1, NG // 2 - 1) as it:
                    for par in range(2):
                        period(it * 2 + par, par, it)
                period(NG - 2, 0, NG // 2 - 1)
                period(NG - 1, 1, NG // 2 - 1, last=True)

            act_e.wait_ge(h_added, n_mixer[0])
            norm(2)
            peer_route(0)
            peer_dense(0)
            act_e.wait_ge(dn_added, n_peer[0])
            norm(3)
            for c in range(2):
                for tt in range(TT):
                    act_e.wait_ge(v_mm, c * TT + tt + 1)
                    nc.scalar.activation(vsb[:, tt, c * CW:(c + 1) * CW], ps[:, (c * TT + tt) % 4, :],
                                         ACT.Gelu_apprx_tanh).then_inc(v_gelu, 1)
            act_e.wait_ge(var_ready, 1)
            nc.scalar.activation(rstd[:, 0, :], rstd[:, 0, :], ACT.Sqrt).then_inc(std_ready, 1)
            for f in range(KT):
                act_e.wait_ge(u_mm, f + 1)
                nc.scalar.activation(uT[:, f, :], ps[:, f % 4, :], ACT.Gelu_apprx_tanh,
                                     bias=bu[:, f:f + 1]).then_inc(u_gelu, 1)
            act_e.wait_ge(h_added, n_mixer[1])
            norm(4)
            peer_route(1)
            peer_dense(1)
            act_e.wait_ge(dn_added, n_peer[1])
            norm(5)

        @block.tensor
        def _(pe):
            def modulation(layer, c):
                n = W_MOD[layer] + c
                pe.wait_ge(w_in[n % RING], 16 * (n // RING + 1))
                if layer == 1 and c == 0:
                    pe.wait_ge(mod_ready, 1)
                for j in range(4):
                    col = (4 * c + j) * 2
                    for k in range(KT):
                        mm = nc.tensor.matmul(ps[:, 7, col:col + 2], slots[n][:, k, j * P:(j + 1) * P],
                                              condS[:, k, :], start=(k == 0), stop=(k == KT - 1))
                mm.then_inc(mod_mm, 1)

            pe.sem_inc(G_mm, 4)
            pe.sem_inc(score_done, 1)
            pe.wait_ge(cond_ready, 1)
            for c in range(NMOD):
                modulation(0, c)
            pe.wait_ge(x_in, 16 * 15)

            def norm(n):
                width = NORMS[n][1]
                for k in range(KT):
                    pe.wait_ge(sq_ready, n * KT + k + 1)
                    nc.tensor.matmul(ps[:, 0, 0:width], ones[:, :], sq[:, k % 2, 0:width],
                                     start=(k == 0), stop=(k == KT - 1)).then_inc(sq_used, 1)

            norm(0)
            pe.wait_ge(rinv_ready, 1)
            norm(1)

            pe.wait_ge(rinv_ready, 2)
            pe.wait_ge(x_ready, 2 * KT)
            def rotate(rope):
                pe.wait_ge(rope_raw, rope + 1)
                at_least(pe, rope_out, rope - 1)
                nc.tensor.matmul(ps[:, 4 + rope % 2, :], rot[:, :], ropein[:, rope % 2, :],
                                 start=True, stop=True).then_inc(rope_mm, 1)

            for j, (kind, bank, _, rope, c, operands) in enumerate(in_jobs):
                n = W_IN + c
                pe.wait_ge(w_in[n % RING], 16 * (n // RING + 1))
                if j >= 4:
                    before = in_jobs[j - 4]
                    if before[0] == "rope":
                        pe.wait_ge(rope_raw, before[3] + 1)
                    else:
                        pe.wait_ge(proj_out, j - 3 - before[3])
                for k in range(KT):
                    w, x = operands(k)
                    mm = nc.tensor.matmul(bank, w, x, start=(k == 0), stop=(k == KT - 1))
                mm.then_inc(proj_mm, 1)
                if j >= 1 and in_jobs[j - 1][0] == "rope":
                    rotate(in_jobs[j - 1][3])

            pe.wait_ge(proj_out, sum(job[0] == "copy" for job in in_jobs))
            pe.wait_ge(rope_out, 2 * HA)

            def scores(u):
                kind, h, qt = units[u]
                for m in range(2 if kind == "diff" else 1):
                    j = job_of[u] + m
                    at_least(pe, exp_done, j - 1)
                    if kind == "diff":
                        q, kx, f, lo = qaT, kaT, h, DH * m
                    else:
                        q, kx, f, lo = qbT, kbT, h // 2, DH * (h % 2)
                    for c0, c1 in ((0, T), (T, TK)):
                        mm = nc.tensor.matmul(wide(j % 2)[:, c0:c1], q[lo:lo + DH, f, qt * P:(qt + 1) * P],
                                              kx[lo:lo + DH, f, c0:c1], start=True, stop=True)
                    mm.then_inc(score_mm, 1)

            def av(u):
                kind, h, qt = units[u]
                pe.wait_ge(probsT_ready, u + 1)
                at_least(pe, o_out, u)
                for kt in range(KK):
                    if kind == "diff":
                        dst, v = ps[:, 6, qt * P:(qt + 1) * P], va[:, kt, h * P:(h + 1) * P]
                    else:
                        lo = DH * (h % 2)
                        dst, v = ps[lo:lo + DH, 6, qt * P:(qt + 1) * P], vb[:, kt, h * DH:(h + 1) * DH]
                    mm = nc.tensor.matmul(dst, v, ATbuf[:, u % 2, kt * P:(kt + 1) * P],
                                          start=(kt == 0), stop=(kt == KK - 1))
                mm.then_inc(av_mm, 1)
                if kind == "diff" and qt == TT - 1:
                    pe.wait_ge(osq_ready, h + 1)
                    nc.tensor.matmul(ps[:, 6, :], ones[:, :], osq[:, :], start=True, stop=True).then_inc(osum_mm, 1)
                    pe.wait_ge(o_normed, h + 1)

            scores(0)
            mods_done = 0
            for u in range(len(units)):
                if u + 1 < len(units):
                    scores(u + 1)
                if u % 4 == 2 and mods_done < NMOD:
                    modulation(1, mods_done)
                    mods_done += 1
                pe.wait_ge(probs_ready, u + 1)
                at_least(pe, probsT_ready, u)
                for kt in range(KK):
                    mm = nc.tensor.transpose(wide(2)[:, kt * P:(kt + 1) * P], Abuf[:, u % 2, kt * P:(kt + 1) * P],
                                             ident[:, :])
                mm.then_inc(probsT_mm, 1)
                if u >= 1:
                    av(u - 1)
            av(len(units) - 1)
            while mods_done < NMOD:
                modulation(1, mods_done)
                mods_done += 1
            pe.wait_ge(o_out, len(units))

            def out_projection(w0, src, done):
                for f in range(KT):
                    n = w0 + f // 4
                    if f % 4 == 0:
                        pe.wait_ge(w_in[n % RING], 16 * (n // RING + 1))
                    at_least(pe, h_added, done + f - 3)
                    for k in range(KT):
                        mm = nc.tensor.matmul(ps[:, f % 4, :], slots[n][:, k, (f % 4) * P:(f % 4 + 1) * P],
                                              src[:, k, :], start=(k == 0), stop=(k == KT - 1))
                    mm.then_inc(h_mm, 1)

            def peer_route(layer):
                for n in range(HP):
                    w = W_Q[layer] + n // 4
                    if n % 4 == 0:
                        pe.wait_ge(w_in[w % RING], 16 * (w // RING + 1))
                    if n >= 4:
                        pe.wait_ge(q_out, layer * HP + n - 3)
                    for k in range(KT):
                        mm = nc.tensor.matmul(ps[:, n % 4, :], slots[w][:, k, (n % 4) * P:(n % 4 + 1) * P],
                                              xm[:, k, :], start=(k == 0), stop=(k == KT - 1))
                    mm.then_inc(q_mm, 1)
                pe.wait_ge(keys_in, 16 * (layer + 1))
                with pe.Fori(0, TT) as r:
                    tile = r + layer * TT
                    pe.wait_ge(qs_ready, tile + 1)
                    pe.wait_ge(pickT_out, tile + 1)
                    for n in range(HP):
                        mm = nc.tensor.matmul(ps[:, 4 + n // 4, (n % 4) * P:(n % 4 + 1) * P], qs[:, n, :],
                                              keysT[:, n, :], start=True, stop=True)
                    mm.then_inc(score_done, 1)
                    pe.wait_ge(pick_ready, tile + 2)
                    for n in range(3):
                        mm = nc.tensor.transpose(ps[:, 4, n * P:(n + 1) * P],
                                                 pick[:, n, :, :].rearrange("p h k -> p (h k)"), ident[:, :])
                    mm.then_inc(pickT_mm, 1)
                    with pe.Fori(0, NB // 2) as it:
                        for par in range(2):
                            n = tile * NB + it * 2 + par
                            pe.wait_ge(hot_ready, n + 1)
                            for t in range(TOK):
                                if t % 4 == 0:
                                    pe.wait_ge(G_out, n * 2 + (t // 4 + 1))
                                mm = nc.tensor.matmul(ps[:, 2 * par + t // 4, (t % 4) * P:(t % 4 + 1) * P],
                                                      Bhot[:, par, t, :], Ahot[:, par, t, :], start=True, stop=True)
                                if t % 4 == 3:
                                    mm.then_inc(G_mm, 1)

            def peer_dense(layer):
                pe.wait_ge(x_split, (layer + 1) * KT)
                pe.wait_ge(G_out, (layer + 1) * TT * (P // 4) + 4)

                def up(g, par):
                    n = g + layer * NG
                    pe.wait_ge(U_split, n + 1)
                    for j in range(2):
                        at_least(pe, act_ready, n * 2 + (j - 1))
                        for k in range(KT):
                            cols = slice(j * P, (j + 1) * P)
                            for i, (w, x) in enumerate(((Uhi, xhi), (Uhi, xlo), (Ulo, xhi))):
                                mm = nc.tensor.matmul(ps[:, j, :], w[:, par, k, cols], x[:, k, :],
                                                      start=(k == 0 and i == 0), stop=(k == KT - 1 and i == 2))
                        mm.then_inc(up_mm, 1)

                def down(g, par):
                    n = g + layer * NG
                    pe.wait_ge(V_split, n + 1)
                    pe.wait_ge(H_ready, n * 2 + 2)
                    for d in range(KT):
                        at_least(pe, dn_added, n * KT + (d - 3))
                        cols = slice(d * P, (d + 1) * P)
                        for j in range(2):
                            for i, (w, x) in enumerate(((Vhi, Hhi), (Vhi, Hlo), (Vlo, Hhi))):
                                mm = nc.tensor.matmul(ps[:, 2 + d % 4, :], w[:, par, j, cols], x[:, par, j, :],
                                                      start=(j == 0 and i == 0), stop=(j == 1 and i == 2))
                        mm.then_inc(dn_mm, 1)

                up(0, 0)
                up(1, 1)
                down(0, 0)
                with pe.Fori(1, NG // 2) as it:
                    for par in range(2):
                        up(it * 2 + par, par)
                        down(it * 2 + (par - 1), 1 - par)
                down(NG - 1, 1)

            out_projection(W_OUT, oT, 0)
            norm(2)
            pe.wait_ge(rinv_ready, 3)
            pe.wait_ge(x_ready, 3 * KT)
            peer_route(0)
            peer_dense(0)
            norm(3)
            pe.wait_ge(rinv_ready, 4)
            pe.wait_ge(x_ready, 4 * KT)
            pe.wait_ge(gl_in, 16 * 5)
            for c in range(2):
                n = W_GIN + c
                pe.wait_ge(w_in[n % RING], 16 * (n // RING + 1))
                for tt in range(TT):
                    i = c * TT + tt
                    at_least(pe, v_gelu, i - 3)
                    for k in range(KT):
                        nc.tensor.matmul(ps[:, i % 4, :], xm[:, k, tt * P:(tt + 1) * P], slots[n][:, k, :],
                                         start=(k == 0), stop=False)
                    nc.tensor.matmul(ps[:, i % 4, :], ones_row[:, :], bvrow[:, c * CW:(c + 1) * CW],
                                     start=False, stop=True).then_inc(v_mm, 1)
            pe.wait_ge(v_gelu, 2 * TT)
            for f in range(KT):
                n = W_GIN + 2 + f // 4
                if f % 4 == 0:
                    pe.wait_ge(w_in[n % RING], 16 * (n // RING + 1))
                at_least(pe, u_gelu, f - 3)
                for k in range(KT):
                    mm = nc.tensor.matmul(ps[:, f % 4, :], slots[n][:, k, (f % 4) * P:(f % 4 + 1) * P],
                                          xm[:, k, :], start=(k == 0), stop=(k == KT - 1))
                mm.then_inc(u_mm, 1)
            pe.wait_ge(v_normed, TT)
            for g in range(KT):
                at_least(pe, y_ready, g - 1)
                for tt in range(TT):
                    mm = nc.tensor.matmul(ps[:, 4 + g % 2, tt * P:(tt + 1) * P], vsb[:, tt, g * P:(g + 1) * P],
                                          wsT[:, g, :], start=True, stop=True)
                mm.then_inc(sv_mm, 1)
            pe.wait_ge(y_ready, KT)
            out_projection(W_GOUT, yT, KT)
            norm(4)
            pe.wait_ge(rinv_ready, 5)
            pe.wait_ge(x_ready, 5 * KT)
            peer_route(1)
            peer_dense(1)
            norm(5)

        @block.vector
        def _(dve):
            step = Chain(dve, dve_step)
            dve.sem_inc(pick_ready, 1)
            dve.sem_inc(pickT_out, 1)

            def modulation(layer):
                dve.wait_ge(mod_mm, NMOD * (layer + 1))
                step(nc.vector.tensor_tensor(mods[:, layer, :, :], ps[:, 7, 0:12 * KT].rearrange("p (n w) -> p n w", w=2),
                                             bmod[:, layer, :].unsqueeze(2).to_broadcast([P, 6 * KT, 2]), ALU.add))
                nc.vector.tensor_scalar(mods[:, layer, sc1:sc1 + KT, :], mods[:, layer, sc1:sc1 + KT, :], 1.0, None,
                                        ALU.add)
                step(nc.vector.tensor_scalar(mods[:, layer, sc2:sc2 + KT, :], mods[:, layer, sc2:sc2 + KT, :], 1.0,
                                             None, ALU.add))
                dve.sem_inc(mod_ready, 1)

            def norm(n):
                src, width, dst, layer, sh, sc, who = NORMS[n]
                dve.wait_ge(sq_used, (n + 1) * KT)
                nc.vector.tensor_scalar(rms[:, 0:width], ps[:, 0, 0:width], EPS, None, ALU.add).then_inc(ms_ready, 1)
                dve.wait_ge(rms_ready, n + 1)
                nc.vector.reciprocal(rinv[:, 0:width], rms[:, 0:width]).then_inc(rinv_ready, 1)
                dve.wait_ge(rinv_ready, n + 1)
                for k in range(KT):
                    scale = fing[:, k:k + 1] if sc is None else mods[:, layer, sc + k, who:who + 1]
                    nc.vector.scalar_tensor_tensor(out=dst[:, k, :], in0=src[:, k, :], scalar=scale,
                                                   in1=rinv[:, 0:width], op0=ALU.mult, op1=ALU.mult
                                                   ).then_inc(x_scaled, 1)

            dve.wait_ge(x_in, 16 * 15)
            step(nc.vector.tensor_tensor(lamtmp[:, :, :], lamin[:, 0:4:2, :], lamin[:, 1:4:2, :], ALU.mult))
            step(nc.vector.tensor_reduce(lamv[:, 0:2], lamtmp[:, :, :], AX, ALU.add))
            nc.vector.tensor_scalar(subg8[:, :], sublg[:, :], 1.0 - LAM_INIT, None, ALU.mult).then_inc(lam_sum, 1)
            modulation(0)
            norm(0)
            norm(1)

            for kind, _, dst, rope, _, _ in in_jobs:
                if kind != "rope":
                    continue
                dve.wait_ge(rope_raw, rope + 1)
                at_least(dve, rope_out, rope)
                step(nc.vector.tensor_tensor(ropetmp[:, 0, :], ropein[:, rope % 2, :], cosT[:, :], ALU.mult))
                dve.wait_ge(rope_mm, rope + 1)
                step(nc.vector.tensor_tensor(ropetmp[:, 1, :], ps[:, 4 + rope % 2, :], sinT[:, :], ALU.mult))
                nc.vector.tensor_tensor(dst, ropetmp[:, 0, :], ropetmp[:, 1, :], ALU.add).then_inc(rope_out, 1)
            dve.wait_ge(rope_out, 2 * HA)
            dve.wait_ge(lam_exp, 1)
            step(nc.vector.tensor_tensor(lamv[:, 4:5], lamv[:, 3:4], lamv[:, 2:3], ALU.subtract))
            step(nc.vector.tensor_scalar(lamv[:, 5:6], lamv[:, 4:5], -LAM_INIT, None, ALU.add))

            def maxima(u):
                kind, h, qt = units[u]
                for m in range(2 if kind == "diff" else 1):
                    j = job_of[u] + m
                    if kind == "near" and qt == 0:
                        dve.wait_ge(bias_in[h % 2], 16 * (h // 2 + 1))
                        step(nc.vector.tensor_tensor(btab[:, h % 2, :, :], btab[:, h % 2, :, :],
                                                     mask[:, :].unsqueeze(1).to_broadcast([P, 16, GRID_W]), ALU.add))
                    dve.wait_ge(score_mm, j + 1)
                    if kind == "diff":
                        step(nc.vector.tensor_reduce(mx[:, j:j + 1], wide(j % 2)[:, 0:TK], AX, ALU.max))
                        nc.vector.tensor_scalar(nmx[:, j:j + 1], mx[:, j:j + 1], -QK_SCALE, None,
                                                ALU.mult).then_inc(nmax_ready, 1)
                        continue
                    dve.wait_ge(exp_done, j - 1)
                    row = NA_ROWS - 1 - 2 * qt
                    bias = nc.vector.scalar_tensor_tensor(
                        out=Sbuf[:, j % 2, 0:T], in0=wide(j % 2)[:, 0:T], scalar=QK_SCALE,
                        in1=btab[:, h % 2, row:row + NA_ROWS, :].rearrange("p r c -> p (r c)"),
                        op0=ALU.mult, op1=ALU.add)
                    if qt == TT - 1:
                        bias.then_inc(bias_used, 1)
                    step(nc.vector.tensor_scalar(Sbuf[:, j % 2, T:TK], wide(j % 2)[:, T:TK], QK_SCALE, None, ALU.mult))
                    step(nc.vector.tensor_reduce(mx[:, j:j + 1], Sbuf[:, j % 2, :], AX, ALU.max))
                    nc.vector.tensor_scalar(nmx[:, j:j + 1], mx[:, j:j + 1], -1.0, None,
                                            ALU.mult).then_inc(nmax_ready, 1)

            def probabilities(u):
                kind, h, qt = units[u]
                j = job_of[u]
                n = 2 if kind == "diff" else 1
                dve.wait_ge(exp_done, j + n)
                step(nc.vector.reciprocal(rz[:, j:j + n], zs[:, j:j + n]))
                at_least(dve, probsT_mm, u - 1)
                dst = Abuf[:, u % 2, :]
                if kind == "diff":
                    i = j // 2
                    step(nc.vector.tensor_tensor(nlr[:, i:i + 1], rz[:, j + 1:j + 2], lamv[:, 5:6], ALU.mult))
                    step(nc.vector.tensor_scalar(dst, Ebuf[:, (j + 1) % 4, :], nlr[:, i:i + 1], None, ALU.mult))
                    nc.vector.scalar_tensor_tensor(out=dst, in0=Ebuf[:, j % 4, :], scalar=rz[:, j:j + 1], in1=dst,
                                                   op0=ALU.mult, op1=ALU.add).then_inc(probs_ready, 1)
                else:
                    nc.vector.tensor_scalar(dst, Ebuf[:, j % 4, :], rz[:, j:j + 1], None,
                                            ALU.mult).then_inc(probs_ready, 1)

            def outputs(u):
                kind, h, qt = units[u]
                cols = slice(qt * P, (qt + 1) * P)
                dve.wait_ge(av_mm, u + 1)
                if kind == "near":
                    lo = DH * (h % 2)
                    nc.vector.tensor_copy(oT[lo:lo + DH, HA + h // 2, cols], ps[lo:lo + DH, 6, cols]
                                          ).then_inc(o_out, 1)
                    return
                nc.vector.tensor_copy(oT[:, h, cols], ps[:, 6, cols]).then_inc(o_out, 1)
                if qt < TT - 1:
                    return
                dve.wait_ge(o_out, u + 1)
                nc.vector.tensor_tensor(osq[:, :], oT[:, h, :], oT[:, h, :], ALU.mult).then_inc(osq_ready, 1)
                dve.wait_ge(osum_mm, h + 1)
                nc.vector.tensor_scalar(osq[:, :], ps[:, 6, :], float(D // P), EPS, ALU.mult, ALU.add
                                        ).then_inc(oms_ready, 1)
                dve.wait_ge(orms_ready, h + 1)
                step(nc.vector.reciprocal(orinv[:, :], osq[:, :]))
                nc.vector.scalar_tensor_tensor(out=oT[:, h, :], in0=oT[:, h, :], scalar=subg8[:, :],
                                               in1=orinv[:, :], op0=ALU.mult, op1=ALU.mult).then_inc(o_normed, 1)
                dve.wait_ge(o_normed, h + 1)

            maxima(0)
            for u in range(len(units)):
                if u + 1 < len(units):
                    maxima(u + 1)
                probabilities(u)
                if u >= 1:
                    outputs(u - 1)
            outputs(len(units) - 1)
            modulation(1)

            def add_projection(layer):
                for f in range(KT):
                    dve.wait_ge(h_mm, layer * KT + f + 1)
                    nc.vector.scalar_tensor_tensor(out=hT[:, f, :], in0=ps[:, f % 4, :],
                                                   scalar=mods[:, layer, g1 + f, 0:1], in1=hT[:, f, :],
                                                   op0=ALU.mult, op1=ALU.add).then_inc(h_added, 1)
                dve.wait_ge(h_added, (layer + 1) * KT)

            ROUTE_STEPS = 18

            def carry_wait():
                nc.vector.memset(carrier[:, :], 0.0)

            def peer_route(layer):
                with dve.Fori(0, TT) as r:
                    tile = r + layer * TT
                    link = Chain(dve, route_step, tile * ROUTE_STEPS)
                    dve.wait_ge(S_ready, tile * 4 + 4)
                    carry_wait()

                    def top16(rows, vals, ids, src, spare):
                        for i in rows:
                            last = nc.vector.max(vals(i)[:, 0:8], src(i))
                        link(last)
                        carry_wait()
                        for i in rows:
                            nc.vector.max_index(ids(i)[:, 0:8], vals(i)[:, 0:8], src(i))
                            last = nc.vector.match_replace(spare(i), vals(i)[:, 0:8], src(i), NEG)
                        link(last)
                        carry_wait()
                        for i in rows:
                            last = nc.vector.max(vals(i)[:, 8:16], spare(i))
                        link(last)
                        carry_wait()
                        for i in rows:
                            last = nc.vector.max_index(ids(i)[:, 8:16], vals(i)[:, 8:16], spare(i))
                        link(last)
                        carry_wait()

                    top16(range(HP), lambda i: topv[:, i // 2, i % 2, :], lambda i: topi[:, i // 2, i % 2, :],
                          lambda i: S[:, i, :], lambda i: S2[:, i, :])
                    shape = [P, PH, TOPK, TOPK]
                    link(nc.vector.tensor_tensor(cand4,
                                                 topv[:, :, 0, :].unsqueeze(3).to_broadcast(shape),
                                                 topv[:, :, 1, :].unsqueeze(2).to_broadcast(shape), ALU.add))
                    carry_wait()
                    top16(range(PH), lambda i: candv[:, i, :], lambda i: candi[:, i, :],
                          lambda i: cand[:, i, :], lambda i: cand2[:, i, :])
                    nc.vector.tensor_scalar(rank[:, 0, :, :], candi[:, :, :], 4, None, ALU.logical_shift_right)
                    link(nc.vector.tensor_scalar(rank[:, 1, :, :], candi[:, :, :], TOPK - 1, None, ALU.bitwise_and))
                    for half in range(2):
                        link(nc.vector.tensor_tensor(eq[:, :, :, :],
                                                     iota16[:, :].unsqueeze(1).unsqueeze(1).to_broadcast(shape),
                                                     rank[:, half, :, :].unsqueeze(3).to_broadcast(shape),
                                                     ALU.is_equal))
                        link(nc.vector.tensor_tensor(eq[:, :, :, :], eq[:, :, :, :],
                                                     topi[:, :, half, :].unsqueeze(2).to_broadcast(shape), ALU.mult))
                        link(nc.vector.tensor_reduce(pick[:, half, :, :], eq[:, :, :, :], AX, ALU.add))
                    nc.vector.tensor_tensor(pick[:, 2, :, :], candv[:, :, :],
                                            candv[:, :, 0:1].to_broadcast([P, PH, TOPK]), ALU.subtract
                                            ).then_inc(gate_logits, 1)
                    dve.wait_ge(gate_exp, tile + 1)
                    link(nc.vector.tensor_reduce(zsum[:, 0, :], pick[:, 2, :, :], AX, ALU.add))
                    link(nc.vector.reciprocal(zsum[:, 1, :], zsum[:, 0, :]))
                    nc.vector.tensor_tensor(pick[:, 2, :, :], pick[:, 2, :, :],
                                            zsum[:, 1, :].unsqueeze(2).to_broadcast([P, PH, TOPK]), ALU.mult
                                            ).then_inc(pick_ready, 1)
                    dve.wait_ge(pickT_mm, tile + 1)
                    nc.vector.tensor_copy(pickT[:, :, :].rearrange("p n t -> p (n t)"), ps[:, 4, 0:3 * P]
                                          ).then_inc(pickT_out, 1)
                    dve.wait_ge(pickT_out, tile + 2)
                    carry_wait()
                    with dve.Fori(0, NB // 2) as it:
                        for par in range(2):
                            n = tile * NB + it * 2 + par
                            dve.wait_ge(G_mm, n * 2 + 2)
                            for t in range(TOK):
                                col = bass.ds((it * 2 + par) * TOK + t, 1)
                                nc.vector.tensor_scalar(Bhot[:, par, t, :], iota[:, :], pickT[:, 1, col], None,
                                                        ALU.is_equal)
                                last = nc.vector.tensor_scalar(Ahot[:, par, t, :], iota[:, :], pickT[:, 0, col],
                                                               pickT[:, 2, col], ALU.is_equal, ALU.mult)
                            last.then_inc(hot_ready, 1)

            def peer_dense(layer):
                for k in range(KT):
                    dve.wait_ge(x_hi, layer * KT + k + 1)
                    nc.vector.tensor_tensor(xlo[:, k, :], xm[:, k, :], xhi[:, k, :].bitcast(F32),
                                            ALU.subtract).then_inc(x_split, 1)

                def rest_of_U(g, par):
                    dve.wait_ge(U_hi, g + layer * NG + 1)
                    nc.vector.tensor_tensor(Ulo[:, par, :, :], Uraw[:, par, :, :], Uhi[:, par, :, :].bitcast(F32),
                                            ALU.subtract).then_inc(U_split, 1)

                def rest_of_V(g, par):
                    dve.wait_ge(V_hi, g + layer * NG + 1)
                    nc.vector.tensor_tensor(Vlo[:, par, :, :], Vraw[:, par, :, :], Vhi[:, par, :, :].bitcast(F32),
                                            ALU.subtract).then_inc(V_split, 1)

                def gated(g, par, it, j):
                    n = (g + layer * NG) * 2 + j
                    dve.wait_ge(act_ready, n + 1)
                    dve.wait_ge(G_in[par], (it + (layer * (NG // 2) + 1)) * 16)
                    at_least(dve, dn_mm, (g + (layer * NG - 1)) * KT)
                    nc.vector.tensor_tensor(Hf[:, j, :], act[:, j, :], Gin[:, par, j, :], ALU.mult
                                            ).then_inc(H_step, 1)
                    dve.wait_ge(H_step, n * 2 + 1)
                    nc.vector.tensor_copy(Hhi[:, par, j, :], Hf[:, j, :]).then_inc(H_step, 1)
                    dve.wait_ge(H_step, n * 2 + 2)
                    nc.vector.tensor_tensor(Hlo[:, par, j, :], Hf[:, j, :], Hhi[:, par, j, :].bitcast(F32),
                                            ALU.subtract).then_inc(H_ready, 1)

                def add_group(g):
                    n = (g + layer * NG) * KT
                    for d in range(KT):
                        dve.wait_ge(dn_mm, n + (d + 1))
                        at_least(dve, dn_added, n + (d + 1 - KT))
                        nc.vector.scalar_tensor_tensor(out=hT[:, d, :], in0=ps[:, 2 + d % 4, :],
                                                       scalar=mods[:, layer, g2 + d, 0:1], in1=hT[:, d, :],
                                                       op0=ALU.mult, op1=ALU.add).then_inc(dn_added, 1)

                def period(g, par, it, first=False, last=False):
                    if not last:
                        rest_of_U(g + 1, 1 - par)
                    gated(g, par, it, 0)
                    rest_of_V(g, par)
                    gated(g, par, it, 1)
                    if not first:
                        add_group(g - 1)

                rest_of_U(0, 0)
                period(0, 0, 0, first=True)
                period(1, 1, 0)
                with dve.Fori(1, NG // 2 - 1) as it:
                    for par in range(2):
                        period(it * 2 + par, par, it)
                period(NG - 2, 0, NG // 2 - 1)
                period(NG - 1, 1, NG // 2 - 1, last=True)
                add_group(NG - 1)
                dve.wait_ge(dn_added, (layer + 1) * NG * KT)

            add_projection(0)
            norm(2)
            peer_route(0)
            peer_dense(0)
            norm(3)
            dve.wait_ge(gl_in, 16 * 5)
            dve.wait_ge(v_gelu, 2 * TT)
            for tt in range(TT):
                for c in range(2):
                    last = nc.vector.bn_stats(bnst[:, tt, c, :], vsb[:, tt, c * CW:(c + 1) * CW])
                step(last)
                last = nc.vector.bn_aggr(bnag[:, tt, :], bnst[:, tt, :, :])
            step(last)
            nc.vector.tensor_scalar(rstd[:, 0, :], bnag[:, :, 1], EPS, None, ALU.add).then_inc(var_ready, 1)
            dve.wait_ge(std_ready, 1)
            step(nc.vector.reciprocal(rstd[:, 1, :], rstd[:, 0, :]))
            for tt in range(TT):
                row = vsb[:, tt, :]
                step(nc.vector.tensor_scalar(row, row, bnag[:, tt, 0:1], rstd[:, 1, tt:tt + 1], ALU.subtract, ALU.mult))
                step(nc.vector.tensor_tensor(row, row, lng[:, :], ALU.mult))
                nc.vector.tensor_tensor(row, row, lnb[:, :], ALU.add).then_inc(v_normed, 1)
            dve.wait_ge(u_gelu, KT)
            for g in range(KT):
                dve.wait_ge(sv_mm, g + 1)
                at_least(dve, y_ready, g - 1)
                step(nc.vector.tensor_tensor(svb[:, g % 2, :].rearrange("p (n t) -> p n t", n=TT),
                                             ps[:, 4 + g % 2, :].rearrange("p (n t) -> p n t", n=TT),
                                             bsb[:, g, :].unsqueeze(1).to_broadcast([P, TT, P]), ALU.add))
                nc.vector.tensor_tensor(yT[:, g, :], svb[:, g % 2, :], uT[:, g, :], ALU.mult).then_inc(y_ready, 1)
            add_projection(1)
            norm(4)
            peer_route(1)
            peer_dense(1)
            norm(5)

    return nc


def constants():
    f = np.float32
    p = np.arange(P)
    d = p % DH
    axis, half, i = d // 32, d % 32 // 16, d % 16
    inv_freq = (1.0 / (f(10000.0) ** (np.arange(0, DH // 2, 2, dtype=f) / f(DH // 2)))).astype(f)
    t = np.arange(T)
    place = np.stack([t // GRID_W, t % GRID_W]).astype(f)
    angle = (place[axis] * inv_freq[i][:, None]).astype(f)
    rot = np.zeros((P, P), f)
    rot[p + 16 * (1 - 2 * half), p] = 2 * half - 1
    col = p % GRID_W
    first = np.clip(col - NA_COLS // 2, 0, GRID_W - NA_COLS)[:, None]
    key = np.arange(GRID_W)[None, :]
    mask = np.where((key >= first) & (key < first + NA_COLS), 0.0, MASKED).astype(f)
    return {
        "ones": np.full((P, P), 1.0 / D, f), "ident": np.eye(P, dtype=f),
        "iota": np.tile(np.arange(P, dtype=f), (P, 1)), "iota16": np.tile(np.arange(TOPK, dtype=f), (P, 1)),
        "cosT": np.cos(angle).astype(f), "sinT": np.sin(angle).astype(f), "rot": rot, "mask": mask,
        "ones_row": np.ones((1, P), f),
    }


def columns_of(v):
    v = v.reshape(v.shape[:-1] + (v.shape[-1] // P, P))
    return np.moveaxis(v, -1, 0)


def layout(i):
    p = np.arange(P)[:, None, None]
    s = np.arange(16)[None, :, None]
    k = np.arange(GRID_W)[None, None, :]
    dr = np.clip(s - p // GRID_W, 0, 2 * NA_ROWS - 2)
    dc = np.clip(k - p % GRID_W + NA_COLS - 1, 0, 2 * NA_COLS - 2)
    U = i["peer_u"].reshape(DEPTH, NG, 2 * P, KT, P)
    arrays = {
        "xT": i["x"][0].T, "ctxT": i["ctx"][0].T,
        "cond": columns_of(np.stack([i["c"][0], i["c_ctx"]])).transpose(0, 2, 1),
        "b_mod": columns_of(i["b_mod"]), "w_mod": i["w_mod"],
        "attn_in": i["attn_w_in"], "attn_out": i["attn_w_out"], "query": i["peer_w_query"],
        "gate_in": np.concatenate([i["chunk_w_in"][:, :, D:], i["chunk_w_in"][:, :, :D]], axis=2),
        "gate_out": i["chunk_w_out"],
        "lam": np.broadcast_to(np.stack([i["lambda_q1"][0], i["lambda_k1"][0], i["lambda_q2"][0],
                                         i["lambda_k2"][0]]), (P, 4, DH)),
        "subln_g": i["subln_g"][0][:, None], "btab": i["na_rpb"][0][:, dr, dc],
        "bu": columns_of(i["chunk_b_in"][0, :D]), "bv": i["chunk_b_in"][:, D:],
        "ln_g": i["chunk_ln_g"][0], "ln_b": i["chunk_ln_b"][0], "b_s": i["chunk_b_s"][0],
        "w_sT": i["chunk_w_s"][0].transpose(2, 0, 1),
        "keysT": i["peer_sub_keys"].reshape(DEPTH, HP, NKEY, P).transpose(0, 3, 1, 2),
        "UT": U.transpose(0, 1, 4, 3, 2), "V": i["peer_v"].reshape(DEPTH, NG, 2, P, D),
        "final_g": columns_of(i["final_norm_g"]),
    }
    arrays.update(constants())
    return arrays


def kernel(**inputs):
    import concourse.bacc as bacc
    from concourse.bass_utils import run_bass_kernel_spmd

    nc = bacc.Bacc("TRN2", target_bir_lowering=False, num_devices=1)
    arrays, aps = {}, {}
    for name, v in layout({k: np.asarray(v) for k, v in inputs.items()}).items():
        v = np.ascontiguousarray(v)
        arrays[f"in_{name}"] = v
        aps[name] = nc.dram_tensor(f"in_{name}", v.shape, mybir.dt.from_np(v.dtype), kind="ExternalInput").ap()
    out = nc.dram_tensor("out_T", (D, T), F32, kind="ExternalOutput").ap()
    backbone(nc, aps, out)
    r = run_bass_kernel_spmd(nc, [arrays], core_ids=[0])
    return np.ascontiguousarray(r.results[0]["out_T"].T)[None]
```

```python
import math
from contextlib import ExitStack

import numpy as np

import concourse.bass as bass
from concourse import mybir

F32 = mybir.dt.float32
F32R = mybir.dt.float32r
U32 = mybir.dt.uint32
ACT = mybir.ActivationFunctionType
ALU = mybir.AluOpType
AX = mybir.AxisListType.X

P = 128
D = 1024
KT = D // P
T = 512
TT = T // P
TC = 256
TK = T + TC
KK = TK // P
CW = 512
NMOD = 6 * D // CW
GRID_W = 64
NA_ROWS, NA_COLS = 8, 16
HA, HB, DH = 4, 8, 64
QK_SCALE = DH ** -0.5
LAM_INIT = 0.8 - 0.6 * math.exp(-0.3 * 0)
EPS = 1e-6
PH, NKEY, TOPK = 8, 128, 16
HP = 2 * PH
NE = NKEY * NKEY
NG = NKEY // 2
DEPTH = 2
NEG = -3.0e38
MASKED = -1.0e30
RING = 3
TOK = 8
NB = P // TOK
NHI = NKEY // TOPK
FULL, SHORT = 4, 4
NCAND = FULL * TOPK + (TOPK - FULL) * SHORT

BASE = 17408


def at_least(eng, sem, value):
    if isinstance(value, int) and value <= 0:
        return
    eng.wait_ge(sem, value)


class Chain:

    def __init__(self, eng, sem, start=0):
        self.eng, self.sem, self.n = eng, sem, start

    def __call__(self, ins):
        self.n = self.n + 1
        ins.then_inc(self.sem, 1)
        self.eng.wait_ge(self.sem, self.n)


def backbone(nc, a, out):
    with ExitStack() as ctx:
        def sb(name, kib, shape, dt=F32):
            return nc.alloc_sbuf_tensor_at(name, shape, dt, offset=BASE + int(kib * 1024))

        def sem(name):
            return ctx.enter_context(nc.semaphore(name))

        hT = sb("hT", 0, [P, KT, T])
        mods = sb("mods", 16, [P, DEPTH, 6 * KT, 2])
        ones = sb("ones", 16.75, [P, P])
        ident = sb("ident", 17.25, [P, P])
        iota = sb("iota", 17.75, [P, P])
        cond = sb("cond", 18.25, [P, KT, 2])
        condS = sb("condS", 18.375, [P, KT, 2])
        bmod = sb("bmod", 18.5, [P, DEPTH, 6 * KT])
        fing = sb("fing", 19, [P, KT])
        rinv = sb("rinv", 20, [P, T])
        rms = sb("rms", 204, [P, T])
        bu = sb("bu", 22, [P, KT])
        iota8 = sb("iota8", 22.75, [P, NHI])
        carrier = sb("carrier", 22.6875, [P, 1])
        iota16 = sb("iota16", 22.125, [P, TOPK])
        lamv = sb("lamv", 22.25, [P, 8])
        sublg = sb("sublg", 22.5, [P, 1])
        subg8 = sb("subg8", 22.53125, [P, 1])
        ones_row = sb("ones_row", 19.25, [1, P])
        lamtmp = sb("lamtmp", 104, [P, 2, DH])
        lamin = sb("lamin", 23, [P, 4, DH])
        xm = sb("xm", 24, [P, KT, T])
        sq = sb("sq", 128, [P, 2, T])
        ring = [sb(f"ring{n}", 134 + 16 * n, [P, KT, CW]) for n in range(RING + 1)]
        modw = [sb(f"modw{n}", at, [P, KT // 2, CW]) for n, at in enumerate((182, 190, 48))]
        macc = sb("macc", 128, [P, 2, CW])
        maccx = sb("maccx", 56, [P, 2, CW])
        xc = sb("xc", 40, [P, KT, TC])
        ctxT = sb("ctxT", 48, [P, KT, TC])
        qaT = sb("qaT", 56, [P, HA, T])
        kaT = sb("kaT", 64, [P, HA, TK])
        qbT = sb("qbT", 76, [P, HB // 2, T])
        kbT = sb("kbT", 84, [P, HB // 2, TK])
        va = sb("va", 96, [P, KK, CW])
        vb = sb("vb", 108, [P, KK, CW])
        cosT = sb("cosT", 120, [P, T])
        sinT = sb("sinT", 122, [P, T])
        ropein = sb("ropein", 124, [P, 2, T])
        rot = sb("rot", 132, [P, P])
        mask = sb("mask", 132.5, [P, GRID_W])
        ropetmp = sb("ropetmp", 198, [P, 2, T])
        oT = sb("oT", 24, [P, KT, T])
        btab = sb("btab", 40, [P, 2, 16, GRID_W])
        osq = sb("osq", 48, [P, T])
        orinv = sb("orinv", 50, [P, T])
        Ebuf = sb("Ebuf", 182, [P, 4, TK])
        ATbuf = sb("ATbuf", 120, [P, 2, TK])
        Abuf = sb("Abuf", 126, [P, 2, TK])
        Sbuf = sb("Sbuf", 194, [P, 2, TK])
        mx = sb("mx", 200, [P, 64])
        nmx = sb("nmx", 200.25, [P, 64])
        zs = sb("zs", 200.5, [P, 64])
        rz = sb("rz", 200.75, [P, 64])
        nlr = sb("nlr", 201, [P, 16])
        vsb = sb("vsb", 40, [P, TT, D])
        uT = sb("uT", 56, [P, KT, T])
        lng = sb("lng", 72, [P, D])
        lnb = sb("lnb", 76, [P, D])
        bsb = sb("bsb", 80, [P, KT, P])
        wsT = sb("wsT", 84, [P, KT, P])
        yT = sb("yT", 88, [P, KT, T])
        svb = sb("svb", 104, [P, 2, T])
        bvrow = sb("bvrow", 116, [1, D])
        bnst = sb("bnst", 120, [P, TT, 2, 6])
        bnag = sb("bnag", 120.25, [P, TT, 2])
        rstd = sb("rstd", 120.5, [P, 2, TT])
        qT = sb("qT", 40, [P, HP, T])
        keysT = sb("keysT", 72, [P, HP, NKEY])
        qs = sb("qs", 80, [P, HP, P])
        S = sb("S", 88, [P, HP, NKEY])
        S2 = sb("S2", 96, [P, HP, NKEY])
        eq = sb("eq", 104, [P, PH, TOPK, TOPK])
        cand = sb("cand", 104, [P, 2, PH, NCAND])
        hot_hi = sb("hot_hi", 104, [P, P // 2, NHI])
        hot_lo = sb("hot_lo", 106, [P, P // 2, TOPK])
        Ahot = sb("Ahot", 112, [P, 2, TOK, P])
        Bhot = sb("Bhot", 120, [P, 2, TOK, P])
        topv = sb("topv", 128, [P, PH, 2, TOPK])
        topi = sb("topi", 129, [P, PH, 2, TOPK], U32)
        candv = sb("candv", 130, [P, PH, TOPK])
        candi = sb("candi", 130.5, [P, PH, TOPK], U32)
        shifted = sb("shifted", 131, [P, 2, PH, TOPK], U32)
        rank = sb("rank", 132, [P, 2, PH, TOPK])
        zsum = sb("zsum", 133, [P, 2, PH])
        key1 = sb("key1", 133.125, [P, PH, TOPK])
        pick = sb("pick", 200, [P, 4, PH, TOPK])
        pickT = sb("pickT", 198, [P, 4, P])
        key1u = sb("key1u", 202, [P, 3, PH, TOPK], U32)
        G_st = sb("G_st", 134, [P, NKEY, P])
        xhi = sb("xhi", 40, [P, KT, T], F32R)
        xlo = sb("xlo", 56, [P, KT, T], F32R)
        Uraw = sb("Uraw", 72, [P, 2, KT, 2 * P])
        Vraw = sb("Vraw", 88, [P, 2, 2, D])
        Uhi = sb("Uhi", 104, [P, 2, KT, 2 * P], F32R)
        Ulo = sb("Ulo", 120, [P, 2, KT, 2 * P], F32R)
        Vhi = sb("Vhi", 136, [P, 2, 2, D], F32R)
        Vlo = sb("Vlo", 152, [P, 2, 2, D], F32R)
        Gin = sb("Gin", 168, [P, 2, 2, T])
        act = sb("act", 176, [P, 2, T])
        Hf = sb("Hf", 180, [P, 2, T])
        Hhi = sb("Hhi", 184, [P, 2, 2, T], F32R)
        Hlo = sb("Hlo", 192, [P, 2, 2, T], F32R)

        G_dram = nc.dram_tensor("G_scratch", (DEPTH, NG, P, 2, TT, P), F32, kind="Internal").ap()
        ps = ctx.enter_context(nc.psum_tensor("ps", [P, 8, T], F32))

        def wide(pair):
            return ps[:, 2 * pair:2 * pair + 2, :].rearrange("p b n -> p (b n)")

        NIN, NOUT, NQ, NGI = 6, 2, 4, 4
        chunks = ([("attn_in", 0, c) for c in range(NIN)] + [("attn_out", 0, c) for c in range(NOUT)]
                  + [("query", 0, c) for c in range(NQ)] + [("gate_in", 0, c) for c in range(NGI)]
                  + [("gate_out", 0, c) for c in range(NOUT)] + [("query", 1, c) for c in range(NQ)])
        W_IN = 0
        W_OUT = NIN
        W_Q0 = W_OUT + NOUT
        W_GIN = W_Q0 + NQ
        W_GOUT = W_GIN + NGI
        W_Q = [W_Q0, W_GOUT + NOUT]
        NFIRST = 2 * D // CW
        NCH = DEPTH * NMOD
        slot_of, landed_by, before = [], [], []
        taken = [[] for _ in range(RING + 1)]
        for n, (kind, layer, c) in enumerate(chunks):
            k = c if kind == "query" else n % RING
            before.append(taken[k][-1] if taken[k] else None)
            taken[k].append(n)
            slot_of.append(k)
            landed_by.append(16 * len(taken[k]))
        slots = [ring[k] for k in slot_of]

        in_jobs = []

        def in_job(kind, c, width, dst, operands):
            rope = sum(job[0] == "rope" for job in in_jobs)
            in_jobs.append((kind, ps[:, len(in_jobs) % 4, 0:width], dst, rope, c, operands))

        def columns(c, f, x):
            slot = slots[W_IN + c]
            return lambda k: (slot[:, k, f * P:(f + 1) * P], x[:, k, :])

        def tokens(c, x, tt):
            slot = slots[W_IN + c]
            return lambda k: (x[:, k, tt * P:(tt + 1) * P], slot[:, k, :])

        for c, (name, dst) in enumerate((("rope", qaT), ("rope", kaT), ("v", va), ("copy", qbT), ("copy", kbT),
                                         ("v", vb))):
            if name == "v":
                for tt in range(TT):
                    in_job("copy", c, CW, dst[:, tt, :], tokens(c, xm, tt))
                for tt in range(TC // P):
                    in_job("copy", c, CW, dst[:, TT + tt, :], tokens(c, xc, tt))
                continue
            for f in range(4):
                in_job(name, c, T, dst[:, f, 0:T], columns(c, f, xm))
            if c in (1, 4):
                for f in range(4):
                    in_job("copy", c, TC, dst[:, f, T:TK], columns(c, f, xc))

        consts_in = sem("consts_in")
        x_in = sem("x_in")
        w_in = [sem(f"w_in{n}") for n in range(RING + 1)]
        mod_mm = sem("mod_mm")
        mod_in = [sem(f"mod_in{n}") for n in range(3)]
        mod_read = sem("mod_read")
        macc_ready = sem("macc_ready")
        cond_ready = sem("cond_ready")
        mod_ready = sem("mod_ready")
        dve_step = sem("dve_step")
        lam_sum = sem("lam_sum")
        lam_exp = sem("lam_exp")
        lam_ready = sem("lam_ready")
        sq_ready = sem("sq_ready")
        sq_used = sem("sq_used")
        ms_ready = sem("ms_ready")
        rms_ready = sem("rms_ready")
        oms_ready = sem("oms_ready")
        orms_ready = sem("orms_ready")
        var_ready = sem("var_ready")
        std_ready = sem("std_ready")
        rinv_ready = sem("rinv_ready")
        x_scaled = sem("x_scaled")
        x_ready = sem("x_ready")
        proj_mm = sem("proj_mm")
        proj_out = sem("proj_out")
        rope_raw = sem("rope_raw")
        rope_mm = sem("rope_mm")
        rope_out = sem("rope_out")
        bias_in = [sem(f"bias_in{n}") for n in range(2)]
        score_mm = sem("score_mm")
        nmax_ready = sem("nmax_ready")
        exp_done = sem("exp_done")
        probs_ready = sem("probs_ready")
        probsT_mm = sem("probsT_mm")
        probsT_ready = sem("probsT_ready")
        av_mm = sem("av_mm")
        o_out = sem("o_out")
        osq_ready = sem("osq_ready")
        osum_mm = sem("osum_mm")
        o_normed = sem("o_normed")
        h_mm = sem("h_mm")
        h_added = sem("h_added")
        q_mm = sem("q_mm")
        q_out = sem("q_out")
        keys_in = sem("keys_in")
        qs_ready = sem("qs_ready")
        score_done = sem("score_done")
        S_ready = sem("S_ready")
        gate_logits = sem("gate_logits")
        gate_exp = sem("gate_exp")
        pick_ready = sem("pick_ready")
        pickT_out = sem("pickT_out")
        route_step = sem("route_step")
        S_free = sem("S_free")
        bias_used = sem("bias_used")
        near_read = sem("near_read")
        H_step = sem("H_step")
        pickT_mm = sem("pickT_mm")
        hot_step = sem("hot_step")
        hot_ready = sem("hot_ready")
        G_mm = sem("G_mm")
        G_out = sem("G_out")
        G_stored = sem("G_stored")
        x_hi = sem("x_hi")
        x_split = sem("x_split")
        U_in = [sem(f"U_in{n}") for n in range(2)]
        V_in = [sem(f"V_in{n}") for n in range(2)]
        G_in = [sem(f"G_in{n}") for n in range(2)]
        U_hi = sem("U_hi")
        U_split = sem("U_split")
        V_hi = sem("V_hi")
        V_split = sem("V_split")
        up_mm = sem("up_mm")
        act_ready = sem("act_ready")
        H_ready = sem("H_ready")
        dn_mm = sem("dn_mm")
        dn_added = sem("dn_added")
        gl_in = sem("gl_in")
        v_mm = sem("v_mm")
        v_gelu = sem("v_gelu")
        v_normed = sem("v_normed")
        u_mm = sem("u_mm")
        u_gelu = sem("u_gelu")
        sv_mm = sem("sv_mm")
        y_ready = sem("y_ready")
        stored = sem("stored")

        NH1 = 2 * NFIRST
        mslot = [m % 2 if m < NH1 else m % 3 for m in range(2 * NCH)]
        mbefore = [max([w for w in range(m) if mslot[w] == mslot[m]], default=None) for m in range(2 * NCH)]
        mlanded = [16 * (1 + sum(mslot[w] == mslot[m] for w in range(m))) for m in range(2 * NCH)]
        MOD_AT = [1 + i * (len(in_jobs) - 5) // (NCH - NFIRST) for i in range(NCH - NFIRST)]

        units = []
        for h in range(HA):
            for qt in range(TT):
                units.append(("diff", h, qt))
        for h in range(HB):
            for qt in range(TT):
                units.append(("near", h, qt))
        job_of = []
        njobs = 0
        for kind, h, qt in units:
            job_of.append(njobs)
            njobs += 2 if kind == "diff" else 1
        HEAD_END = HA * TT
        sh1, sc1, g1, sh2, sc2, g2 = [KT * n for n in range(6)]
        NORMS = [(ctxT, TC, xc, 0, sh1, sc1, 1), (hT, T, xm, 0, sh1, sc1, 0), (hT, T, xm, 0, sh2, sc2, 0),
                 (hT, T, xm, 1, sh1, sc1, 0), (hT, T, xm, 1, sh2, sc2, 0), (hT, T, xm, None, None, None, 0)]
        n_mixer = [KT, 2 * KT]
        n_peer = [KT * NG, 2 * KT * NG]

        def chunk_used(n):
            kind, layer, c = chunks[n]
            if kind == "attn_in":
                return proj_mm, sum(job[4] <= c for job in in_jobs)
            if kind == "attn_out":
                return h_mm, 4 * (c + 1)
            if kind == "gate_out":
                return h_mm, KT + 4 * (c + 1)
            if kind == "query":
                return q_mm, (layer * TT + TT - 1) * HP + 4 * (c + 1)
            return (v_mm, TT * (c + 1)) if c < 2 else (u_mm, 4 * (c - 1))

        block = ctx.enter_context(nc.Block())

        @block.sync
        def _(sp):
            sp.sem_inc(G_stored, 32)
            sp.dma_start(cond[:, :, :], a["cond"]).then_inc(consts_in, 16)
            sp.dma_start(bmod[:, :, :], a["b_mod"]).then_inc(consts_in, 16)

            def load_chunk(n):
                if before[n] is not None:
                    sp.wait_ge(*chunk_used(before[n]))
                kind, layer, c = chunks[n]
                sp.dma_start(slots[n][:, :, :],
                             a[kind][layer].rearrange("(k p) n -> p k n", p=P)[:, :, c * CW:(c + 1) * CW]
                             ).then_inc(w_in[slot_of[n]], 16)

            sp.dma_start(hT[:, :, :], a["xT"].rearrange("(k p) t -> p k t", p=P)).then_inc(x_in, 16)
            sp.dma_start(ctxT[:, :, :], a["ctxT"].rearrange("(k p) t -> p k t", p=P)).then_inc(x_in, 16)
            for dst, name in ((ones, "ones"), (ident, "ident"), (iota, "iota"), (iota16, "iota16"), (iota8, "iota8"),
                              (fing, "final_g"), (bu, "bu"), (cosT, "cosT"), (sinT, "sinT"), (rot, "rot"),
                              (mask, "mask"), (sublg, "subln_g"), (lamin, "lam"), (ones_row, "ones_row")):
                sp.dma_start(dst[tuple(slice(None) for _ in dst.shape)], a[name]).then_inc(x_in, 16)
            def load_mod_half(m):
                if mbefore[m] is not None:
                    sp.wait_ge(mod_read, mbefore[m] + 1)
                if m >= NH1 and mslot[m] == 2 and mbefore[m] is None:
                    sp.wait_ge(x_scaled, KT)
                layer, c, half = m // (2 * NMOD), m // 2 % NMOD, m % 2
                sp.dma_start(modw[mslot[m]][:, :, :],
                             a["w_mod"][layer].rearrange("(k p) n -> p k n", p=P)[
                                 :, half * KT // 2:(half + 1) * KT // 2, c * CW:(c + 1) * CW]
                             ).then_inc(mod_in[mslot[m]], 16)

            for m in range(NH1):
                load_mod_half(m)
            events = [(-1 if before[n] is None else chunk_used(before[n])[1], "chunk", n) for n in range(NIN)]
            events += [(0 if mbefore[m] < NH1 else MOD_AT[mbefore[m] // 2 - NFIRST] + 1, "half", m)
                       for m in range(NH1, 2 * NCH) if mbefore[m] is not None]
            events += [(0, "half", m) for m in range(NH1, 2 * NCH) if mbefore[m] is None]
            for _, what, n in sorted(events):
                (load_chunk if what == "chunk" else load_mod_half)(n)
            for n in range(W_OUT, W_OUT + NOUT):
                load_chunk(n)
            for h in range(HB):
                if h < 2:
                    sp.wait_ge(proj_mm, len(in_jobs))
                else:
                    sp.wait_ge(bias_used, h - 1)
                sp.dma_start(btab[:, h % 2, :, :], a["btab"][h]).then_inc(bias_in[h % 2], 16)
            for n in range(W_Q0, W_GIN):
                if slot_of[n] == RING:
                    sp.wait_ge(h_mm, 1)
                load_chunk(n)

            def peer_loads(layer):
                sp.wait_ge(h_added, n_mixer[layer])
                sp.dma_start(keysT[:, :, :], a["keysT"][layer]).then_inc(keys_in, 16)
                with sp.Fori(0, TT) as r:
                    sp.wait_ge(G_out, (r + (layer * TT + 1)) * (P // 4) + 4)
                    for j in range(2):
                        sp.dma_start(G_dram[layer, :, :, j, bass.ds(r, 1), :].rearrange("g p r t -> p g (r t)"),
                                     G_st[:, :, :].rearrange("p (g j) t -> p g j t", j=2)[:, :, j, :]
                                     ).then_inc(G_stored, 16)
                sp.wait_ge(G_stored, 32 * (TT * (layer + 1) + 1))

                def load_group(g, par):
                    n = g + layer * NG
                    at_least(sp, U_split, n - 1)
                    sp.dma_start(Uraw[:, par, :, :], a["UT"][layer][bass.ds(g, 1)].rearrange("o p k e -> p (o k) e")
                                 ).then_inc(U_in[par], 16)
                    at_least(sp, V_split, n - 1)
                    sp.dma_start(Vraw[:, par, :, :], a["V"][layer][bass.ds(g, 1)].rearrange("o j p d -> p (o j) d")
                                 ).then_inc(V_in[par], 16)
                    at_least(sp, H_ready, (n - 1) * 2)
                    sp.dma_start(Gin[:, par, :, :], G_dram[layer][bass.ds(g, 1)].rearrange("o p j r t -> p (o j) (r t)")
                                 ).then_inc(G_in[par], 16)

                for g in range(2):
                    load_group(g, g)
                with sp.Fori(1, NG // 2) as it:
                    for par in range(2):
                        load_group(it * 2 + par, par)

            peer_loads(0)
            sp.wait_ge(h_added, n_mixer[0])
            sp.wait_ge(dn_added, n_peer[0])
            for n in range(W_GIN, W_GIN + RING):
                load_chunk(n)
            for dst, name in ((lng, "ln_g"), (lnb, "ln_b"), (bsb, "b_s")):
                sp.dma_start(dst[tuple(slice(None) for _ in dst.shape)],
                             a[name].partition_broadcast(P)).then_inc(gl_in, 16)
            sp.dma_start(wsT[:, :, :], a["w_sT"]).then_inc(gl_in, 16)
            sp.dma_start(bvrow[:, :], a["bv"]).then_inc(gl_in, 16)
            for n in range(W_GIN + RING, len(chunks)):
                load_chunk(n)
            peer_loads(1)
            for k in range(KT):
                sp.wait_ge(x_scaled, 5 * KT + k + 1)
                sp.dma_start(out[k * P:(k + 1) * P, :], xm[:, k, :]).then_inc(stored, 16)
            sp.wait_ge(stored, 16 * KT)

        @block.scalar
        def _(act_e):
            act_e.sem_inc(G_out, 4)
            act_e.wait_ge(consts_in, 32)
            nc.scalar.activation(condS[:, :, :], cond[:, :, :], ACT.Silu).then_inc(cond_ready, 1)
            act_e.wait_ge(x_in, 16 * 16)

            def norm(n):
                src, width, dst, layer, sh, sc, who = NORMS[n]
                for k in range(KT):
                    at_least(act_e, sq_used, n * KT + k - 1)
                    nc.scalar.activation(sq[:, k % 2, 0:width], src[:, k, :], ACT.Square).then_inc(sq_ready, 1)
                act_e.wait_ge(ms_ready, n + 1)
                nc.scalar.activation(rms[:, 0:width], rms[:, 0:width], ACT.Sqrt).then_inc(rms_ready, 1)
                if sh is None:
                    return
                for k in range(KT):
                    act_e.wait_ge(x_scaled, n * KT + k + 1)
                    nc.scalar.activation(dst[:, k, :], dst[:, k, :], ACT.Identity,
                                         bias=mods[:, layer, sh + k, who:who + 1]).then_inc(x_ready, 1)

            act_e.wait_ge(mod_ready, 1)
            norm(0)
            norm(1)

            for j, (kind, bank, dst, rope, _, _) in enumerate(in_jobs):
                act_e.wait_ge(proj_mm, j + 1)
                if kind == "copy":
                    nc.scalar.copy(dst, bank).then_inc(proj_out, 1)
                else:
                    at_least(act_e, rope_out, rope - 1)
                    nc.scalar.copy(ropein[:, rope % 2, :], bank).then_inc(rope_raw, 1)
            act_e.wait_ge(lam_sum, 1)
            nc.scalar.activation(lamv[:, 2:4], lamv[:, 0:2], ACT.Exp).then_inc(lam_exp, 1)

            def evac_probsT(u):
                act_e.wait_ge(probsT_mm, u + 1)
                at_least(act_e, av_mm, u - 1)
                nc.scalar.copy(ATbuf[:, u % 2, :], wide(2)[:, 0:TK]).then_inc(probsT_ready, 1)

            def finish(u):
                evac_probsT(u)
                kind, h, qt = units[u]
                if kind == "diff" and qt == TT - 1:
                    act_e.wait_ge(oms_ready, h + 1)
                    nc.scalar.activation(osq[:, :], osq[:, :], ACT.Sqrt).then_inc(orms_ready, 1)

            for u, (kind, h, qt) in enumerate(units):
                j = job_of[u]
                for m in range(2 if kind == "diff" else 1):
                    act_e.wait_ge(nmax_ready, j + m + 1)
                    first_over = [w for w in range(u) if job_of[w] <= j + m - 4]
                    if first_over:
                        act_e.wait_ge(probs_ready, first_over[-1] + 1)
                    src = wide((j + m) % 2)[:, 0:TK] if kind == "diff" else Sbuf[:, (j + m) % 2, :]
                    nc.scalar.activation(Ebuf[:, (j + m) % 4, :], src, ACT.Exp, bias=nmx[:, j + m:j + m + 1],
                                         scale=QK_SCALE if kind == "diff" else 1.0,
                                         accum_out=zs[:, j + m:j + m + 1]).then_inc(exp_done, 1)
                if u >= 2:
                    finish(u - 2)
            finish(len(units) - 2)
            finish(len(units) - 1)

            def peer_route(layer):
                def queries(r, n0, n1):
                    for n in range(n0, n1):
                        act_e.wait_ge(q_mm, (layer * TT + r) * HP + n + 1)
                        nc.scalar.copy(qT[:, n, r * P:(r + 1) * P], ps[:, n % 4, 0:P]).then_inc(q_out, 1)

                def stage_queries(r):
                    at_least(act_e, score_done, r + layer * TT)
                    nc.scalar.copy(qs[:, :, :], qT[:, :, bass.ds(r * P, P)]).then_inc(qs_ready, 1)

                def read_scores(r):
                    tile = r + layer * TT
                    act_e.wait_ge(score_done, tile + 1)
                    at_least(act_e, S_free, tile)
                    for b in range(4):
                        nc.scalar.copy(S[:, 4 * b:4 * b + 4, :].rearrange("p a n -> p (a n)"), ps[:, 4 + b, :]
                                       ).then_inc(S_ready, 1)

                def gate_exps(r):
                    act_e.wait_ge(gate_logits, r + layer * TT + 1)
                    nc.scalar.activation(pick[:, 3, :, :], pick[:, 3, :, :], ACT.Exp).then_inc(gate_exp, 1)

                def gate_weights(r):
                    tile = r + layer * TT
                    act_e.wait_ge(G_stored, (tile + 1) * 32)
                    with act_e.Fori(0, NB // 2) as it:
                        for par in range(2):
                            for b in range(2):
                                act_e.wait_ge(G_mm, (tile * NB + it * 2 + par) * 2 + b + 5)
                                nc.scalar.copy(
                                    G_st[:, :, bass.ds((it * 2 + par) * TOK + 4 * b, 4)].rearrange("p i t -> p t i"),
                                    ps[:, 2 * par + b, :].rearrange("p (t i) -> p t i", t=4)).then_inc(G_out, 1)

                queries(0, 0, HP)
                act_e.wait_ge(q_out, (layer * TT + 1) * HP)
                stage_queries(0)
                read_scores(0)
                queries(1, 0, HP)
                act_e.wait_ge(q_out, (layer * TT + 2) * HP)
                stage_queries(1)
                read_scores(1)
                queries(2, 0, HP // 2)
                gate_exps(0)
                queries(2, HP // 2, HP)
                queries(3, 0, HP)
                act_e.wait_ge(q_out, (layer * TT + 4) * HP)
                with act_e.Fori(1, TT - 1) as r:
                    stage_queries(r + 1)
                    read_scores(r + 1)
                    gate_exps(r)
                    gate_weights(r - 1)
                gate_exps(TT - 1)
                gate_weights(TT - 2)
                gate_weights(TT - 1)

            def peer_dense(layer):
                act_e.wait_ge(G_stored, 32 * ((layer + 1) * TT + 1))
                for k in range(KT):
                    nc.scalar.copy(xhi[:, k, :], xm[:, k, :]).then_inc(x_hi, 1)

                def split_U(g, par, it):
                    n = g + layer * NG
                    act_e.wait_ge(U_in[par], (it + (layer * (NG // 2) + 1)) * 16)
                    at_least(act_e, up_mm, (n - 1) * 2)
                    nc.scalar.copy(Uhi[:, par, :, :], Uraw[:, par, :, :]).then_inc(U_hi, 1)

                def split_V(g, par, it):
                    n = g + layer * NG
                    act_e.wait_ge(V_in[par], (it + (layer * (NG // 2) + 1)) * 16)
                    at_least(act_e, dn_mm, (n - 1) * KT)
                    nc.scalar.copy(Vhi[:, par, :, :], Vraw[:, par, :, :]).then_inc(V_hi, 1)

                def gelus(g, j):
                    n = (g + layer * NG) * 2 + j
                    act_e.wait_ge(up_mm, n + 1)
                    at_least(act_e, H_ready, n - 1)
                    nc.scalar.activation(act[:, j, :], ps[:, j, :], ACT.Gelu_apprx_tanh).then_inc(act_ready, 1)

                def period(g, par, it, last=False):
                    if not last:
                        split_U(g + 1, 1 - par, it + par)
                    split_V(g, par, it)
                    gelus(g, 0)
                    gelus(g, 1)

                split_U(0, 0, 0)
                period(0, 0, 0)
                period(1, 1, 0)
                with act_e.Fori(1, NG // 2 - 1) as it:
                    for par in range(2):
                        period(it * 2 + par, par, it)
                period(NG - 2, 0, NG // 2 - 1)
                period(NG - 1, 1, NG // 2 - 1, last=True)

            act_e.wait_ge(h_added, n_mixer[0])
            norm(2)
            peer_route(0)
            peer_dense(0)
            act_e.wait_ge(dn_added, n_peer[0])
            norm(3)
            for c in range(2):
                for tt in range(TT):
                    act_e.wait_ge(v_mm, c * TT + tt + 1)
                    nc.scalar.activation(vsb[:, tt, c * CW:(c + 1) * CW], ps[:, (c * TT + tt) % 4, :],
                                         ACT.Gelu_apprx_tanh).then_inc(v_gelu, 1)
            act_e.wait_ge(var_ready, 1)
            nc.scalar.activation(rstd[:, 0, :], rstd[:, 0, :], ACT.Sqrt).then_inc(std_ready, 1)
            for f in range(KT):
                act_e.wait_ge(u_mm, f + 1)
                nc.scalar.activation(uT[:, f, :], ps[:, f % 4, :], ACT.Gelu_apprx_tanh,
                                     bias=bu[:, f:f + 1]).then_inc(u_gelu, 1)
            act_e.wait_ge(h_added, n_mixer[1])
            norm(4)
            peer_route(1)
            peer_dense(1)
            act_e.wait_ge(dn_added, n_peer[1])
            norm(5)

        @block.tensor
        def _(pe):
            def chunk_landed(n):
                pe.wait_ge(w_in[slot_of[n]], landed_by[n])

            def modulation(i):
                pe.wait_ge(macc_ready, i + 1)
                if i == NFIRST:
                    pe.wait_ge(mod_ready, 1)
                for j in range(4):
                    for who, acc in enumerate((macc, maccx) if i < NFIRST else (macc,)):
                        col = (4 * i + j) * 2 + who
                        mm = nc.tensor.matmul(ps[:, 7, col:col + 1], acc[:, i % 2, j * P:(j + 1) * P],
                                              ones[:, 0:1], start=True, stop=True)
                mm.then_inc(mod_mm, 1)

            pe.sem_inc(G_mm, 4)
            pe.wait_ge(x_in, 16 * 16)
            for i in range(NFIRST):
                modulation(i)

            def norm(n):
                width = NORMS[n][1]
                for k in range(KT):
                    pe.wait_ge(sq_ready, n * KT + k + 1)
                    nc.tensor.matmul(ps[:, 0, 0:width], ones[:, :], sq[:, k % 2, 0:width],
                                     start=(k == 0), stop=(k == KT - 1)).then_inc(sq_used, 1)

            norm(0)
            pe.wait_ge(rinv_ready, 1)
            norm(1)

            pe.wait_ge(rinv_ready, 2)
            pe.wait_ge(x_ready, 2 * KT)
            def rotate(rope):
                pe.wait_ge(rope_raw, rope + 1)
                at_least(pe, rope_out, rope - 1)
                nc.tensor.matmul(ps[:, 4 + rope % 2, :], rot[:, :], ropein[:, rope % 2, :],
                                 start=True, stop=True).then_inc(rope_mm, 1)

            for j, (kind, bank, _, rope, c, operands) in enumerate(in_jobs):
                n = W_IN + c
                chunk_landed(n)
                if j >= 4:
                    before = in_jobs[j - 4]
                    if before[0] == "rope":
                        pe.wait_ge(rope_raw, before[3] + 1)
                    else:
                        pe.wait_ge(proj_out, j - 3 - before[3])
                for k in range(KT):
                    w, x = operands(k)
                    mm = nc.tensor.matmul(bank, w, x, start=(k == 0), stop=(k == KT - 1))
                mm.then_inc(proj_mm, 1)
                if j >= 1 and in_jobs[j - 1][0] == "rope":
                    rotate(in_jobs[j - 1][3])
                for i, at in enumerate(MOD_AT):
                    if at == j - 2:
                        modulation(NFIRST + i)

            pe.wait_ge(proj_out, sum(job[0] == "copy" for job in in_jobs))
            pe.wait_ge(rope_out, 2 * HA)

            def scores(u):
                kind, h, qt = units[u]
                for m in range(2 if kind == "diff" else 1):
                    j = job_of[u] + m
                    if j - 2 < 2 * HEAD_END:
                        at_least(pe, exp_done, j - 1)
                    else:
                        pe.wait_ge(near_read, j - 1 - 2 * HEAD_END)
                    if kind == "diff":
                        q, kx, f, lo = qaT, kaT, h, DH * m
                    else:
                        q, kx, f, lo = qbT, kbT, h // 2, DH * (h % 2)
                    for c0, c1 in ((0, T), (T, TK)):
                        mm = nc.tensor.matmul(wide(j % 2)[:, c0:c1], q[lo:lo + DH, f, qt * P:(qt + 1) * P],
                                              kx[lo:lo + DH, f, c0:c1], start=True, stop=True)
                    mm.then_inc(score_mm, 1)

            def av(u):
                kind, h, qt = units[u]
                pe.wait_ge(probsT_ready, u + 1)
                at_least(pe, o_out, u)
                for kt in range(KK):
                    if kind == "diff":
                        dst, v = ps[:, 6, qt * P:(qt + 1) * P], va[:, kt, h * P:(h + 1) * P]
                    else:
                        lo = DH * (h % 2)
                        dst, v = ps[lo:lo + DH, 6, qt * P:(qt + 1) * P], vb[:, kt, h * DH:(h + 1) * DH]
                    mm = nc.tensor.matmul(dst, v, ATbuf[:, u % 2, kt * P:(kt + 1) * P],
                                          start=(kt == 0), stop=(kt == KK - 1))
                mm.then_inc(av_mm, 1)
                if kind == "diff" and qt == TT - 1:
                    pe.wait_ge(osq_ready, h + 1)
                    nc.tensor.matmul(ps[:, 6, :], ones[:, :], osq[:, :], start=True, stop=True).then_inc(osum_mm, 1)
                    pe.wait_ge(oms_ready, h + 1)

            scores(0)
            for u in range(len(units) + 2):
                if u + 1 < len(units):
                    scores(u + 1)
                if 1 <= u <= len(units):
                    pe.wait_ge(probs_ready, u)
                    at_least(pe, probsT_ready, u - 1)
                    for kt in range(KK):
                        mm = nc.tensor.transpose(wide(2)[:, kt * P:(kt + 1) * P],
                                                 Abuf[:, (u - 1) % 2, kt * P:(kt + 1) * P], ident[:, :])
                    mm.then_inc(probsT_mm, 1)
                if u >= 2:
                    av(u - 2)
            pe.wait_ge(o_out, len(units))
            pe.wait_ge(o_normed, HA)

            def out_projection(w0, src, done):
                for f in range(KT):
                    n = w0 + f // 4
                    if f % 4 == 0:
                        chunk_landed(n)
                    at_least(pe, h_added, done + f - 3)
                    for k in range(KT):
                        mm = nc.tensor.matmul(ps[:, f % 4, :], slots[n][:, k, (f % 4) * P:(f % 4 + 1) * P],
                                              src[:, k, :], start=(k == 0), stop=(k == KT - 1))
                    mm.then_inc(h_mm, 1)

            def peer_route(layer):
                def queries(r):
                    for n in range(HP):
                        w = W_Q[layer] + n // 4
                        i = (layer * TT + r) * HP + n
                        if r == 0 and n % 4 == 0:
                            chunk_landed(w)
                        at_least(pe, q_out, i - 3)
                        for k in range(KT):
                            mm = nc.tensor.matmul(ps[:, n % 4, 0:P], slots[w][:, k, (n % 4) * P:(n % 4 + 1) * P],
                                                  xm[:, k, r * P:(r + 1) * P], start=(k == 0), stop=(k == KT - 1))
                        mm.then_inc(q_mm, 1)

                def key_scores(r):
                    tile = r + layer * TT
                    pe.wait_ge(qs_ready, tile + 1)
                    at_least(pe, S_ready, tile * 4)
                    for n in range(HP):
                        mm = nc.tensor.matmul(ps[:, 4 + n // 4, (n % 4) * P:(n % 4 + 1) * P], qs[:, n, :],
                                              keysT[:, n, :], start=True, stop=True)
                    mm.then_inc(score_done, 1)

                def turn_picks(r):
                    tile = r + layer * TT
                    pe.wait_ge(pick_ready, tile + 1)
                    pe.wait_ge(G_out, tile * (P // 4) + 4)
                    for n in range(4):
                        mm = nc.tensor.transpose(ps[:, 0, n * P:(n + 1) * P],
                                                 pick[:, n, :, :].rearrange("p h k -> p (h k)"), ident[:, :])
                    mm.then_inc(pickT_mm, 1)

                def gate_weights(r):
                    with pe.Fori(0, NB // 2) as it:
                        for par in range(2):
                            n = (r + layer * TT) * NB + it * 2 + par
                            pe.wait_ge(hot_ready, n + 1)
                            for t in range(TOK):
                                if t % 4 == 0:
                                    pe.wait_ge(G_out, n * 2 + (t // 4 + 1))
                                mm = nc.tensor.matmul(ps[:, 2 * par + t // 4, (t % 4) * P:(t % 4 + 1) * P],
                                                      Bhot[:, par, t, :], Ahot[:, par, t, :], start=True, stop=True)
                                if t % 4 == 3:
                                    mm.then_inc(G_mm, 1)

                pe.wait_ge(keys_in, 16 * (layer + 1))
                queries(0)
                key_scores(0)
                queries(1)
                key_scores(1)
                queries(2)
                queries(3)
                pe.wait_ge(q_out, (layer + 1) * TT * HP)
                with pe.Fori(1, TT - 1) as r:
                    turn_picks(r - 1)
                    key_scores(r + 1)
                    gate_weights(r - 1)
                for r in range(TT - 2, TT):
                    turn_picks(r)
                    gate_weights(r)

            def peer_dense(layer):
                pe.wait_ge(x_split, (layer + 1) * KT)
                pe.wait_ge(G_out, (layer + 1) * TT * (P // 4) + 4)

                def up(g, par):
                    n = g + layer * NG
                    pe.wait_ge(U_split, n + 1)
                    for j in range(2):
                        at_least(pe, act_ready, n * 2 + (j - 1))
                        for k in range(KT):
                            cols = slice(j * P, (j + 1) * P)
                            for i, (w, x) in enumerate(((Uhi, xhi), (Uhi, xlo), (Ulo, xhi))):
                                mm = nc.tensor.matmul(ps[:, j, :], w[:, par, k, cols], x[:, k, :],
                                                      start=(k == 0 and i == 0), stop=(k == KT - 1 and i == 2))
                        mm.then_inc(up_mm, 1)

                def down(g, par):
                    n = g + layer * NG
                    pe.wait_ge(V_split, n + 1)
                    pe.wait_ge(H_ready, n * 2 + 2)
                    for d in range(KT):
                        at_least(pe, dn_added, n * KT + (d - 3))
                        cols = slice(d * P, (d + 1) * P)
                        for j in range(2):
                            for i, (w, x) in enumerate(((Vhi, Hhi), (Vhi, Hlo), (Vlo, Hhi))):
                                mm = nc.tensor.matmul(ps[:, 2 + d % 4, :], w[:, par, j, cols], x[:, par, j, :],
                                                      start=(j == 0 and i == 0), stop=(j == 1 and i == 2))
                        mm.then_inc(dn_mm, 1)

                up(0, 0)
                up(1, 1)
                down(0, 0)
                with pe.Fori(1, NG // 2) as it:
                    for par in range(2):
                        up(it * 2 + par, par)
                        down(it * 2 + (par - 1), 1 - par)
                down(NG - 1, 1)

            out_projection(W_OUT, oT, 0)
            norm(2)
            pe.wait_ge(rinv_ready, 3)
            pe.wait_ge(x_ready, 3 * KT)
            peer_route(0)
            peer_dense(0)
            norm(3)
            pe.wait_ge(rinv_ready, 4)
            pe.wait_ge(x_ready, 4 * KT)
            pe.wait_ge(gl_in, 16 * 5)
            for c in range(2):
                n = W_GIN + c
                chunk_landed(n)
                for tt in range(TT):
                    i = c * TT + tt
                    at_least(pe, v_gelu, i - 3)
                    for k in range(KT):
                        nc.tensor.matmul(ps[:, i % 4, :], xm[:, k, tt * P:(tt + 1) * P], slots[n][:, k, :],
                                         start=(k == 0), stop=False)
                    nc.tensor.matmul(ps[:, i % 4, :], ones_row[:, :], bvrow[:, c * CW:(c + 1) * CW],
                                     start=False, stop=True).then_inc(v_mm, 1)
            pe.wait_ge(v_gelu, 2 * TT)
            for f in range(KT):
                n = W_GIN + 2 + f // 4
                if f % 4 == 0:
                    chunk_landed(n)
                at_least(pe, u_gelu, f - 3)
                for k in range(KT):
                    mm = nc.tensor.matmul(ps[:, f % 4, :], slots[n][:, k, (f % 4) * P:(f % 4 + 1) * P],
                                          xm[:, k, :], start=(k == 0), stop=(k == KT - 1))
                mm.then_inc(u_mm, 1)
            pe.wait_ge(v_normed, TT)
            for g in range(KT):
                at_least(pe, y_ready, g - 1)
                for tt in range(TT):
                    mm = nc.tensor.matmul(ps[:, 4 + g % 2, tt * P:(tt + 1) * P], vsb[:, tt, g * P:(g + 1) * P],
                                          wsT[:, g, :], start=True, stop=True)
                mm.then_inc(sv_mm, 1)
            pe.wait_ge(y_ready, KT)
            out_projection(W_GOUT, yT, KT)
            norm(4)
            pe.wait_ge(rinv_ready, 5)
            pe.wait_ge(x_ready, 5 * KT)
            peer_route(1)
            peer_dense(1)
            norm(5)

        @block.vector
        def _(dve):
            step = Chain(dve, dve_step)

            def modulation(layer, n0, n1, who):
                dve.wait_ge(mod_mm, NFIRST if (layer, n0) == (0, 0) else NCH)
                col = 2 * 6 * KT * layer
                sums = ps[:, 7, col + 2 * n0:col + 2 * n1].rearrange("p (n w) -> p n w", w=2)[:, :, 0:who]
                step(nc.vector.scalar_tensor_tensor(
                    out=mods[:, layer, n0:n1, 0:who], in0=sums, scalar=float(D),
                    in1=bmod[:, layer, n0:n1].unsqueeze(2).to_broadcast([P, n1 - n0, who]),
                    op0=ALU.mult, op1=ALU.add))
                for sc in (sc1, sc2):
                    if n0 <= sc < n1:
                        step(nc.vector.tensor_scalar(mods[:, layer, sc:sc + KT, 0:who],
                                                     mods[:, layer, sc:sc + KT, 0:who], 1.0, None, ALU.add))

            def norm(n):
                src, width, dst, layer, sh, sc, who = NORMS[n]
                dve.wait_ge(sq_used, (n + 1) * KT)
                nc.vector.tensor_scalar(rms[:, 0:width], ps[:, 0, 0:width], EPS, None, ALU.add).then_inc(ms_ready, 1)
                dve.wait_ge(rms_ready, n + 1)
                nc.vector.reciprocal(rinv[:, 0:width], rms[:, 0:width]).then_inc(rinv_ready, 1)
                dve.wait_ge(rinv_ready, n + 1)
                for k in range(KT):
                    scale = fing[:, k:k + 1] if sc is None else mods[:, layer, sc + k, who:who + 1]
                    nc.vector.scalar_tensor_tensor(out=dst[:, k, :], in0=src[:, k, :], scalar=scale,
                                                   in1=rinv[:, 0:width], op0=ALU.mult, op1=ALU.mult
                                                   ).then_inc(x_scaled, 1)

            def sum_chunk(i):
                at_least(dve, mod_mm, i - 1)
                for half in range(2):
                    m = 2 * i + half
                    dve.wait_ge(mod_in[mslot[m]], mlanded[m])
                    for k in range(KT // 2):
                        for who, acc in enumerate((macc, maccx) if i < NFIRST else (macc,)):
                            w, c = modw[mslot[m]][:, k, :], condS[:, half * (KT // 2) + k, who:who + 1]
                            if m % 2 == 0 and k == 0:
                                ins = nc.vector.tensor_scalar(acc[:, i % 2, :], w, c, None, ALU.mult)
                            else:
                                ins = nc.vector.scalar_tensor_tensor(out=acc[:, i % 2, :], in0=w, scalar=c,
                                                                     in1=acc[:, i % 2, :], op0=ALU.mult, op1=ALU.add)
                        if k < KT // 2 - 1:
                            step(ins)
                    ins.then_inc(mod_read, 1)
                    dve.wait_ge(mod_read, m + 1)
                dve.sem_inc(macc_ready, 1)

            dve.wait_ge(x_in, 16 * 16)
            step(nc.vector.tensor_tensor(lamtmp[:, :, :], lamin[:, 0:4:2, :], lamin[:, 1:4:2, :], ALU.mult))
            step(nc.vector.tensor_reduce(lamv[:, 0:2], lamtmp[:, :, :], AX, ALU.add))
            nc.vector.tensor_scalar(subg8[:, :], sublg[:, :], 1.0 - LAM_INIT, None, ALU.mult).then_inc(lam_sum, 1)
            dve.wait_ge(cond_ready, 1)
            for i in range(NFIRST):
                sum_chunk(i)
            modulation(0, 0, g1, 2)
            dve.sem_inc(mod_ready, 1)
            norm(0)
            norm(1)

            for j, (kind, _, dst, rope, _, _) in enumerate(in_jobs):
                if j >= 1:
                    for i, at in enumerate(MOD_AT):
                        if at == j - 1:
                            sum_chunk(NFIRST + i)
                if kind != "rope":
                    continue
                dve.wait_ge(rope_raw, rope + 1)
                at_least(dve, rope_out, rope)
                step(nc.vector.tensor_tensor(ropetmp[:, 0, :], ropein[:, rope % 2, :], cosT[:, :], ALU.mult))
                dve.wait_ge(rope_mm, rope + 1)
                step(nc.vector.tensor_tensor(ropetmp[:, 1, :], ps[:, 4 + rope % 2, :], sinT[:, :], ALU.mult))
                nc.vector.tensor_tensor(dst, ropetmp[:, 0, :], ropetmp[:, 1, :], ALU.add).then_inc(rope_out, 1)
            modulation(0, g1, 6 * KT, 1)
            modulation(1, 0, 6 * KT, 1)
            dve.wait_ge(rope_out, 2 * HA)
            dve.wait_ge(lam_exp, 1)
            step(nc.vector.tensor_tensor(lamv[:, 4:5], lamv[:, 3:4], lamv[:, 2:3], ALU.subtract))
            step(nc.vector.tensor_scalar(lamv[:, 5:6], lamv[:, 4:5], -LAM_INIT, None, ALU.add))

            def maxima(u):
                kind, h, qt = units[u]
                for m in range(2 if kind == "diff" else 1):
                    j = job_of[u] + m
                    if kind == "near" and qt == 0:
                        dve.wait_ge(bias_in[h % 2], 16 * (h // 2 + 1))
                        step(nc.vector.tensor_tensor(btab[:, h % 2, :, :], btab[:, h % 2, :, :],
                                                     mask[:, :].unsqueeze(1).to_broadcast([P, 16, GRID_W]), ALU.add))
                    dve.wait_ge(score_mm, j + 1)
                    if kind == "diff":
                        step(nc.vector.tensor_reduce(mx[:, j:j + 1], wide(j % 2)[:, 0:TK], AX, ALU.max))
                        nc.vector.tensor_scalar(nmx[:, j:j + 1], mx[:, j:j + 1], -QK_SCALE, None,
                                                ALU.mult).then_inc(nmax_ready, 1)
                        continue
                    dve.wait_ge(exp_done, j - 1)
                    row = NA_ROWS - 1 - 2 * qt
                    bias = nc.vector.scalar_tensor_tensor(
                        out=Sbuf[:, j % 2, 0:T], in0=wide(j % 2)[:, 0:T], scalar=QK_SCALE,
                        in1=btab[:, h % 2, row:row + NA_ROWS, :].rearrange("p r c -> p (r c)"),
                        op0=ALU.mult, op1=ALU.add)
                    if qt == TT - 1:
                        bias.then_inc(bias_used, 1)
                    nc.vector.tensor_scalar(Sbuf[:, j % 2, T:TK], wide(j % 2)[:, T:TK], QK_SCALE, None, ALU.mult
                                            ).then_inc(near_read, 1)
                    dve.wait_ge(near_read, j + 1 - 2 * HEAD_END)
                    step(nc.vector.tensor_reduce(mx[:, j:j + 1], Sbuf[:, j % 2, :], AX, ALU.max))
                    nc.vector.tensor_scalar(nmx[:, j:j + 1], mx[:, j:j + 1], -1.0, None,
                                            ALU.mult).then_inc(nmax_ready, 1)

            def probabilities(u):
                kind, h, qt = units[u]
                j = job_of[u]
                n = 2 if kind == "diff" else 1
                dve.wait_ge(exp_done, j + n)
                step(nc.vector.reciprocal(rz[:, j:j + n], zs[:, j:j + n]))
                at_least(dve, probsT_mm, u - 1)
                dst = Abuf[:, u % 2, :]
                if kind == "diff":
                    i = j // 2
                    step(nc.vector.tensor_tensor(nlr[:, i:i + 1], rz[:, j + 1:j + 2], lamv[:, 5:6], ALU.mult))
                    step(nc.vector.tensor_scalar(dst, Ebuf[:, (j + 1) % 4, :], nlr[:, i:i + 1], None, ALU.mult))
                    nc.vector.scalar_tensor_tensor(out=dst, in0=Ebuf[:, j % 4, :], scalar=rz[:, j:j + 1], in1=dst,
                                                   op0=ALU.mult, op1=ALU.add).then_inc(probs_ready, 1)
                else:
                    nc.vector.tensor_scalar(dst, Ebuf[:, j % 4, :], rz[:, j:j + 1], None,
                                            ALU.mult).then_inc(probs_ready, 1)

            def outputs(u):
                kind, h, qt = units[u]
                cols = slice(qt * P, (qt + 1) * P)
                dve.wait_ge(av_mm, u + 1)
                if kind == "near":
                    lo = DH * (h % 2)
                    nc.vector.tensor_copy(oT[lo:lo + DH, HA + h // 2, cols], ps[lo:lo + DH, 6, cols]
                                          ).then_inc(o_out, 1)
                    return
                nc.vector.tensor_copy(oT[:, h, cols], ps[:, 6, cols]).then_inc(o_out, 1)
                if qt < TT - 1:
                    return
                dve.wait_ge(o_out, u + 1)
                nc.vector.tensor_tensor(osq[:, :], oT[:, h, :], oT[:, h, :], ALU.mult).then_inc(osq_ready, 1)
                dve.wait_ge(osum_mm, h + 1)
                nc.vector.tensor_scalar(osq[:, :], ps[:, 6, :], float(D // P), EPS, ALU.mult, ALU.add
                                        ).then_inc(oms_ready, 1)
                dve.wait_ge(orms_ready, h + 1)
                step(nc.vector.reciprocal(orinv[:, :], osq[:, :]))
                nc.vector.scalar_tensor_tensor(out=oT[:, h, :], in0=oT[:, h, :], scalar=subg8[:, :],
                                               in1=orinv[:, :], op0=ALU.mult, op1=ALU.mult).then_inc(o_normed, 1)
                dve.wait_ge(o_normed, h + 1)

            maxima(0)
            for u in range(len(units)):
                if u + 1 < len(units):
                    maxima(u + 1)
                probabilities(u)
                if u >= 2:
                    outputs(u - 2)
            outputs(len(units) - 2)
            outputs(len(units) - 1)

            def add_projection(layer):
                for f in range(KT):
                    dve.wait_ge(h_mm, layer * KT + f + 1)
                    nc.vector.scalar_tensor_tensor(out=hT[:, f, :], in0=ps[:, f % 4, :],
                                                   scalar=mods[:, layer, g1 + f, 0:1], in1=hT[:, f, :],
                                                   op0=ALU.mult, op1=ALU.add).then_inc(h_added, 1)
                dve.wait_ge(h_added, (layer + 1) * KT)

            ROUTE_STEPS = 24

            def carry_wait():
                nc.vector.memset(carrier[:, :], 0.0)

            def peer_route(layer):
                def picks(r):
                    tile = r + layer * TT
                    link = Chain(dve, route_step, tile * ROUTE_STEPS)
                    dve.wait_ge(S_ready, tile * 4 + 4)
                    carry_wait()

                    def top16(rows, vals, ids, src, spare, src_free=None):
                        for i in rows:
                            last = nc.vector.max(vals(i)[:, 0:8], src(i))
                        link(last)
                        carry_wait()
                        for i in rows:
                            nc.vector.max_index(ids(i)[:, 0:8], vals(i)[:, 0:8], src(i))
                            last = nc.vector.match_replace(spare(i), vals(i)[:, 0:8], src(i), NEG)
                        link(last)
                        if src_free is not None:
                            dve.sem_inc(src_free, 1)
                        carry_wait()
                        for i in rows:
                            last = nc.vector.max(vals(i)[:, 8:16], spare(i))
                        link(last)
                        carry_wait()
                        for i in rows:
                            last = nc.vector.max_index(ids(i)[:, 8:16], vals(i)[:, 8:16], spare(i))
                        link(last)

                    top16(range(HP), lambda i: topv[:, i // 2, i % 2, :], lambda i: topi[:, i // 2, i % 2, :],
                          lambda i: S[:, i, :], lambda i: S2[:, i, :], S_free)
                    for a0, a1, nb in ((0, FULL, TOPK), (FULL, TOPK, SHORT)):
                        shape = [P, PH, a1 - a0, nb]
                        c0 = 0 if a0 == 0 else FULL * TOPK
                        last = nc.vector.tensor_tensor(
                            cand[:, 0, :, c0:c0 + (a1 - a0) * nb].rearrange("p h (a b) -> p h a b", b=nb),
                            topv[:, :, 0, a0:a1].unsqueeze(3).to_broadcast(shape),
                            topv[:, :, 1, 0:nb].unsqueeze(2).to_broadcast(shape), ALU.add)
                    link(last)
                    carry_wait()
                    top16(range(PH), lambda i: candv[:, i, :], lambda i: candi[:, i, :],
                          lambda i: cand[:, 0, i, :], lambda i: cand[:, 1, i, :])
                    nc.vector.tensor_scalar(shifted[:, 0, :, :], candi[:, :, :], 4, None, ALU.logical_shift_right)
                    link(nc.vector.tensor_scalar(shifted[:, 1, :, :], candi[:, :, :], 2, None,
                                                 ALU.logical_shift_right))
                    link(nc.vector.scalar_tensor_tensor(
                        out=rank[:, 0, :, :], in0=shifted[:, 1, :, :], scalar=float(FULL - FULL * TOPK // SHORT),
                        in1=shifted[:, 0, :, :], op0=ALU.add, op1=ALU.max))
                    link(nc.vector.tensor_scalar(rank[:, 1, :, :], rank[:, 0, :, :], float(SHORT),
                                                 float(FULL * (TOPK - SHORT)), ALU.mult, ALU.add))
                    link(nc.vector.scalar_tensor_tensor(
                        out=rank[:, 1, :, :], in0=rank[:, 0, :, :], scalar=float(TOPK), in1=rank[:, 1, :, :],
                        op0=ALU.mult, op1=ALU.min))
                    link(nc.vector.tensor_tensor(rank[:, 1, :, :], candi[:, :, :], rank[:, 1, :, :], ALU.subtract))
                    at_least(dve, pickT_mm, tile)
                    shape = [P, PH, TOPK, TOPK]
                    for half, keys in enumerate((key1[:, :, :], pick[:, 2, :, :])):
                        link(nc.vector.tensor_tensor(eq[:, :, :, :],
                                                     iota16[:, :].unsqueeze(1).unsqueeze(1).to_broadcast(shape),
                                                     rank[:, half, :, :].unsqueeze(3).to_broadcast(shape),
                                                     ALU.is_equal))
                        link(nc.vector.tensor_tensor(eq[:, :, :, :], eq[:, :, :, :],
                                                     topi[:, :, half, :].unsqueeze(2).to_broadcast(shape), ALU.mult))
                        link(nc.vector.tensor_reduce(keys, eq[:, :, :, :], AX, ALU.add))
                    nc.vector.tensor_tensor(pick[:, 3, :, :], candv[:, :, :],
                                            candv[:, :, 0:1].to_broadcast([P, PH, TOPK]), ALU.subtract
                                            ).then_inc(gate_logits, 1)
                    link(nc.vector.tensor_copy(key1u[:, 0, :, :], key1[:, :, :]))
                    nc.vector.tensor_scalar(key1u[:, 1, :, :], key1u[:, 0, :, :], NKEY - TOPK, None, ALU.bitwise_and)
                    link(nc.vector.tensor_scalar(key1u[:, 2, :, :], key1u[:, 0, :, :], TOPK - 1, None,
                                                 ALU.bitwise_and))
                    nc.vector.tensor_copy(pick[:, 0:2, :, :], key1u[:, 1:3, :, :])
                    dve.wait_ge(gate_exp, tile + 1)
                    link(nc.vector.tensor_reduce(zsum[:, 0, :], pick[:, 3, :, :], AX, ALU.add))
                    link(nc.vector.reciprocal(zsum[:, 1, :], zsum[:, 0, :]))
                    nc.vector.tensor_tensor(pick[:, 3, :, :], pick[:, 3, :, :],
                                            zsum[:, 1, :].unsqueeze(2).to_broadcast([P, PH, TOPK]), ALU.mult
                                            ).then_inc(pick_ready, 1)
                    used = link.n - tile * ROUTE_STEPS
                    if isinstance(used, int):
                        assert used == ROUTE_STEPS, used

                def one_hots(r):
                    tile = r + layer * TT
                    dve.wait_ge(pickT_mm, tile + 1)
                    nc.vector.tensor_copy(pickT[:, :, :].rearrange("p n t -> p (n t)"), ps[:, 0, :]
                                          ).then_inc(pickT_out, 1)
                    dve.wait_ge(pickT_out, tile + 1)
                    for half in range(2):
                        cols = slice(half * P // 2, (half + 1) * P // 2)
                        if half == 1:
                            dve.wait_ge(hot_ready, tile * NB + NB // 2)
                        link = Chain(dve, hot_step, (tile * 2 + half) * 2)
                        nc.vector.tensor_tensor(hot_lo[:, :, :],
                                                iota16[:, :].unsqueeze(1).to_broadcast([P, P // 2, TOPK]),
                                                pickT[:, 1, cols].unsqueeze(2).to_broadcast([P, P // 2, TOPK]),
                                                ALU.is_equal)
                        shape = [P, P // 2, NHI]
                        link(nc.vector.tensor_tensor(hot_hi[:, :, :], iota8[:, :].unsqueeze(1).to_broadcast(shape),
                                                     pickT[:, 0, cols].unsqueeze(2).to_broadcast(shape),
                                                     ALU.is_equal))
                        link(nc.vector.tensor_tensor(hot_hi[:, :, :], hot_hi[:, :, :],
                                                     pickT[:, 3, cols].unsqueeze(2).to_broadcast(shape), ALU.mult))
                        carry_wait()
                        with dve.Fori(0, NB // 4) as it:
                            for par in range(2):
                                n = tile * NB + half * (NB // 2) + it * 2 + par
                                dve.wait_ge(G_mm, n * 2 + 2)
                                t0 = (it * 2 + par) * TOK
                                shape = [P, TOK, P]
                                nc.vector.tensor_tensor(
                                    Bhot[:, par, :, :], iota[:, :].unsqueeze(1).to_broadcast(shape),
                                    pickT[:, 2, bass.ds(t0 + half * (P // 2), TOK)].unsqueeze(2).to_broadcast(shape),
                                    ALU.is_equal)
                                shape = [P, TOK, NHI, TOPK]
                                nc.vector.tensor_tensor(
                                    Ahot[:, par, :, :].rearrange("p t (a b) -> p t a b", b=TOPK),
                                    hot_hi[:, bass.ds(t0, TOK), :].unsqueeze(3).to_broadcast(shape),
                                    hot_lo[:, bass.ds(t0, TOK), :].unsqueeze(2).to_broadcast(shape),
                                    ALU.mult).then_inc(hot_ready, 1)
                    dve.wait_ge(hot_ready, (tile + 1) * NB)

                picks(0)
                with dve.Fori(1, TT) as r:
                    picks(r)
                    one_hots(r - 1)
                one_hots(TT - 1)

            def peer_dense(layer):
                for k in range(KT):
                    dve.wait_ge(x_hi, layer * KT + k + 1)
                    nc.vector.tensor_tensor(xlo[:, k, :], xm[:, k, :], xhi[:, k, :].bitcast(F32),
                                            ALU.subtract).then_inc(x_split, 1)

                def rest_of_U(g, par):
                    dve.wait_ge(U_hi, g + layer * NG + 1)
                    nc.vector.tensor_tensor(Ulo[:, par, :, :], Uraw[:, par, :, :], Uhi[:, par, :, :].bitcast(F32),
                                            ALU.subtract).then_inc(U_split, 1)

                def rest_of_V(g, par):
                    dve.wait_ge(V_hi, g + layer * NG + 1)
                    nc.vector.tensor_tensor(Vlo[:, par, :, :], Vraw[:, par, :, :], Vhi[:, par, :, :].bitcast(F32),
                                            ALU.subtract).then_inc(V_split, 1)

                def gated(g, par, it, j):
                    n = (g + layer * NG) * 2 + j
                    dve.wait_ge(act_ready, n + 1)
                    dve.wait_ge(G_in[par], (it + (layer * (NG // 2) + 1)) * 16)
                    at_least(dve, dn_mm, (g + (layer * NG - 1)) * KT)
                    nc.vector.tensor_tensor(Hf[:, j, :], act[:, j, :], Gin[:, par, j, :], ALU.mult
                                            ).then_inc(H_step, 1)
                    dve.wait_ge(H_step, n * 2 + 1)
                    nc.vector.tensor_copy(Hhi[:, par, j, :], Hf[:, j, :]).then_inc(H_step, 1)
                    dve.wait_ge(H_step, n * 2 + 2)
                    nc.vector.tensor_tensor(Hlo[:, par, j, :], Hf[:, j, :], Hhi[:, par, j, :].bitcast(F32),
                                            ALU.subtract).then_inc(H_ready, 1)

                def add_group(g):
                    n = (g + layer * NG) * KT
                    for d in range(KT):
                        dve.wait_ge(dn_mm, n + (d + 1))
                        at_least(dve, dn_added, n + (d + 1 - KT))
                        nc.vector.scalar_tensor_tensor(out=hT[:, d, :], in0=ps[:, 2 + d % 4, :],
                                                       scalar=mods[:, layer, g2 + d, 0:1], in1=hT[:, d, :],
                                                       op0=ALU.mult, op1=ALU.add).then_inc(dn_added, 1)

                def period(g, par, it, first=False, last=False):
                    if not last:
                        rest_of_U(g + 1, 1 - par)
                    gated(g, par, it, 0)
                    rest_of_V(g, par)
                    gated(g, par, it, 1)
                    if not first:
                        add_group(g - 1)

                rest_of_U(0, 0)
                period(0, 0, 0, first=True)
                period(1, 1, 0)
                with dve.Fori(1, NG // 2 - 1) as it:
                    for par in range(2):
                        period(it * 2 + par, par, it)
                period(NG - 2, 0, NG // 2 - 1)
                period(NG - 1, 1, NG // 2 - 1, last=True)
                add_group(NG - 1)
                dve.wait_ge(dn_added, (layer + 1) * NG * KT)

            add_projection(0)
            norm(2)
            peer_route(0)
            peer_dense(0)
            norm(3)
            dve.wait_ge(gl_in, 16 * 5)
            dve.wait_ge(v_gelu, 2 * TT)
            for tt in range(TT):
                for c in range(2):
                    last = nc.vector.bn_stats(bnst[:, tt, c, :], vsb[:, tt, c * CW:(c + 1) * CW])
                step(last)
                last = nc.vector.bn_aggr(bnag[:, tt, :], bnst[:, tt, :, :])
            step(last)
            nc.vector.tensor_scalar(rstd[:, 0, :], bnag[:, :, 1], EPS, None, ALU.add).then_inc(var_ready, 1)
            dve.wait_ge(std_ready, 1)
            step(nc.vector.reciprocal(rstd[:, 1, :], rstd[:, 0, :]))
            for tt in range(TT):
                row = vsb[:, tt, :]
                step(nc.vector.tensor_scalar(row, row, bnag[:, tt, 0:1], rstd[:, 1, tt:tt + 1], ALU.subtract, ALU.mult))
                step(nc.vector.tensor_tensor(row, row, lng[:, :], ALU.mult))
                nc.vector.tensor_tensor(row, row, lnb[:, :], ALU.add).then_inc(v_normed, 1)
            dve.wait_ge(u_gelu, KT)
            for g in range(KT):
                dve.wait_ge(sv_mm, g + 1)
                at_least(dve, y_ready, g - 1)
                step(nc.vector.tensor_tensor(svb[:, g % 2, :].rearrange("p (n t) -> p n t", n=TT),
                                             ps[:, 4 + g % 2, :].rearrange("p (n t) -> p n t", n=TT),
                                             bsb[:, g, :].unsqueeze(1).to_broadcast([P, TT, P]), ALU.add))
                nc.vector.tensor_tensor(yT[:, g, :], svb[:, g % 2, :], uT[:, g, :], ALU.mult).then_inc(y_ready, 1)
            add_projection(1)
            norm(4)
            peer_route(1)
            peer_dense(1)
            norm(5)

    return nc


def constants():
    f = np.float32
    p = np.arange(P)
    d = p % DH
    axis, half, i = d // 32, d % 32 // 16, d % 16
    inv_freq = (1.0 / (f(10000.0) ** (np.arange(0, DH // 2, 2, dtype=f) / f(DH // 2)))).astype(f)
    t = np.arange(T)
    place = np.stack([t // GRID_W, t % GRID_W]).astype(f)
    angle = (place[axis] * inv_freq[i][:, None]).astype(f)
    rot = np.zeros((P, P), f)
    rot[p + 16 * (1 - 2 * half), p] = 2 * half - 1
    col = p % GRID_W
    first = np.clip(col - NA_COLS // 2, 0, GRID_W - NA_COLS)[:, None]
    key = np.arange(GRID_W)[None, :]
    mask = np.where((key >= first) & (key < first + NA_COLS), 0.0, MASKED).astype(f)
    return {
        "ones": np.full((P, P), 1.0 / D, f), "ident": np.eye(P, dtype=f),
        "iota": np.tile(np.arange(P, dtype=f), (P, 1)), "iota16": np.tile(np.arange(TOPK, dtype=f), (P, 1)),
        "iota8": np.tile(np.arange(0, NKEY, TOPK, dtype=f), (P, 1)),
        "cosT": np.cos(angle).astype(f), "sinT": np.sin(angle).astype(f), "rot": rot, "mask": mask,
        "ones_row": np.ones((1, P), f),
    }


def columns_of(v):
    v = v.reshape(v.shape[:-1] + (v.shape[-1] // P, P))
    return np.moveaxis(v, -1, 0)


def layout(i):
    p = np.arange(P)[:, None, None]
    s = np.arange(16)[None, :, None]
    k = np.arange(GRID_W)[None, None, :]
    dr = np.clip(s - p // GRID_W, 0, 2 * NA_ROWS - 2)
    dc = np.clip(k - p % GRID_W + NA_COLS - 1, 0, 2 * NA_COLS - 2)
    U = i["peer_u"].reshape(DEPTH, NG, 2 * P, KT, P)
    arrays = {
        "xT": i["x"][0].T, "ctxT": i["ctx"][0].T,
        "cond": columns_of(np.stack([i["c"][0], i["c_ctx"]])).transpose(0, 2, 1),
        "b_mod": columns_of(i["b_mod"]), "w_mod": i["w_mod"],
        "attn_in": i["attn_w_in"], "attn_out": i["attn_w_out"], "query": i["peer_w_query"],
        "gate_in": np.concatenate([i["chunk_w_in"][:, :, D:], i["chunk_w_in"][:, :, :D]], axis=2),
        "gate_out": i["chunk_w_out"],
        "lam": np.broadcast_to(np.stack([i["lambda_q1"][0], i["lambda_k1"][0], i["lambda_q2"][0],
                                         i["lambda_k2"][0]]), (P, 4, DH)),
        "subln_g": i["subln_g"][0][:, None], "btab": i["na_rpb"][0][:, dr, dc],
        "bu": columns_of(i["chunk_b_in"][0, :D]), "bv": i["chunk_b_in"][:, D:],
        "ln_g": i["chunk_ln_g"][0], "ln_b": i["chunk_ln_b"][0], "b_s": i["chunk_b_s"][0],
        "w_sT": i["chunk_w_s"][0].transpose(2, 0, 1),
        "keysT": i["peer_sub_keys"].reshape(DEPTH, HP, NKEY, P).transpose(0, 3, 1, 2),
        "UT": U.transpose(0, 1, 4, 3, 2), "V": i["peer_v"].reshape(DEPTH, NG, 2, P, D),
        "final_g": columns_of(i["final_norm_g"]),
    }
    arrays.update(constants())
    return arrays


def kernel(**inputs):
    import concourse.bacc as bacc
    from concourse.bass_utils import run_bass_kernel_spmd

    nc = bacc.Bacc("TRN2", target_bir_lowering=False, num_devices=1)
    arrays, aps = {}, {}
    for name, v in layout({k: np.asarray(v) for k, v in inputs.items()}).items():
        v = np.ascontiguousarray(v)
        arrays[f"in_{name}"] = v
        aps[name] = nc.dram_tensor(f"in_{name}", v.shape, mybir.dt.from_np(v.dtype), kind="ExternalInput").ap()
    out = nc.dram_tensor("out_T", (D, T), F32, kind="ExternalOutput").ap()
    backbone(nc, aps, out)
    r = run_bass_kernel_spmd(nc, [arrays], core_ids=[0])
    return np.ascontiguousarray(r.results[0]["out_T"].T)[None]
```

```python
import math
from contextlib import ExitStack

import numpy as np

import concourse.bass as bass
from concourse import mybir

F32 = mybir.dt.float32
F32R = mybir.dt.float32r
U32 = mybir.dt.uint32
ACT = mybir.ActivationFunctionType
ALU = mybir.AluOpType
AX = mybir.AxisListType.X

P = 128
D = 1024
KT = D // P
T = 512
TT = T // P
TC = 256
TK = T + TC
KK = TK // P
CW = 512
NMOD = 6 * D // CW
GRID_W = 64
NA_ROWS, NA_COLS = 8, 16
HA, HB, DH = 4, 8, 64
QK_SCALE = DH ** -0.5
LAM_INIT = 0.8 - 0.6 * math.exp(-0.3 * 0)
EPS = 1e-6
PH, NKEY, TOPK = 8, 128, 16
HP = 2 * PH
NE = NKEY * NKEY
NG = NKEY // 2
DEPTH = 2
NEG = -3.0e38
MASKED = -1.0e30
RING = 3
TOK = 8
NB = P // TOK
BESIDE, AFTER, TAIL = 2, 4, 6
EARLY = (TT - 1) * BESIDE + (TT - 2) * AFTER + TAIL
EG = EARLY // 2
NHI = NKEY // TOPK
FULL, SHORT = 4, 4
NCAND = FULL * TOPK + (TOPK - FULL) * SHORT

BASE = 17408


def at_least(eng, sem, value):
    if isinstance(value, int) and value <= 0:
        return
    eng.wait_ge(sem, value)


class Chain:

    def __init__(self, eng, sem, start=0):
        self.eng, self.sem, self.n = eng, sem, start

    def __call__(self, ins):
        self.n = self.n + 1
        ins.then_inc(self.sem, 1)
        self.eng.wait_ge(self.sem, self.n)


def backbone(nc, a, out):
    with ExitStack() as ctx:
        def sb(name, kib, shape, dt=F32):
            return nc.alloc_sbuf_tensor_at(name, shape, dt, offset=BASE + int(kib * 1024))

        def sem(name):
            return ctx.enter_context(nc.semaphore(name))

        hT = sb("hT", 0, [P, KT, T])
        mods = sb("mods", 16, [P, DEPTH, 6 * KT, 2])
        ones = sb("ones", 16.75, [P, P])
        ident = sb("ident", 17.25, [P, P])
        iota = sb("iota", 17.75, [P, P])
        cond = sb("cond", 18.25, [P, KT, 2])
        condS = sb("condS", 18.375, [P, KT, 2])
        bmod = sb("bmod", 18.5, [P, DEPTH, 6 * KT])
        fing = sb("fing", 19, [P, KT])
        rinv = sb("rinv", 20, [P, T])
        rms = sb("rms", 204, [P, T])
        bu = sb("bu", 22, [P, KT])
        iota8 = sb("iota8", 22.75, [P, NHI])
        carrier = sb("carrier", 22.6875, [P, 1])
        iota16 = sb("iota16", 22.125, [P, TOPK])
        lamv = sb("lamv", 22.25, [P, 8])
        sublg = sb("sublg", 22.5, [P, 1])
        subg8 = sb("subg8", 22.53125, [P, 1])
        ones_row = sb("ones_row", 19.25, [1, P])
        lamtmp = sb("lamtmp", 104, [P, 2, DH])
        lamin = sb("lamin", 23, [P, 4, DH])
        xm = sb("xm", 24, [P, KT, T])
        sq = sb("sq", 128, [P, 2, T])
        ring = [sb(f"ring{n}", 134 + 16 * n, [P, KT, CW]) for n in range(RING + 1)]
        modw = [sb(f"modw{n}", at, [P, KT // 2, CW]) for n, at in enumerate((182, 190, 48))]
        macc = sb("macc", 128, [P, 2, CW])
        maccx = sb("maccx", 56, [P, 2, CW])
        xc = sb("xc", 40, [P, KT, TC])
        ctxT = sb("ctxT", 48, [P, KT, TC])
        qaT = sb("qaT", 56, [P, HA, T])
        kaT = sb("kaT", 64, [P, HA, TK])
        qbT = sb("qbT", 76, [P, HB // 2, T])
        kbT = sb("kbT", 84, [P, HB // 2, TK])
        va = sb("va", 96, [P, KK, CW])
        vb = sb("vb", 108, [P, KK, CW])
        cosT = sb("cosT", 120, [P, T])
        sinT = sb("sinT", 122, [P, T])
        ropein = sb("ropein", 124, [P, 2, T])
        rot = sb("rot", 132, [P, P])
        mask = sb("mask", 132.5, [P, GRID_W])
        ropetmp = sb("ropetmp", 198, [P, 2, T])
        oT = sb("oT", 24, [P, KT, T])
        btab = sb("btab", 40, [P, 2, 16, GRID_W])
        osq = sb("osq", 48, [P, T])
        orinv = sb("orinv", 50, [P, T])
        Ebuf = sb("Ebuf", 182, [P, 4, TK])
        ATbuf = sb("ATbuf", 120, [P, 2, TK])
        Abuf = sb("Abuf", 126, [P, 2, TK])
        Sbuf = sb("Sbuf", 194, [P, 2, TK])
        mx = sb("mx", 200, [P, 64])
        nmx = sb("nmx", 200.25, [P, 64])
        zs = sb("zs", 200.5, [P, 64])
        rz = sb("rz", 200.75, [P, 64])
        nlr = sb("nlr", 201, [P, 16])
        vsb = sb("vsb", 40, [P, TT, D])
        uT = sb("uT", 56, [P, KT, T])
        lng = sb("lng", 72, [P, D])
        lnb = sb("lnb", 76, [P, D])
        bsb = sb("bsb", 80, [P, KT, P])
        wsT = sb("wsT", 84, [P, KT, P])
        yT = sb("yT", 88, [P, KT, T])
        svb = sb("svb", 104, [P, 2, T])
        bvrow = sb("bvrow", 116, [1, D])
        bnst = sb("bnst", 120, [P, TT, 2, 6])
        bnag = sb("bnag", 120.25, [P, TT, 2])
        rstd = sb("rstd", 120.5, [P, 2, TT])
        qT = sb("qT", 40, [P, TT, HP, P])
        keysT = sb("keysT", 72, [P, HP, NKEY])
        qs = sb("qs", 80, [P, HP, P])
        S = sb("S", 88, [P, HP, NKEY])
        S2 = sb("S2", 96, [P, HP, NKEY])
        eq = sb("eq", 104, [P, PH, TOPK, TOPK])
        cand = sb("cand", 104, [P, 2, PH, NCAND])
        hot_hi = sb("hot_hi", 104, [P, P // 2, NHI])
        hot_lo = sb("hot_lo", 106, [P, P // 2, TOPK])
        Ahot = sb("Ahot", 112, [P, 2, TOK, P])
        Bhot = sb("Bhot", 120, [P, 2, TOK, P])
        topv = sb("topv", 128, [P, PH, 2, TOPK])
        topi = sb("topi", 129, [P, PH, 2, TOPK], U32)
        candv = sb("candv", 130, [P, PH, TOPK])
        candi = sb("candi", 130.5, [P, PH, TOPK], U32)
        shifted = sb("shifted", 131, [P, 2, PH, TOPK], U32)
        rank = sb("rank", 132, [P, 2, PH, TOPK])
        zsum = sb("zsum", 133, [P, 2, PH])
        key1 = sb("key1", 133.125, [P, PH, TOPK])
        pick = sb("pick", 200, [P, 4, PH, TOPK])
        pickT = sb("pickT", 198, [P, 4, P])
        key1u = sb("key1u", 202, [P, 3, PH, TOPK], U32)
        G_st = sb("G_st", 134, [P, NKEY, P])
        G_last = sb("G_last", 40, [P, NKEY, P])
        Uearly = [sb("Uearly0", 40, [P, KT, P]), sb("Uearly1", 44, [P, KT, P])]
        act_st = [sb("act_st0", 204, [P, T]), sb("act_st1", 48, [P, T])]
        Utail = [sb("Utail0", 144, [P, KT, P]), sb("Utail1", 148, [P, KT, P])]
        act_tail = [sb("act_tail0", 204, [P, T]), sb("act_tail1", 134, [P, T])]
        xhi = sb("xhi", 40, [P, KT, T], F32R)
        xlo = sb("xlo", 56, [P, KT, T], F32R)
        Uraw = sb("Uraw", 72, [P, 2, KT, 2 * P])
        Vraw = sb("Vraw", 88, [P, 2, 2, D])
        Uhi = sb("Uhi", 104, [P, 2, KT, 2 * P], F32R)
        Ulo = sb("Ulo", 120, [P, 2, KT, 2 * P], F32R)
        Vhi = sb("Vhi", 136, [P, 2, 2, D], F32R)
        Vlo = sb("Vlo", 152, [P, 2, 2, D], F32R)
        Gin = sb("Gin", 168, [P, 2, 2, T])
        act = sb("act", 176, [P, 2, T])
        act_odd = sb("act_odd", 200, [P, 2, T])
        Hf = sb("Hf", 180, [P, 2, T])
        Hhi = sb("Hhi", 184, [P, 2, 2, T], F32R)
        Hlo = sb("Hlo", 192, [P, 2, 2, T], F32R)

        G_dram = nc.dram_tensor("G_scratch", (DEPTH, NG, P, 2, TT, P), F32, kind="Internal").ap()
        act_dram = nc.dram_tensor("act_scratch", (DEPTH, EARLY, P, T), F32, kind="Internal").ap()
        ps = ctx.enter_context(nc.psum_tensor("ps", [P, 8, T], F32))

        def wide(pair):
            return ps[:, 2 * pair:2 * pair + 2, :].rearrange("p b n -> p (b n)")

        NIN, NOUT, NQ, NGI = 6, 2, 4, 4
        chunks = ([("attn_in", 0, c) for c in range(NIN)] + [("attn_out", 0, c) for c in range(NOUT)]
                  + [("query", 0, c) for c in range(NQ)] + [("gate_in", 0, c) for c in range(NGI)]
                  + [("gate_out", 0, c) for c in range(NOUT)] + [("query", 1, c) for c in range(NQ)])
        W_IN = 0
        W_OUT = NIN
        W_Q0 = W_OUT + NOUT
        W_GIN = W_Q0 + NQ
        W_GOUT = W_GIN + NGI
        W_Q = [W_Q0, W_GOUT + NOUT]
        NFIRST = 2 * D // CW
        NCH = DEPTH * NMOD
        slot_of, landed_by, before = [], [], []
        taken = [[] for _ in range(RING + 1)]
        for n, (kind, layer, c) in enumerate(chunks):
            k = c if kind == "query" else n % RING
            before.append(taken[k][-1] if taken[k] else None)
            taken[k].append(n)
            slot_of.append(k)
            landed_by.append(16 * len(taken[k]))
        slots = [ring[k] for k in slot_of]

        in_jobs = []

        def in_job(kind, c, width, dst, operands):
            rope = sum(job[0] == "rope" for job in in_jobs)
            in_jobs.append((kind, ps[:, len(in_jobs) % 4, 0:width], dst, rope, c, operands))

        def columns(c, f, x):
            slot = slots[W_IN + c]
            return lambda k: (slot[:, k, f * P:(f + 1) * P], x[:, k, :])

        def tokens(c, x, tt):
            slot = slots[W_IN + c]
            return lambda k: (x[:, k, tt * P:(tt + 1) * P], slot[:, k, :])

        for c, (name, dst) in enumerate((("rope", qaT), ("rope", kaT), ("v", va), ("copy", qbT), ("copy", kbT),
                                         ("v", vb))):
            if name == "v":
                for tt in range(TT):
                    in_job("copy", c, CW, dst[:, tt, :], tokens(c, xm, tt))
                for tt in range(TC // P):
                    in_job("copy", c, CW, dst[:, TT + tt, :], tokens(c, xc, tt))
                continue
            for f in range(4):
                in_job(name, c, T, dst[:, f, 0:T], columns(c, f, xm))
            if c in (1, 4):
                for f in range(4):
                    in_job("copy", c, TC, dst[:, f, T:TK], columns(c, f, xc))

        consts_in = sem("consts_in")
        x_in = sem("x_in")
        w_in = [sem(f"w_in{n}") for n in range(RING + 1)]
        mod_mm = sem("mod_mm")
        mod_in = [sem(f"mod_in{n}") for n in range(3)]
        mod_read = sem("mod_read")
        macc_ready = sem("macc_ready")
        cond_ready = sem("cond_ready")
        mod_ready = sem("mod_ready")
        dve_step = sem("dve_step")
        lam_sum = sem("lam_sum")
        lam_exp = sem("lam_exp")
        lam_ready = sem("lam_ready")
        sq_ready = sem("sq_ready")
        sq_used = sem("sq_used")
        ms_ready = sem("ms_ready")
        rms_ready = sem("rms_ready")
        oms_ready = sem("oms_ready")
        orms_ready = sem("orms_ready")
        var_ready = sem("var_ready")
        std_ready = sem("std_ready")
        rinv_ready = sem("rinv_ready")
        x_scaled = sem("x_scaled")
        x_ready = sem("x_ready")
        proj_mm = sem("proj_mm")
        proj_out = sem("proj_out")
        rope_raw = sem("rope_raw")
        rope_mm = sem("rope_mm")
        rope_out = sem("rope_out")
        bias_in = [sem(f"bias_in{n}") for n in range(2)]
        score_mm = sem("score_mm")
        nmax_ready = sem("nmax_ready")
        exp_done = sem("exp_done")
        probs_ready = sem("probs_ready")
        probsT_mm = sem("probsT_mm")
        probsT_ready = sem("probsT_ready")
        av_mm = sem("av_mm")
        o_out = sem("o_out")
        osq_ready = sem("osq_ready")
        osum_mm = sem("osum_mm")
        o_normed = sem("o_normed")
        h_mm = sem("h_mm")
        h_added = sem("h_added")
        q_mm = sem("q_mm")
        q_out = sem("q_out")
        keys_in = sem("keys_in")
        qs_ready = sem("qs_ready")
        score_done = sem("score_done")
        S_ready = sem("S_ready")
        gate_logits = sem("gate_logits")
        gate_exp = sem("gate_exp")
        pick_ready = sem("pick_ready")
        pickT_out = sem("pickT_out")
        route_step = sem("route_step")
        S_free = sem("S_free")
        bias_used = sem("bias_used")
        near_read = sem("near_read")
        H_step = sem("H_step")
        pickT_mm = sem("pickT_mm")
        hot_step = sem("hot_step")
        hot_ready = sem("hot_ready")
        G_mm = sem("G_mm")
        G_out = sem("G_out")
        G_stored = sem("G_stored")
        early_in = [sem(f"early_in{n}") for n in range(2)]
        early_mm = sem("early_mm")
        early_act = sem("early_act")
        early_stored = [sem(f"early_stored{n}") for n in range(2)]
        act_in = [sem(f"act_in{n}") for n in range(2)]
        x_hi = sem("x_hi")
        x_split = sem("x_split")
        U_in = [sem(f"U_in{n}") for n in range(2)]
        V_in = [sem(f"V_in{n}") for n in range(2)]
        G_in = [sem(f"G_in{n}") for n in range(2)]
        U_hi = sem("U_hi")
        U_split = sem("U_split")
        V_hi = sem("V_hi")
        V_split = sem("V_split")
        up_mm = sem("up_mm")
        act_ready = sem("act_ready")
        H_ready = sem("H_ready")
        dn_mm = sem("dn_mm")
        dn_added = sem("dn_added")
        gl_in = sem("gl_in")
        v_mm = sem("v_mm")
        v_gelu = sem("v_gelu")
        v_normed = sem("v_normed")
        u_mm = sem("u_mm")
        u_gelu = sem("u_gelu")
        sv_mm = sem("sv_mm")
        y_ready = sem("y_ready")
        stored = sem("stored")

        NH1 = 2 * NFIRST
        mslot = [m % 2 if m < NH1 else m % 3 for m in range(2 * NCH)]
        mbefore = [max([w for w in range(m) if mslot[w] == mslot[m]], default=None) for m in range(2 * NCH)]
        mlanded = [16 * (1 + sum(mslot[w] == mslot[m] for w in range(m))) for m in range(2 * NCH)]
        MOD_AT = [1 + i * (len(in_jobs) - 5) // (NCH - NFIRST) for i in range(NCH - NFIRST)]

        PER = BESIDE + AFTER
        SLOT_LOADS = [BESIDE * (TT - 1) + AFTER // 2 * (TT - 2) + TAIL // 2, AFTER // 2 * (TT - 2) + TAIL // 2]

        def early_beside(layer, r, i):
            return r * PER + (i + layer * EARLY), 0, r * (BESIDE + AFTER // 2) + (i + layer * SLOT_LOADS[0])

        def early_after(layer, r, e):
            slot = (e + 1) % 2
            loads = (r * (AFTER // 2) + e // 2 + layer * SLOT_LOADS[1] if slot else
                     r * (BESIDE + AFTER // 2) + (BESIDE + e // 2 + layer * SLOT_LOADS[0]))
            return r * PER + (BESIDE + e + layer * EARLY), slot, loads

        units = []
        for h in range(HA):
            for qt in range(TT):
                units.append(("diff", h, qt))
        for h in range(HB):
            for qt in range(TT):
                units.append(("near", h, qt))
        job_of = []
        njobs = 0
        for kind, h, qt in units:
            job_of.append(njobs)
            njobs += 2 if kind == "diff" else 1
        HEAD_END = HA * TT
        sh1, sc1, g1, sh2, sc2, g2 = [KT * n for n in range(6)]
        NORMS = [(ctxT, TC, xc, 0, sh1, sc1, 1), (hT, T, xm, 0, sh1, sc1, 0), (hT, T, xm, 0, sh2, sc2, 0),
                 (hT, T, xm, 1, sh1, sc1, 0), (hT, T, xm, 1, sh2, sc2, 0), (hT, T, xm, None, None, None, 0)]
        n_mixer = [KT, 2 * KT]
        n_peer = [KT * NG, 2 * KT * NG]

        def chunk_used(n):
            kind, layer, c = chunks[n]
            if kind == "attn_in":
                return proj_mm, sum(job[4] <= c for job in in_jobs)
            if kind == "attn_out":
                return h_mm, 4 * (c + 1)
            if kind == "gate_out":
                return h_mm, KT + 4 * (c + 1)
            if kind == "query":
                return q_mm, (layer * TT + TT - 1) * HP + 4 * (c + 1)
            return (v_mm, TT * (c + 1)) if c < 2 else (u_mm, 4 * (c - 1))

        block = ctx.enter_context(nc.Block())

        @block.sync
        def _(sp):
            sp.sem_inc(G_stored, 64)
            sp.dma_start(cond[:, :, :], a["cond"]).then_inc(consts_in, 16)
            sp.dma_start(bmod[:, :, :], a["b_mod"]).then_inc(consts_in, 16)

            def load_chunk(n):
                if before[n] is not None:
                    sp.wait_ge(*chunk_used(before[n]))
                kind, layer, c = chunks[n]
                sp.dma_start(slots[n][:, :, :],
                             a[kind][layer].rearrange("(k p) n -> p k n", p=P)[:, :, c * CW:(c + 1) * CW]
                             ).then_inc(w_in[slot_of[n]], 16)

            sp.dma_start(hT[:, :, :], a["xT"].rearrange("(k p) t -> p k t", p=P)).then_inc(x_in, 16)
            sp.dma_start(ctxT[:, :, :], a["ctxT"].rearrange("(k p) t -> p k t", p=P)).then_inc(x_in, 16)
            for dst, name in ((ones, "ones"), (ident, "ident"), (iota, "iota"), (iota16, "iota16"), (iota8, "iota8"),
                              (fing, "final_g"), (bu, "bu"), (cosT, "cosT"), (sinT, "sinT"), (rot, "rot"),
                              (mask, "mask"), (sublg, "subln_g"), (lamin, "lam"), (ones_row, "ones_row")):
                sp.dma_start(dst[tuple(slice(None) for _ in dst.shape)], a[name]).then_inc(x_in, 16)
            def load_mod_half(m):
                if mbefore[m] is not None:
                    sp.wait_ge(mod_read, mbefore[m] + 1)
                if m >= NH1 and mslot[m] == 2 and mbefore[m] is None:
                    sp.wait_ge(x_scaled, KT)
                layer, c, half = m // (2 * NMOD), m // 2 % NMOD, m % 2
                sp.dma_start(modw[mslot[m]][:, :, :],
                             a["w_mod"][layer].rearrange("(k p) n -> p k n", p=P)[
                                 :, half * KT // 2:(half + 1) * KT // 2, c * CW:(c + 1) * CW]
                             ).then_inc(mod_in[mslot[m]], 16)

            for m in range(NH1):
                load_mod_half(m)
            events = [(-1 if before[n] is None else chunk_used(before[n])[1], "chunk", n) for n in range(NIN)]
            events += [(0 if mbefore[m] < NH1 else MOD_AT[mbefore[m] // 2 - NFIRST] + 1, "half", m)
                       for m in range(NH1, 2 * NCH) if mbefore[m] is not None]
            events += [(0, "half", m) for m in range(NH1, 2 * NCH) if mbefore[m] is None]
            for _, what, n in sorted(events):
                (load_chunk if what == "chunk" else load_mod_half)(n)
            for n in range(W_OUT, W_OUT + NOUT):
                load_chunk(n)
            for h in range(HB):
                if h < 2:
                    sp.wait_ge(proj_mm, len(in_jobs))
                else:
                    sp.wait_ge(bias_used, h - 1)
                sp.dma_start(btab[:, h % 2, :, :], a["btab"][h]).then_inc(bias_in[h % 2], 16)
            for n in range(W_Q0, W_GIN):
                if slot_of[n] == RING:
                    sp.wait_ge(h_mm, 1)
                load_chunk(n)

            def peer_loads(layer):
                sp.wait_ge(h_added, n_mixer[layer])
                sp.dma_start(keysT[:, :, :], a["keysT"][layer]).then_inc(keys_in, 16)

                def load_early(job, r, i, before, dst=Uearly):
                    m, slot, loads = job
                    sp.wait_ge(early_mm, m + (2 - before))
                    sp.dma_start(dst[slot][:, :, :],
                                 a["UT"][layer][bass.ds(r * (PER // 2) + i // 2, 1), :, :,
                                                i % 2 * P:(i % 2 + 1) * P].rearrange("o p k e -> p (o k) e")
                                 ).then_inc(early_in[slot], 16)

                def load_beside(r, i):
                    load_early(early_beside(layer, r, i), r, i, 0)

                def load_after(r, e, dst=Uearly):
                    load_early(early_after(layer, r, e), r, BESIDE + e, 1, dst)

                def store_gates(r, src, piece):
                    if piece == 0:
                        sp.wait_ge(G_out, (r + (layer * TT + 1)) * (P // 4) + 4)
                    j, half = piece % 2, piece // 2
                    gs = slice(half * NG // 2, (half + 1) * NG // 2)
                    sp.dma_start(G_dram[layer, gs, :, j, bass.ds(r, 1), :].rearrange("g p r t -> p g (r t)"),
                                 src[:, :, :].rearrange("p (g j) t -> p g j t", j=2)[:, gs, j, :]
                                 ).then_inc(G_stored, 16)

                sp.wait_ge(qs_ready, layer * TT + 2)
                with sp.Fori(0, TT - 2) as r:
                    load_beside(r, 0)
                    load_after(r, 0)
                    load_beside(r, 1)
                    load_after(r, 1)
                    for piece in range(4):
                        store_gates(r, G_st, piece)
                        if 2 + piece < AFTER:
                            load_after(r, 2 + piece)
                load_beside(TT - 2, 0)
                load_beside(TT - 2, 1)
                for piece in range(4):
                    store_gates(TT - 2, G_st, piece)
                sp.wait_ge(G_stored, 64 * (TT * (layer + 1)))
                load_after(TT - 2, 0, Utail)
                load_after(TT - 2, 1, Utail)
                store_gates(TT - 1, G_last, 0)
                for piece in range(1, 4):
                    store_gates(TT - 1, G_last, piece)
                    load_after(TT - 2, 1 + piece, Utail)
                load_after(TT - 2, 5, Utail)
                sp.wait_ge(G_stored, 64 * (TT * (layer + 1) + 1))

                def load_group(g, par, early):
                    n = g + layer * NG
                    if early:
                        at_least(sp, H_ready, (n - 1) * 2)
                        sp.dma_start((act_odd if par else act)[:, :, :],
                                     act_dram[layer, bass.ds(g * 2, 2)].rearrange("j p t -> p j t")
                                     ).then_inc(act_in[par], 16)
                    else:
                        at_least(sp, U_split, g + (layer * (NG - EG) - EG - 1))
                        sp.dma_start(Uraw[:, par, :, :], a["UT"][layer][bass.ds(g, 1)].rearrange("o p k e -> p (o k) e")
                                     ).then_inc(U_in[par], 16)
                    at_least(sp, V_split, n - 1)
                    sp.dma_start(Vraw[:, par, :, :], a["V"][layer][bass.ds(g, 1)].rearrange("o j p d -> p (o j) d")
                                 ).then_inc(V_in[par], 16)
                    at_least(sp, H_ready, (n - 1) * 2)
                    sp.dma_start(Gin[:, par, :, :], G_dram[layer][bass.ds(g, 1)].rearrange("o p j r t -> p (o j) (r t)")
                                 ).then_inc(G_in[par], 16)

                for slot in range(2):
                    sp.wait_ge(early_stored[slot], 16 * (1 + SLOT_LOADS[slot] * (layer + 1) - TAIL // 2))
                for g in range(2):
                    load_group(g, g, True)
                for slot in range(2):
                    sp.wait_ge(early_stored[slot], 16 * (1 + SLOT_LOADS[slot] * (layer + 1)))
                with sp.Fori(1, EG // 2) as it:
                    for par in range(2):
                        load_group(it * 2 + par, par, True)
                for g in range(EG, EG + 2):
                    load_group(g, g % 2, False)
                with sp.Fori(EG // 2 + 1, NG // 2) as it:
                    for par in range(2):
                        load_group(it * 2 + par, par, False)

            peer_loads(0)
            sp.wait_ge(h_added, n_mixer[0])
            sp.wait_ge(dn_added, n_peer[0])
            for n in range(W_GIN, W_GIN + RING):
                load_chunk(n)
            for dst, name in ((lng, "ln_g"), (lnb, "ln_b"), (bsb, "b_s")):
                sp.dma_start(dst[tuple(slice(None) for _ in dst.shape)],
                             a[name].partition_broadcast(P)).then_inc(gl_in, 16)
            sp.dma_start(wsT[:, :, :], a["w_sT"]).then_inc(gl_in, 16)
            sp.dma_start(bvrow[:, :], a["bv"]).then_inc(gl_in, 16)
            for n in range(W_GIN + RING, len(chunks)):
                load_chunk(n)
            peer_loads(1)
            for k in range(KT):
                sp.wait_ge(x_scaled, 5 * KT + k + 1)
                sp.dma_start(out[k * P:(k + 1) * P, :], xm[:, k, :]).then_inc(stored, 16)
            sp.wait_ge(stored, 16 * KT)

        @block.scalar
        def _(act_e):
            act_e.sem_inc(G_out, 4)
            act_e.sem_inc(early_act, 2)
            for slot in range(2):
                act_e.sem_inc(early_stored[slot], 16)
            act_e.wait_ge(consts_in, 32)
            nc.scalar.activation(condS[:, :, :], cond[:, :, :], ACT.Silu).then_inc(cond_ready, 1)
            act_e.wait_ge(x_in, 16 * 16)

            def norm(n):
                src, width, dst, layer, sh, sc, who = NORMS[n]
                for k in range(KT):
                    if n >= 2:
                        added, count = ((h_added, n_mixer[0]), (dn_added, n_peer[0]),
                                        (h_added, n_mixer[1]), (dn_added, n_peer[1]))[n - 2]
                        act_e.wait_ge(added, count - KT + k + 1)
                    at_least(act_e, sq_used, n * KT + k - 1)
                    nc.scalar.activation(sq[:, k % 2, 0:width], src[:, k, :], ACT.Square).then_inc(sq_ready, 1)
                act_e.wait_ge(ms_ready, n + 1)
                nc.scalar.activation(rms[:, 0:width], rms[:, 0:width], ACT.Sqrt).then_inc(rms_ready, 1)
                if sh is None:
                    return
                for k in range(KT):
                    act_e.wait_ge(x_scaled, n * KT + k + 1)
                    nc.scalar.activation(dst[:, k, :], dst[:, k, :], ACT.Identity,
                                         bias=mods[:, layer, sh + k, who:who + 1]).then_inc(x_ready, 1)

            act_e.wait_ge(mod_ready, 1)
            norm(0)
            norm(1)

            for j, (kind, bank, dst, rope, _, _) in enumerate(in_jobs):
                act_e.wait_ge(proj_mm, j + 1)
                if kind == "copy":
                    nc.scalar.copy(dst, bank).then_inc(proj_out, 1)
                else:
                    at_least(act_e, rope_out, rope - 1)
                    nc.scalar.copy(ropein[:, rope % 2, :], bank).then_inc(rope_raw, 1)
            act_e.wait_ge(lam_sum, 1)
            nc.scalar.activation(lamv[:, 2:4], lamv[:, 0:2], ACT.Exp).then_inc(lam_exp, 1)

            def evac_probsT(u):
                act_e.wait_ge(probsT_mm, u + 1)
                at_least(act_e, av_mm, u - 1)
                nc.scalar.copy(ATbuf[:, u % 2, :], wide(2)[:, 0:TK]).then_inc(probsT_ready, 1)

            def finish(u):
                evac_probsT(u)
                kind, h, qt = units[u]
                if kind == "diff" and qt == TT - 1:
                    act_e.wait_ge(oms_ready, h + 1)
                    nc.scalar.activation(osq[:, :], osq[:, :], ACT.Sqrt).then_inc(orms_ready, 1)

            for u, (kind, h, qt) in enumerate(units):
                j = job_of[u]
                for m in range(2 if kind == "diff" else 1):
                    act_e.wait_ge(nmax_ready, j + m + 1)
                    first_over = [w for w in range(u) if job_of[w] <= j + m - 4]
                    if first_over:
                        act_e.wait_ge(probs_ready, first_over[-1] + 1)
                    src = wide((j + m) % 2)[:, 0:TK] if kind == "diff" else Sbuf[:, (j + m) % 2, :]
                    nc.scalar.activation(Ebuf[:, (j + m) % 4, :], src, ACT.Exp, bias=nmx[:, j + m:j + m + 1],
                                         scale=QK_SCALE if kind == "diff" else 1.0,
                                         accum_out=zs[:, j + m:j + m + 1]).then_inc(exp_done, 1)
                if u >= 2:
                    finish(u - 2)
            finish(len(units) - 2)
            finish(len(units) - 1)

            def peer_route(layer):
                def queries(r, n0, n1):
                    for n in range(n0, n1):
                        act_e.wait_ge(q_mm, (layer * TT + r) * HP + n + 1)
                        nc.scalar.copy(qT[:, r, n, :], ps[:, n % 4, 0:P]).then_inc(q_out, 1)

                def stage_queries(r):
                    at_least(act_e, score_done, r + layer * TT)
                    nc.scalar.copy(qs[:, :, :], qT[:, bass.ds(r, 1), :, :].rearrange("p o n t -> p (o n) t")
                                   ).then_inc(qs_ready, 1)

                def read_scores(r):
                    tile = r + layer * TT
                    act_e.wait_ge(score_done, tile + 1)
                    at_least(act_e, S_free, tile)
                    for b in range(4):
                        nc.scalar.copy(S[:, 4 * b:4 * b + 4, :].rearrange("p a n -> p (a n)"), ps[:, 4 + b, :]
                                       ).then_inc(S_ready, 1)

                def gate_exps(r):
                    act_e.wait_ge(gate_logits, r + layer * TT + 1)
                    nc.scalar.activation(pick[:, 3, :, :], pick[:, 3, :, :], ACT.Exp).then_inc(gate_exp, 1)

                def early_gelu(job, tile, dst=act_st):
                    m, slot, loads = job
                    act_e.wait_ge(early_mm, m + 3)
                    act_e.wait_ge(early_stored[slot], loads * 16 + 16)
                    nc.scalar.activation(dst[slot][:, :], ps[:, 4 + slot, :], ACT.Gelu_apprx_tanh
                                         ).then_inc(early_act, 1)
                    act_e.wait_ge(early_act, m + 3)
                    act_e.dma_start(act_dram[layer, bass.ds(tile, 1)].rearrange("o p t -> p (o t)"), dst[slot][:, :]
                                    ).then_inc(early_stored[slot], 16)

                def gelus_after(r, e0, e1, dst=act_st):
                    for e in range(e0, e1):
                        early_gelu(early_after(layer, r, e), r * PER + (BESIDE + e), dst)

                def gate_weights(r, dst=G_st, beside=True):
                    tile = r + layer * TT
                    if dst is G_st:
                        act_e.wait_ge(G_stored, (tile + 1) * 64)
                    else:
                        act_e.wait_ge(early_stored[1], 16 * (1 + SLOT_LOADS[1] * (layer + 1) - TAIL // 2))
                    with act_e.Fori(0, BESIDE) as it:
                        for q in range(NB // BESIDE):
                            for b in range(2):
                                act_e.wait_ge(G_mm, (tile * NB + it * (NB // BESIDE) + q) * 2 + b + 5)
                                nc.scalar.copy(
                                    dst[:, :, bass.ds((it * (NB // BESIDE) + q) * TOK + 4 * b, 4)
                                        ].rearrange("p i t -> p t i"),
                                    ps[:, 2 * (q % 2) + b, :].rearrange("p (t i) -> p t i", t=4)).then_inc(G_out, 1)
                        if beside:
                            early_gelu(early_beside(layer, r, it), r * PER + it)

                queries(0, 0, HP)
                act_e.wait_ge(q_out, (layer * TT + 1) * HP)
                stage_queries(0)
                read_scores(0)
                queries(1, 0, HP)
                act_e.wait_ge(q_out, (layer * TT + 2) * HP)
                stage_queries(1)
                read_scores(1)
                queries(2, 0, HP // 2)
                gate_exps(0)
                queries(2, HP // 2, HP)
                queries(3, 0, HP)
                act_e.wait_ge(q_out, (layer * TT + 4) * HP)
                gate_exps(1)
                with act_e.Fori(0, TT - 2) as r:
                    stage_queries(r + 2)
                    read_scores(r + 2)
                    gate_weights(r)
                    gelus_after(r, 0, 3)
                    gate_exps(r + 2)
                    gelus_after(r, 3, AFTER)
                gate_weights(TT - 2)
                gate_weights(TT - 1, G_last, beside=False)
                gelus_after(TT - 2, 0, 4, act_tail)
                return lambda: gelus_after(TT - 2, 4, TAIL, act_tail)

            def peer_dense(layer, last_early_gelus):
                act_e.wait_ge(G_stored, 64 * ((layer + 1) * TT + 1))

                def split_U(g, par, it):
                    n = g + (layer * (NG - EG) - EG)
                    act_e.wait_ge(U_in[par], (it + (layer * (NG - EG) // 2 - EG // 2 + 1)) * 16)
                    at_least(act_e, up_mm, (n - 1) * 2)
                    nc.scalar.copy(Uhi[:, par, :, :], Uraw[:, par, :, :]).then_inc(U_hi, 1)

                def split_V(g, par, it):
                    n = g + layer * NG
                    act_e.wait_ge(V_in[par], (it + (layer * (NG // 2) + 1)) * 16)
                    at_least(act_e, dn_mm, (n - 1) * KT)
                    nc.scalar.copy(Vhi[:, par, :, :], Vraw[:, par, :, :]).then_inc(V_hi, 1)

                def gelus(g, j):
                    n = (g + layer * NG) * 2 + j
                    act_e.wait_ge(up_mm, n + (layer * (NG - EG) - EG - layer * NG) * 2 + 1)
                    at_least(act_e, H_ready, n - 1)
                    nc.scalar.activation(act[:, j, :], ps[:, j, :], ACT.Gelu_apprx_tanh).then_inc(act_ready, 1)

                def period(g, par, it, last=False):
                    if not last:
                        split_U(g + 1, 1 - par, it + par)
                    split_V(g, par, it)
                    gelus(g, 0)
                    gelus(g, 1)

                split_V(0, 0, 0)
                last_early_gelus()
                split_V(1, 1, 0)
                for k in range(KT):
                    nc.scalar.copy(xhi[:, k, :], xm[:, k, :]).then_inc(x_hi, 1)
                with act_e.Fori(1, EG // 2 - 1) as it:
                    for par in range(2):
                        split_V(it * 2 + par, par, it)
                split_V(EG - 2, 0, EG // 2 - 1)
                split_U(EG, 0, EG // 2)
                split_V(EG - 1, 1, EG // 2 - 1)
                period(EG, 0, EG // 2)
                period(EG + 1, 1, EG // 2)
                with act_e.Fori(EG // 2 + 1, NG // 2 - 1) as it:
                    for par in range(2):
                        period(it * 2 + par, par, it)
                period(NG - 2, 0, NG // 2 - 1)
                period(NG - 1, 1, NG // 2 - 1, last=True)

            norm(2)
            peer_dense(0, peer_route(0))
            norm(3)
            for c in range(2):
                for tt in range(TT):
                    act_e.wait_ge(v_mm, c * TT + tt + 1)
                    nc.scalar.activation(vsb[:, tt, c * CW:(c + 1) * CW], ps[:, (c * TT + tt) % 4, :],
                                         ACT.Gelu_apprx_tanh).then_inc(v_gelu, 1)
            act_e.wait_ge(var_ready, 1)
            nc.scalar.activation(rstd[:, 0, :], rstd[:, 0, :], ACT.Sqrt).then_inc(std_ready, 1)
            for f in range(KT):
                act_e.wait_ge(u_mm, f + 1)
                nc.scalar.activation(uT[:, f, :], ps[:, f % 4, :], ACT.Gelu_apprx_tanh,
                                     bias=bu[:, f:f + 1]).then_inc(u_gelu, 1)
            norm(4)
            peer_dense(1, peer_route(1))
            norm(5)

        @block.tensor
        def _(pe):
            def chunk_landed(n):
                pe.wait_ge(w_in[slot_of[n]], landed_by[n])

            def modulation(i):
                pe.wait_ge(macc_ready, i + 1)
                if i == NFIRST:
                    pe.wait_ge(mod_ready, 1)
                for j in range(4):
                    for who, acc in enumerate((macc, maccx) if i < NFIRST else (macc,)):
                        col = (4 * i + j) * 2 + who
                        mm = nc.tensor.matmul(ps[:, 7, col:col + 1], acc[:, i % 2, j * P:(j + 1) * P],
                                              ones[:, 0:1], start=True, stop=True)
                mm.then_inc(mod_mm, 1)

            pe.sem_inc(G_mm, 4)
            pe.sem_inc(early_mm, 2)
            pe.wait_ge(x_in, 16 * 16)
            for i in range(NFIRST):
                modulation(i)

            def norm(n):
                width = NORMS[n][1]
                for k in range(KT):
                    pe.wait_ge(sq_ready, n * KT + k + 1)
                    nc.tensor.matmul(ps[:, 6, 0:width], ones[:, :], sq[:, k % 2, 0:width],
                                     start=(k == 0), stop=(k == KT - 1)).then_inc(sq_used, 1)

            norm(0)
            pe.wait_ge(rinv_ready, 1)
            norm(1)

            pe.wait_ge(rinv_ready, 2)
            pe.wait_ge(x_ready, 2 * KT)
            def rotate(rope):
                pe.wait_ge(rope_raw, rope + 1)
                at_least(pe, rope_out, rope - 1)
                nc.tensor.matmul(ps[:, 4 + rope % 2, :], rot[:, :], ropein[:, rope % 2, :],
                                 start=True, stop=True).then_inc(rope_mm, 1)

            for j, (kind, bank, _, rope, c, operands) in enumerate(in_jobs):
                n = W_IN + c
                chunk_landed(n)
                if j >= 4:
                    before = in_jobs[j - 4]
                    if before[0] == "rope":
                        pe.wait_ge(rope_raw, before[3] + 1)
                    else:
                        pe.wait_ge(proj_out, j - 3 - before[3])
                for k in range(KT):
                    w, x = operands(k)
                    mm = nc.tensor.matmul(bank, w, x, start=(k == 0), stop=(k == KT - 1))
                mm.then_inc(proj_mm, 1)
                if j >= 1 and in_jobs[j - 1][0] == "rope":
                    rotate(in_jobs[j - 1][3])
                for i, at in enumerate(MOD_AT):
                    if at == j - 2:
                        modulation(NFIRST + i)

            pe.wait_ge(proj_out, sum(job[0] == "copy" for job in in_jobs))
            pe.wait_ge(rope_out, 2 * HA)

            def scores(u):
                kind, h, qt = units[u]
                for m in range(2 if kind == "diff" else 1):
                    j = job_of[u] + m
                    if j - 2 < 2 * HEAD_END:
                        at_least(pe, exp_done, j - 1)
                    else:
                        pe.wait_ge(near_read, j - 1 - 2 * HEAD_END)
                    if kind == "diff":
                        q, kx, f, lo = qaT, kaT, h, DH * m
                    else:
                        q, kx, f, lo = qbT, kbT, h // 2, DH * (h % 2)
                    for c0, c1 in ((0, T), (T, TK)):
                        mm = nc.tensor.matmul(wide(j % 2)[:, c0:c1], q[lo:lo + DH, f, qt * P:(qt + 1) * P],
                                              kx[lo:lo + DH, f, c0:c1], start=True, stop=True)
                    mm.then_inc(score_mm, 1)

            def av(u):
                kind, h, qt = units[u]
                pe.wait_ge(probsT_ready, u + 1)
                at_least(pe, o_out, u)
                for kt in range(KK):
                    if kind == "diff":
                        dst, v = ps[:, 6, qt * P:(qt + 1) * P], va[:, kt, h * P:(h + 1) * P]
                    else:
                        lo = DH * (h % 2)
                        dst, v = ps[lo:lo + DH, 6, qt * P:(qt + 1) * P], vb[:, kt, h * DH:(h + 1) * DH]
                    mm = nc.tensor.matmul(dst, v, ATbuf[:, u % 2, kt * P:(kt + 1) * P],
                                          start=(kt == 0), stop=(kt == KK - 1))
                mm.then_inc(av_mm, 1)
                if kind == "diff" and qt == TT - 1:
                    pe.wait_ge(osq_ready, h + 1)
                    nc.tensor.matmul(ps[:, 6, :], ones[:, :], osq[:, :], start=True, stop=True).then_inc(osum_mm, 1)
                    pe.wait_ge(oms_ready, h + 1)

            scores(0)
            for u in range(len(units) + 2):
                if u + 1 < len(units):
                    scores(u + 1)
                if 1 <= u <= len(units):
                    pe.wait_ge(probs_ready, u)
                    at_least(pe, probsT_ready, u - 1)
                    for kt in range(KK):
                        mm = nc.tensor.transpose(wide(2)[:, kt * P:(kt + 1) * P],
                                                 Abuf[:, (u - 1) % 2, kt * P:(kt + 1) * P], ident[:, :])
                    mm.then_inc(probsT_mm, 1)
                if u >= 2:
                    av(u - 2)
            pe.wait_ge(o_out, len(units))
            pe.wait_ge(o_normed, HA)

            def out_projection(w0, src, done):
                for f in range(KT):
                    n = w0 + f // 4
                    if f % 4 == 0:
                        chunk_landed(n)
                    at_least(pe, h_added, done + f - 3)
                    for k in range(KT):
                        mm = nc.tensor.matmul(ps[:, f % 4, :], slots[n][:, k, (f % 4) * P:(f % 4 + 1) * P],
                                              src[:, k, :], start=(k == 0), stop=(k == KT - 1))
                    mm.then_inc(h_mm, 1)

            def peer_route(layer):
                def queries(r):
                    for n in range(HP):
                        w = W_Q[layer] + n // 4
                        i = (layer * TT + r) * HP + n
                        if r == 0 and n % 4 == 0:
                            chunk_landed(w)
                        at_least(pe, q_out, i - 3)
                        for k in range(KT):
                            if r == 0 and n == 0:
                                pe.wait_ge(x_ready, (2 * layer + 2) * KT + k + 1)
                            mm = nc.tensor.matmul(ps[:, n % 4, 0:P], slots[w][:, k, (n % 4) * P:(n % 4 + 1) * P],
                                                  xm[:, k, r * P:(r + 1) * P], start=(k == 0), stop=(k == KT - 1))
                        mm.then_inc(q_mm, 1)

                def key_scores(r):
                    tile = r + layer * TT
                    pe.wait_ge(qs_ready, tile + 1)
                    at_least(pe, S_ready, tile * 4)
                    for n in range(HP):
                        mm = nc.tensor.matmul(ps[:, 4 + n // 4, (n % 4) * P:(n % 4 + 1) * P], qs[:, n, :],
                                              keysT[:, n, :], start=True, stop=True)
                    mm.then_inc(score_done, 1)

                def turn_picks(r):
                    tile = r + layer * TT
                    pe.wait_ge(pick_ready, tile + 1)
                    pe.wait_ge(G_out, tile * (P // 4) + 4)
                    for n in range(4):
                        mm = nc.tensor.transpose(ps[:, 0, n * P:(n + 1) * P],
                                                 pick[:, n, :, :].rearrange("p h k -> p (h k)"), ident[:, :])
                    mm.then_inc(pickT_mm, 1)

                def early_start(job, before):
                    m, slot, loads = job
                    pe.wait_ge(early_in[slot], loads * 16 + 16)
                    pe.wait_ge(early_act, m + (2 - before))

                def early_product(slot, k, src=Uearly):
                    mm = nc.tensor.matmul(ps[:, 4 + slot, :], src[slot][:, k, :], xm[:, k, :],
                                          start=(k == 0), stop=(k == KT - 1))
                    if k == KT - 1:
                        mm.then_inc(early_mm, 1)

                def early_ups(r, count, src=Uearly):
                    for e in range(count):
                        job = early_after(layer, r, e)
                        early_start(job, 1)
                        for k in range(KT):
                            early_product(job[1], k, src)

                AMONG = [[], [], [0], [1], [2], [3], [4, 5], [6, 7]]

                def gate_weights(r, beside=True):
                    tile = r + layer * TT
                    with pe.Fori(0, BESIDE) as it:
                        for q in range(NB // BESIDE):
                            par = q % 2
                            n = tile * NB + it * (NB // BESIDE) + q
                            pe.wait_ge(hot_ready, n + 1)
                            for t in range(TOK):
                                if t % 4 == 0:
                                    pe.wait_ge(G_out, n * 2 + (t // 4 + 1))
                                mm = nc.tensor.matmul(ps[:, 2 * par + t // 4, (t % 4) * P:(t % 4 + 1) * P],
                                                      Bhot[:, par, t, :], Ahot[:, par, t, :], start=True, stop=True)
                                if t % 4 == 3:
                                    mm.then_inc(G_mm, 1)
                            for k in AMONG[q] if beside else ():
                                if k == 0:
                                    pe.wait_ge(S_ready, (r + (layer * TT + 2)) * 4)
                                    early_start(early_beside(layer, r, it), 0)
                                early_product(0, k)

                pe.wait_ge(keys_in, 16 * (layer + 1))
                queries(0)
                key_scores(0)
                queries(1)
                key_scores(1)
                queries(2)
                queries(3)
                pe.wait_ge(q_out, (layer + 1) * TT * HP)
                turn_picks(0)
                with pe.Fori(0, TT - 2) as r:
                    key_scores(r + 2)
                    gate_weights(r)
                    turn_picks(r + 1)
                    early_ups(r, AFTER)
                gate_weights(TT - 2)
                turn_picks(TT - 1)
                gate_weights(TT - 1, beside=False)
                early_ups(TT - 2, TAIL, Utail)

            def peer_dense(layer):
                pe.wait_ge(G_out, (layer + 1) * TT * (P // 4) + 4)
                pe.wait_ge(early_act, (layer + 1) * EARLY + 2)

                def up(g, par):
                    n = g + (layer * (NG - EG) - EG)
                    pe.wait_ge(U_split, n + 1)
                    for j in range(2):
                        at_least(pe, act_ready, n * 2 + (j - 1))
                        for k in range(KT):
                            cols = slice(j * P, (j + 1) * P)
                            for i, (w, x) in enumerate(((Uhi, xhi), (Uhi, xlo), (Ulo, xhi))):
                                mm = nc.tensor.matmul(ps[:, j, :], w[:, par, k, cols], x[:, k, :],
                                                      start=(k == 0 and i == 0), stop=(k == KT - 1 and i == 2))
                        mm.then_inc(up_mm, 1)

                def down(g, par, early=False):
                    n = g + layer * NG
                    pe.wait_ge(V_split, n + 1)
                    pe.wait_ge(H_ready, n * 2 + 2)
                    for d in range(KT):
                        bank = d if early else 2 + d % 4
                        at_least(pe, dn_added, n * KT + (d - 7 if early else d - 3))
                        cols = slice(d * P, (d + 1) * P)
                        for j in range(2):
                            for i, (w, x) in enumerate(((Vhi, Hhi), (Vhi, Hlo), (Vlo, Hhi))):
                                mm = nc.tensor.matmul(ps[:, bank, :], w[:, par, j, cols], x[:, par, j, :],
                                                      start=(j == 0 and i == 0), stop=(j == 1 and i == 2))
                        mm.then_inc(dn_mm, 1)

                down(0, 0, True)
                with pe.Fori(0, EG // 2 - 1) as it:
                    down(it * 2 + 1, 1, True)
                    down(it * 2 + 2, 0, True)
                pe.wait_ge(x_split, (layer + 1) * KT)
                pe.wait_ge(dn_added, (layer * NG + EG - 2) * KT + 2)
                up(EG, 0)
                down(EG - 1, 1)
                up(EG + 1, 1)
                down(EG, 0)
                with pe.Fori(EG // 2 + 1, NG // 2) as it:
                    for par in range(2):
                        up(it * 2 + par, par)
                        down(it * 2 + (par - 1), 1 - par)
                down(NG - 1, 1)

            out_projection(W_OUT, oT, 0)
            norm(2)
            peer_route(0)
            peer_dense(0)
            norm(3)
            pe.wait_ge(gl_in, 16 * 5)
            for c in range(2):
                n = W_GIN + c
                chunk_landed(n)
                for tt in range(TT):
                    i = c * TT + tt
                    at_least(pe, v_gelu, i - 3)
                    for k in range(KT):
                        if i == 0:
                            pe.wait_ge(x_ready, 3 * KT + k + 1)
                        nc.tensor.matmul(ps[:, i % 4, :], xm[:, k, tt * P:(tt + 1) * P], slots[n][:, k, :],
                                         start=(k == 0), stop=False)
                    nc.tensor.matmul(ps[:, i % 4, :], ones_row[:, :], bvrow[:, c * CW:(c + 1) * CW],
                                     start=False, stop=True).then_inc(v_mm, 1)
            pe.wait_ge(v_gelu, 2 * TT)
            for f in range(KT):
                n = W_GIN + 2 + f // 4
                if f % 4 == 0:
                    chunk_landed(n)
                at_least(pe, u_gelu, f - 3)
                for k in range(KT):
                    mm = nc.tensor.matmul(ps[:, f % 4, :], slots[n][:, k, (f % 4) * P:(f % 4 + 1) * P],
                                          xm[:, k, :], start=(k == 0), stop=(k == KT - 1))
                mm.then_inc(u_mm, 1)
            pe.wait_ge(v_normed, TT)
            for g in range(KT):
                at_least(pe, y_ready, g - 1)
                for tt in range(TT):
                    mm = nc.tensor.matmul(ps[:, 4 + g % 2, tt * P:(tt + 1) * P], vsb[:, tt, g * P:(g + 1) * P],
                                          wsT[:, g, :], start=True, stop=True)
                mm.then_inc(sv_mm, 1)
            pe.wait_ge(y_ready, KT)
            out_projection(W_GOUT, yT, KT)
            norm(4)
            peer_route(1)
            peer_dense(1)
            norm(5)

        @block.vector
        def _(dve):
            step = Chain(dve, dve_step)

            def modulation(layer, n0, n1, who):
                dve.wait_ge(mod_mm, NFIRST if (layer, n0) == (0, 0) else NCH)
                col = 2 * 6 * KT * layer
                sums = ps[:, 7, col + 2 * n0:col + 2 * n1].rearrange("p (n w) -> p n w", w=2)[:, :, 0:who]
                step(nc.vector.scalar_tensor_tensor(
                    out=mods[:, layer, n0:n1, 0:who], in0=sums, scalar=float(D),
                    in1=bmod[:, layer, n0:n1].unsqueeze(2).to_broadcast([P, n1 - n0, who]),
                    op0=ALU.mult, op1=ALU.add))
                for sc in (sc1, sc2):
                    if n0 <= sc < n1:
                        step(nc.vector.tensor_scalar(mods[:, layer, sc:sc + KT, 0:who],
                                                     mods[:, layer, sc:sc + KT, 0:who], 1.0, None, ALU.add))

            def norm(n):
                src, width, dst, layer, sh, sc, who = NORMS[n]
                dve.wait_ge(sq_used, (n + 1) * KT)
                nc.vector.tensor_scalar(rms[:, 0:width], ps[:, 6, 0:width], EPS, None, ALU.add).then_inc(ms_ready, 1)
                dve.wait_ge(rms_ready, n + 1)
                nc.vector.reciprocal(rinv[:, 0:width], rms[:, 0:width]).then_inc(rinv_ready, 1)
                dve.wait_ge(rinv_ready, n + 1)
                for k in range(KT):
                    scale = fing[:, k:k + 1] if sc is None else mods[:, layer, sc + k, who:who + 1]
                    nc.vector.scalar_tensor_tensor(out=dst[:, k, :], in0=src[:, k, :], scalar=scale,
                                                   in1=rinv[:, 0:width], op0=ALU.mult, op1=ALU.mult
                                                   ).then_inc(x_scaled, 1)

            def sum_chunk(i):
                at_least(dve, mod_mm, i - 1)
                for half in range(2):
                    m = 2 * i + half
                    dve.wait_ge(mod_in[mslot[m]], mlanded[m])
                    for k in range(KT // 2):
                        for who, acc in enumerate((macc, maccx) if i < NFIRST else (macc,)):
                            w, c = modw[mslot[m]][:, k, :], condS[:, half * (KT // 2) + k, who:who + 1]
                            if m % 2 == 0 and k == 0:
                                ins = nc.vector.tensor_scalar(acc[:, i % 2, :], w, c, None, ALU.mult)
                            else:
                                ins = nc.vector.scalar_tensor_tensor(out=acc[:, i % 2, :], in0=w, scalar=c,
                                                                     in1=acc[:, i % 2, :], op0=ALU.mult, op1=ALU.add)
                        if k < KT // 2 - 1:
                            step(ins)
                    ins.then_inc(mod_read, 1)
                    dve.wait_ge(mod_read, m + 1)
                dve.sem_inc(macc_ready, 1)

            dve.wait_ge(x_in, 16 * 16)
            step(nc.vector.tensor_tensor(lamtmp[:, :, :], lamin[:, 0:4:2, :], lamin[:, 1:4:2, :], ALU.mult))
            step(nc.vector.tensor_reduce(lamv[:, 0:2], lamtmp[:, :, :], AX, ALU.add))
            nc.vector.tensor_scalar(subg8[:, :], sublg[:, :], 1.0 - LAM_INIT, None, ALU.mult).then_inc(lam_sum, 1)
            dve.wait_ge(cond_ready, 1)
            for i in range(NFIRST):
                sum_chunk(i)
            modulation(0, 0, g1, 2)
            dve.sem_inc(mod_ready, 1)
            norm(0)
            norm(1)

            for j, (kind, _, dst, rope, _, _) in enumerate(in_jobs):
                if j >= 1:
                    for i, at in enumerate(MOD_AT):
                        if at == j - 1:
                            sum_chunk(NFIRST + i)
                if kind != "rope":
                    continue
                dve.wait_ge(rope_raw, rope + 1)
                at_least(dve, rope_out, rope)
                step(nc.vector.tensor_tensor(ropetmp[:, 0, :], ropein[:, rope % 2, :], cosT[:, :], ALU.mult))
                dve.wait_ge(rope_mm, rope + 1)
                step(nc.vector.tensor_tensor(ropetmp[:, 1, :], ps[:, 4 + rope % 2, :], sinT[:, :], ALU.mult))
                nc.vector.tensor_tensor(dst, ropetmp[:, 0, :], ropetmp[:, 1, :], ALU.add).then_inc(rope_out, 1)
            modulation(0, g1, 6 * KT, 1)
            modulation(1, 0, 6 * KT, 1)
            dve.wait_ge(rope_out, 2 * HA)
            dve.wait_ge(lam_exp, 1)
            step(nc.vector.tensor_tensor(lamv[:, 4:5], lamv[:, 3:4], lamv[:, 2:3], ALU.subtract))
            step(nc.vector.tensor_scalar(lamv[:, 5:6], lamv[:, 4:5], -LAM_INIT, None, ALU.add))

            def maxima(u):
                kind, h, qt = units[u]
                for m in range(2 if kind == "diff" else 1):
                    j = job_of[u] + m
                    if kind == "near" and qt == 0:
                        dve.wait_ge(bias_in[h % 2], 16 * (h // 2 + 1))
                        step(nc.vector.tensor_tensor(btab[:, h % 2, :, :], btab[:, h % 2, :, :],
                                                     mask[:, :].unsqueeze(1).to_broadcast([P, 16, GRID_W]), ALU.add))
                    dve.wait_ge(score_mm, j + 1)
                    if kind == "diff":
                        step(nc.vector.tensor_reduce(mx[:, j:j + 1], wide(j % 2)[:, 0:TK], AX, ALU.max))
                        nc.vector.tensor_scalar(nmx[:, j:j + 1], mx[:, j:j + 1], -QK_SCALE, None,
                                                ALU.mult).then_inc(nmax_ready, 1)
                        continue
                    dve.wait_ge(exp_done, j - 1)
                    row = NA_ROWS - 1 - 2 * qt
                    bias = nc.vector.scalar_tensor_tensor(
                        out=Sbuf[:, j % 2, 0:T], in0=wide(j % 2)[:, 0:T], scalar=QK_SCALE,
                        in1=btab[:, h % 2, row:row + NA_ROWS, :].rearrange("p r c -> p (r c)"),
                        op0=ALU.mult, op1=ALU.add)
                    if qt == TT - 1:
                        bias.then_inc(bias_used, 1)
                    nc.vector.tensor_scalar(Sbuf[:, j % 2, T:TK], wide(j % 2)[:, T:TK], QK_SCALE, None, ALU.mult
                                            ).then_inc(near_read, 1)
                    dve.wait_ge(near_read, j + 1 - 2 * HEAD_END)
                    step(nc.vector.tensor_reduce(mx[:, j:j + 1], Sbuf[:, j % 2, :], AX, ALU.max))
                    nc.vector.tensor_scalar(nmx[:, j:j + 1], mx[:, j:j + 1], -1.0, None,
                                            ALU.mult).then_inc(nmax_ready, 1)

            def probabilities(u):
                kind, h, qt = units[u]
                j = job_of[u]
                n = 2 if kind == "diff" else 1
                dve.wait_ge(exp_done, j + n)
                step(nc.vector.reciprocal(rz[:, j:j + n], zs[:, j:j + n]))
                at_least(dve, probsT_mm, u - 1)
                dst = Abuf[:, u % 2, :]
                if kind == "diff":
                    i = j // 2
                    step(nc.vector.tensor_tensor(nlr[:, i:i + 1], rz[:, j + 1:j + 2], lamv[:, 5:6], ALU.mult))
                    step(nc.vector.tensor_scalar(dst, Ebuf[:, (j + 1) % 4, :], nlr[:, i:i + 1], None, ALU.mult))
                    nc.vector.scalar_tensor_tensor(out=dst, in0=Ebuf[:, j % 4, :], scalar=rz[:, j:j + 1], in1=dst,
                                                   op0=ALU.mult, op1=ALU.add).then_inc(probs_ready, 1)
                else:
                    nc.vector.tensor_scalar(dst, Ebuf[:, j % 4, :], rz[:, j:j + 1], None,
                                            ALU.mult).then_inc(probs_ready, 1)

            def outputs(u):
                kind, h, qt = units[u]
                cols = slice(qt * P, (qt + 1) * P)
                dve.wait_ge(av_mm, u + 1)
                if kind == "near":
                    lo = DH * (h % 2)
                    nc.vector.tensor_copy(oT[lo:lo + DH, HA + h // 2, cols], ps[lo:lo + DH, 6, cols]
                                          ).then_inc(o_out, 1)
                    return
                nc.vector.tensor_copy(oT[:, h, cols], ps[:, 6, cols]).then_inc(o_out, 1)
                if qt < TT - 1:
                    return
                dve.wait_ge(o_out, u + 1)
                nc.vector.tensor_tensor(osq[:, :], oT[:, h, :], oT[:, h, :], ALU.mult).then_inc(osq_ready, 1)
                dve.wait_ge(osum_mm, h + 1)
                nc.vector.tensor_scalar(osq[:, :], ps[:, 6, :], float(D // P), EPS, ALU.mult, ALU.add
                                        ).then_inc(oms_ready, 1)
                dve.wait_ge(orms_ready, h + 1)
                step(nc.vector.reciprocal(orinv[:, :], osq[:, :]))
                nc.vector.scalar_tensor_tensor(out=oT[:, h, :], in0=oT[:, h, :], scalar=subg8[:, :],
                                               in1=orinv[:, :], op0=ALU.mult, op1=ALU.mult).then_inc(o_normed, 1)
                dve.wait_ge(o_normed, h + 1)

            maxima(0)
            for u in range(len(units)):
                if u + 1 < len(units):
                    maxima(u + 1)
                probabilities(u)
                if u >= 2:
                    outputs(u - 2)
            outputs(len(units) - 2)
            outputs(len(units) - 1)

            def add_projection(layer):
                for f in range(KT):
                    dve.wait_ge(h_mm, layer * KT + f + 1)
                    nc.vector.scalar_tensor_tensor(out=hT[:, f, :], in0=ps[:, f % 4, :],
                                                   scalar=mods[:, layer, g1 + f, 0:1], in1=hT[:, f, :],
                                                   op0=ALU.mult, op1=ALU.add).then_inc(h_added, 1)
                dve.wait_ge(h_added, (layer + 1) * KT)

            ROUTE_STEPS = 24

            def carry_wait():
                nc.vector.memset(carrier[:, :], 0.0)

            def peer_route(layer):
                def picks(r):
                    tile = r + layer * TT
                    link = Chain(dve, route_step, tile * ROUTE_STEPS)
                    dve.wait_ge(S_ready, tile * 4 + 4)
                    carry_wait()

                    def top16(rows, vals, ids, src, spare, src_free=None):
                        for i in rows:
                            last = nc.vector.max(vals(i)[:, 0:8], src(i))
                        link(last)
                        carry_wait()
                        for i in rows:
                            nc.vector.max_index(ids(i)[:, 0:8], vals(i)[:, 0:8], src(i))
                            last = nc.vector.match_replace(spare(i), vals(i)[:, 0:8], src(i), NEG)
                        link(last)
                        if src_free is not None:
                            dve.sem_inc(src_free, 1)
                        carry_wait()
                        for i in rows:
                            last = nc.vector.max(vals(i)[:, 8:16], spare(i))
                        link(last)
                        carry_wait()
                        for i in rows:
                            last = nc.vector.max_index(ids(i)[:, 8:16], vals(i)[:, 8:16], spare(i))
                        link(last)

                    top16(range(HP), lambda i: topv[:, i // 2, i % 2, :], lambda i: topi[:, i // 2, i % 2, :],
                          lambda i: S[:, i, :], lambda i: S2[:, i, :], S_free)
                    for a0, a1, nb in ((0, FULL, TOPK), (FULL, TOPK, SHORT)):
                        shape = [P, PH, a1 - a0, nb]
                        c0 = 0 if a0 == 0 else FULL * TOPK
                        last = nc.vector.tensor_tensor(
                            cand[:, 0, :, c0:c0 + (a1 - a0) * nb].rearrange("p h (a b) -> p h a b", b=nb),
                            topv[:, :, 0, a0:a1].unsqueeze(3).to_broadcast(shape),
                            topv[:, :, 1, 0:nb].unsqueeze(2).to_broadcast(shape), ALU.add)
                    link(last)
                    carry_wait()
                    top16(range(PH), lambda i: candv[:, i, :], lambda i: candi[:, i, :],
                          lambda i: cand[:, 0, i, :], lambda i: cand[:, 1, i, :])
                    nc.vector.tensor_scalar(shifted[:, 0, :, :], candi[:, :, :], 4, None, ALU.logical_shift_right)
                    link(nc.vector.tensor_scalar(shifted[:, 1, :, :], candi[:, :, :], 2, None,
                                                 ALU.logical_shift_right))
                    link(nc.vector.scalar_tensor_tensor(
                        out=rank[:, 0, :, :], in0=shifted[:, 1, :, :], scalar=float(FULL - FULL * TOPK // SHORT),
                        in1=shifted[:, 0, :, :], op0=ALU.add, op1=ALU.max))
                    link(nc.vector.tensor_scalar(rank[:, 1, :, :], rank[:, 0, :, :], float(SHORT),
                                                 float(FULL * (TOPK - SHORT)), ALU.mult, ALU.add))
                    link(nc.vector.scalar_tensor_tensor(
                        out=rank[:, 1, :, :], in0=rank[:, 0, :, :], scalar=float(TOPK), in1=rank[:, 1, :, :],
                        op0=ALU.mult, op1=ALU.min))
                    link(nc.vector.tensor_tensor(rank[:, 1, :, :], candi[:, :, :], rank[:, 1, :, :], ALU.subtract))
                    at_least(dve, pickT_mm, tile)
                    shape = [P, PH, TOPK, TOPK]
                    for half, keys in enumerate((key1[:, :, :], pick[:, 2, :, :])):
                        link(nc.vector.tensor_tensor(eq[:, :, :, :],
                                                     iota16[:, :].unsqueeze(1).unsqueeze(1).to_broadcast(shape),
                                                     rank[:, half, :, :].unsqueeze(3).to_broadcast(shape),
                                                     ALU.is_equal))
                        link(nc.vector.tensor_tensor(eq[:, :, :, :], eq[:, :, :, :],
                                                     topi[:, :, half, :].unsqueeze(2).to_broadcast(shape), ALU.mult))
                        link(nc.vector.tensor_reduce(keys, eq[:, :, :, :], AX, ALU.add))
                    nc.vector.tensor_tensor(pick[:, 3, :, :], candv[:, :, :],
                                            candv[:, :, 0:1].to_broadcast([P, PH, TOPK]), ALU.subtract
                                            ).then_inc(gate_logits, 1)
                    link(nc.vector.tensor_copy(key1u[:, 0, :, :], key1[:, :, :]))
                    nc.vector.tensor_scalar(key1u[:, 1, :, :], key1u[:, 0, :, :], NKEY - TOPK, None, ALU.bitwise_and)
                    link(nc.vector.tensor_scalar(key1u[:, 2, :, :], key1u[:, 0, :, :], TOPK - 1, None,
                                                 ALU.bitwise_and))
                    nc.vector.tensor_copy(pick[:, 0:2, :, :], key1u[:, 1:3, :, :])
                    dve.wait_ge(gate_exp, tile + 1)
                    link(nc.vector.tensor_reduce(zsum[:, 0, :], pick[:, 3, :, :], AX, ALU.add))
                    link(nc.vector.reciprocal(zsum[:, 1, :], zsum[:, 0, :]))
                    nc.vector.tensor_tensor(pick[:, 3, :, :], pick[:, 3, :, :],
                                            zsum[:, 1, :].unsqueeze(2).to_broadcast([P, PH, TOPK]), ALU.mult
                                            ).then_inc(pick_ready, 1)
                    used = link.n - tile * ROUTE_STEPS
                    if isinstance(used, int):
                        assert used == ROUTE_STEPS, used

                def one_hots(r):
                    tile = r + layer * TT
                    dve.wait_ge(pickT_mm, tile + 1)
                    nc.vector.tensor_copy(pickT[:, :, :].rearrange("p n t -> p (n t)"), ps[:, 0, :]
                                          ).then_inc(pickT_out, 1)
                    dve.wait_ge(pickT_out, tile + 1)
                    for half in range(2):
                        cols = slice(half * P // 2, (half + 1) * P // 2)
                        if half == 1:
                            dve.wait_ge(hot_ready, tile * NB + NB // 2)
                        link = Chain(dve, hot_step, (tile * 2 + half) * 2)
                        nc.vector.tensor_tensor(hot_lo[:, :, :],
                                                iota16[:, :].unsqueeze(1).to_broadcast([P, P // 2, TOPK]),
                                                pickT[:, 1, cols].unsqueeze(2).to_broadcast([P, P // 2, TOPK]),
                                                ALU.is_equal)
                        shape = [P, P // 2, NHI]
                        link(nc.vector.tensor_tensor(hot_hi[:, :, :], iota8[:, :].unsqueeze(1).to_broadcast(shape),
                                                     pickT[:, 0, cols].unsqueeze(2).to_broadcast(shape),
                                                     ALU.is_equal))
                        link(nc.vector.tensor_tensor(hot_hi[:, :, :], hot_hi[:, :, :],
                                                     pickT[:, 3, cols].unsqueeze(2).to_broadcast(shape), ALU.mult))
                        carry_wait()
                        with dve.Fori(0, NB // 4) as it:
                            for par in range(2):
                                n = tile * NB + half * (NB // 2) + it * 2 + par
                                dve.wait_ge(G_mm, n * 2 + 2)
                                t0 = (it * 2 + par) * TOK
                                shape = [P, TOK, P]
                                nc.vector.tensor_tensor(
                                    Bhot[:, par, :, :], iota[:, :].unsqueeze(1).to_broadcast(shape),
                                    pickT[:, 2, bass.ds(t0 + half * (P // 2), TOK)].unsqueeze(2).to_broadcast(shape),
                                    ALU.is_equal)
                                shape = [P, TOK, NHI, TOPK]
                                nc.vector.tensor_tensor(
                                    Ahot[:, par, :, :].rearrange("p t (a b) -> p t a b", b=TOPK),
                                    hot_hi[:, bass.ds(t0, TOK), :].unsqueeze(3).to_broadcast(shape),
                                    hot_lo[:, bass.ds(t0, TOK), :].unsqueeze(2).to_broadcast(shape),
                                    ALU.mult).then_inc(hot_ready, 1)
                    dve.wait_ge(hot_ready, (tile + 1) * NB)

                picks(0)
                with dve.Fori(1, TT) as r:
                    picks(r)
                    one_hots(r - 1)
                one_hots(TT - 1)

            def peer_dense(layer):
                def rest_of_x():
                    for k in range(KT):
                        dve.wait_ge(x_hi, layer * KT + k + 1)
                        nc.vector.tensor_tensor(xlo[:, k, :], xm[:, k, :], xhi[:, k, :].bitcast(F32),
                                                ALU.subtract).then_inc(x_split, 1)

                def rest_of_U(g, par):
                    dve.wait_ge(U_hi, g + (layer * (NG - EG) - EG + 1))
                    nc.vector.tensor_tensor(Ulo[:, par, :, :], Uraw[:, par, :, :], Uhi[:, par, :, :].bitcast(F32),
                                            ALU.subtract).then_inc(U_split, 1)

                def rest_of_V(g, par):
                    dve.wait_ge(V_hi, g + layer * NG + 1)
                    nc.vector.tensor_tensor(Vlo[:, par, :, :], Vraw[:, par, :, :], Vhi[:, par, :, :].bitcast(F32),
                                            ALU.subtract).then_inc(V_split, 1)

                def gated(g, par, it, j, early=False):
                    n = (g + layer * NG) * 2 + j
                    if early:
                        dve.wait_ge(act_in[par], (it + (layer * (EG // 2) + 1)) * 16)
                    else:
                        dve.wait_ge(act_ready, n + (layer * (NG - EG) - EG - layer * NG) * 2 + 1)
                    src = act_odd if early and par else act
                    dve.wait_ge(G_in[par], (it + (layer * (NG // 2) + 1)) * 16)
                    at_least(dve, dn_mm, (g + (layer * NG - 1)) * KT)
                    nc.vector.tensor_tensor(Hf[:, j, :], src[:, j, :], Gin[:, par, j, :], ALU.mult
                                            ).then_inc(H_step, 1)
                    dve.wait_ge(H_step, n * 2 + 1)
                    nc.vector.tensor_copy(Hhi[:, par, j, :], Hf[:, j, :]).then_inc(H_step, 1)
                    dve.wait_ge(H_step, n * 2 + 2)
                    nc.vector.tensor_tensor(Hlo[:, par, j, :], Hf[:, j, :], Hhi[:, par, j, :].bitcast(F32),
                                            ALU.subtract).then_inc(H_ready, 1)

                def add_group(g, early=False):
                    n = (g + layer * NG) * KT
                    for d in range(KT):
                        dve.wait_ge(dn_mm, n + (d + 1))
                        at_least(dve, dn_added, n + (d + 1 - KT))
                        nc.vector.scalar_tensor_tensor(out=hT[:, d, :], in0=ps[:, d if early else 2 + d % 4, :],
                                                       scalar=mods[:, layer, g2 + d, 0:1], in1=hT[:, d, :],
                                                       op0=ALU.mult, op1=ALU.add).then_inc(dn_added, 1)

                def period(g, par, it, last=False):
                    if not last:
                        rest_of_U(g + 1, 1 - par)
                    gated(g, par, it, 0)
                    rest_of_V(g, par)
                    gated(g, par, it, 1)
                    add_group(g - 1)

                def early_period(g, par, it, first=False):
                    gated(g, par, it, 0, early=True)
                    rest_of_V(g, par)
                    gated(g, par, it, 1, early=True)
                    if not first:
                        add_group(g - 1, early=True)

                early_period(0, 0, 0, first=True)
                early_period(1, 1, 0)
                rest_of_x()
                with dve.Fori(1, EG // 2 - 1) as it:
                    for par in range(2):
                        early_period(it * 2 + par, par, it)
                early_period(EG - 2, 0, EG // 2 - 1)
                rest_of_U(EG, 0)
                early_period(EG - 1, 1, EG // 2 - 1)
                period(EG, 0, EG // 2)
                period(EG + 1, 1, EG // 2)
                with dve.Fori(EG // 2 + 1, NG // 2 - 1) as it:
                    for par in range(2):
                        period(it * 2 + par, par, it)
                period(NG - 2, 0, NG // 2 - 1)
                period(NG - 1, 1, NG // 2 - 1, last=True)
                add_group(NG - 1)
                dve.wait_ge(dn_added, (layer + 1) * NG * KT)

            add_projection(0)
            norm(2)
            peer_route(0)
            peer_dense(0)
            norm(3)
            dve.wait_ge(gl_in, 16 * 5)
            dve.wait_ge(v_gelu, 2 * TT)
            for tt in range(TT):
                for c in range(2):
                    last = nc.vector.bn_stats(bnst[:, tt, c, :], vsb[:, tt, c * CW:(c + 1) * CW])
                step(last)
                last = nc.vector.bn_aggr(bnag[:, tt, :], bnst[:, tt, :, :])
            step(last)
            nc.vector.tensor_scalar(rstd[:, 0, :], bnag[:, :, 1], EPS, None, ALU.add).then_inc(var_ready, 1)
            dve.wait_ge(std_ready, 1)
            step(nc.vector.reciprocal(rstd[:, 1, :], rstd[:, 0, :]))
            for tt in range(TT):
                row = vsb[:, tt, :]
                step(nc.vector.tensor_scalar(row, row, bnag[:, tt, 0:1], rstd[:, 1, tt:tt + 1], ALU.subtract, ALU.mult))
                step(nc.vector.tensor_tensor(row, row, lng[:, :], ALU.mult))
                nc.vector.tensor_tensor(row, row, lnb[:, :], ALU.add).then_inc(v_normed, 1)
            dve.wait_ge(u_gelu, KT)
            for g in range(KT):
                dve.wait_ge(sv_mm, g + 1)
                at_least(dve, y_ready, g - 1)
                step(nc.vector.tensor_tensor(svb[:, g % 2, :].rearrange("p (n t) -> p n t", n=TT),
                                             ps[:, 4 + g % 2, :].rearrange("p (n t) -> p n t", n=TT),
                                             bsb[:, g, :].unsqueeze(1).to_broadcast([P, TT, P]), ALU.add))
                nc.vector.tensor_tensor(yT[:, g, :], svb[:, g % 2, :], uT[:, g, :], ALU.mult).then_inc(y_ready, 1)
            add_projection(1)
            norm(4)
            peer_route(1)
            peer_dense(1)
            norm(5)

    return nc


def constants():
    f = np.float32
    p = np.arange(P)
    d = p % DH
    axis, half, i = d // 32, d % 32 // 16, d % 16
    inv_freq = (1.0 / (f(10000.0) ** (np.arange(0, DH // 2, 2, dtype=f) / f(DH // 2)))).astype(f)
    t = np.arange(T)
    place = np.stack([t // GRID_W, t % GRID_W]).astype(f)
    angle = (place[axis] * inv_freq[i][:, None]).astype(f)
    rot = np.zeros((P, P), f)
    rot[p + 16 * (1 - 2 * half), p] = 2 * half - 1
    col = p % GRID_W
    first = np.clip(col - NA_COLS // 2, 0, GRID_W - NA_COLS)[:, None]
    key = np.arange(GRID_W)[None, :]
    mask = np.where((key >= first) & (key < first + NA_COLS), 0.0, MASKED).astype(f)
    return {
        "ones": np.full((P, P), 1.0 / D, f), "ident": np.eye(P, dtype=f),
        "iota": np.tile(np.arange(P, dtype=f), (P, 1)), "iota16": np.tile(np.arange(TOPK, dtype=f), (P, 1)),
        "iota8": np.tile(np.arange(0, NKEY, TOPK, dtype=f), (P, 1)),
        "cosT": np.cos(angle).astype(f), "sinT": np.sin(angle).astype(f), "rot": rot, "mask": mask,
        "ones_row": np.ones((1, P), f),
    }


def columns_of(v):
    v = v.reshape(v.shape[:-1] + (v.shape[-1] // P, P))
    return np.moveaxis(v, -1, 0)


def layout(i):
    p = np.arange(P)[:, None, None]
    s = np.arange(16)[None, :, None]
    k = np.arange(GRID_W)[None, None, :]
    dr = np.clip(s - p // GRID_W, 0, 2 * NA_ROWS - 2)
    dc = np.clip(k - p % GRID_W + NA_COLS - 1, 0, 2 * NA_COLS - 2)
    U = i["peer_u"].reshape(DEPTH, NG, 2 * P, KT, P)
    arrays = {
        "xT": i["x"][0].T, "ctxT": i["ctx"][0].T,
        "cond": columns_of(np.stack([i["c"][0], i["c_ctx"]])).transpose(0, 2, 1),
        "b_mod": columns_of(i["b_mod"]), "w_mod": i["w_mod"],
        "attn_in": i["attn_w_in"], "attn_out": i["attn_w_out"], "query": i["peer_w_query"],
        "gate_in": np.concatenate([i["chunk_w_in"][:, :, D:], i["chunk_w_in"][:, :, :D]], axis=2),
        "gate_out": i["chunk_w_out"],
        "lam": np.broadcast_to(np.stack([i["lambda_q1"][0], i["lambda_k1"][0], i["lambda_q2"][0],
                                         i["lambda_k2"][0]]), (P, 4, DH)),
        "subln_g": i["subln_g"][0][:, None], "btab": i["na_rpb"][0][:, dr, dc],
        "bu": columns_of(i["chunk_b_in"][0, :D]), "bv": i["chunk_b_in"][:, D:],
        "ln_g": i["chunk_ln_g"][0], "ln_b": i["chunk_ln_b"][0], "b_s": i["chunk_b_s"][0],
        "w_sT": i["chunk_w_s"][0].transpose(2, 0, 1),
        "keysT": i["peer_sub_keys"].reshape(DEPTH, HP, NKEY, P).transpose(0, 3, 1, 2),
        "UT": U.transpose(0, 1, 4, 3, 2), "V": i["peer_v"].reshape(DEPTH, NG, 2, P, D),
        "final_g": columns_of(i["final_norm_g"]),
    }
    arrays.update(constants())
    return arrays


def kernel(**inputs):
    import concourse.bacc as bacc
    from concourse.bass_utils import run_bass_kernel_spmd

    nc = bacc.Bacc("TRN2", target_bir_lowering=False, num_devices=1)
    arrays, aps = {}, {}
    for name, v in layout({k: np.asarray(v) for k, v in inputs.items()}).items():
        v = np.ascontiguousarray(v)
        arrays[f"in_{name}"] = v
        aps[name] = nc.dram_tensor(f"in_{name}", v.shape, mybir.dt.from_np(v.dtype), kind="ExternalInput").ap()
    out = nc.dram_tensor("out_T", (D, T), F32, kind="ExternalOutput").ap()
    backbone(nc, aps, out)
    r = run_bass_kernel_spmd(nc, [arrays], core_ids=[0])
    return np.ascontiguousarray(r.results[0]["out_T"].T)[None]
```
